# Optimizing a Trainium2 kernel written in Bass

```python
import math
import jax, jax.numpy as jnp
from jax import lax
import numpy as np

D_MODEL = 1024
BATCH = 1
SEQ = 1024
DEPTH = 1

N_META = 16
D_MIX = D_MODEL
D_LRU = D_MIX // 2
D_CC = D_MIX - D_LRU
LRU_HEADS = 8
LRU_HEAD_DIM = D_LRU // LRU_HEADS
CC_GROUPS = 8
LRU_CONV_W = 4
CC_CONV_W = 31
LRU_C = 8.0
D_FF = 4 * D_MODEL
EPS = 1e-6


def rmsnorm(x, g):
    xf = x.astype(jnp.float32)
    y = xf * lax.rsqrt(jnp.mean(xf * xf, axis=-1, keepdims=True) + EPS)
    return (y * g.astype(jnp.float32)).astype(x.dtype)

def layernorm(x, g, b):
    xf = x.astype(jnp.float32)
    mu = jnp.mean(xf, axis=-1, keepdims=True)
    var = jnp.mean(jnp.square(xf - mu), axis=-1, keepdims=True)
    y = (xf - mu) * lax.rsqrt(var + EPS)
    return (y * g.astype(jnp.float32) + b.astype(jnp.float32)).astype(x.dtype)

def causal_depthwise_conv(x, w, b):
    k = w.shape[0]
    y = lax.conv_general_dilated(
        x, w[:, None, :].astype(x.dtype), window_strides=(1,), padding=[(k - 1, 0)],
        dimension_numbers=("NWC", "WIO", "NWC"), feature_group_count=x.shape[-1])
    return y + b.astype(x.dtype)

def block_diag_linear(x, w, b):
    B, T, _ = x.shape
    h, dh, _ = w.shape
    y = jnp.einsum("bthi,hij->bthj", x.reshape(B, T, h, dh), w.astype(x.dtype))
    return y.reshape(B, T, h * dh) + b.astype(x.dtype)

def rg_lru(x, w_a, b_a, w_x, b_x, a_param):
    xf = x.astype(jnp.float32)
    r = jax.nn.sigmoid(block_diag_linear(xf, w_a, b_a))
    i = jax.nn.sigmoid(block_diag_linear(xf, w_x, b_x))
    log_a = -LRU_C * r * jax.nn.softplus(-a_param.astype(jnp.float32))
    a = jnp.exp(log_a)
    mult = jnp.sqrt(-jnp.expm1(2.0 * log_a))
    bterm = mult * (i * xf)

    def combine(left, right):
        a1, b1 = left
        a2, b2 = right
        return a1 * a2, a2 * b1 + b2

    _, h = lax.associative_scan(combine, (a, bterm), axis=1)
    return h.astype(x.dtype)

def first_inputs(seed: int = 0) -> dict:
    key = jax.random.key(seed)
    ks = jax.random.split(key, 24)
    f32 = jnp.float32

    def nrm(k, shape, scale):
        return jax.random.normal(k, shape, f32) * scale

    x = jax.random.normal(ks[0], (BATCH, SEQ, D_MODEL), f32)
    meta_tokens = nrm(ks[1], (N_META, D_MODEL), 1.0)
    norm_mix_g = 1.0 + nrm(ks[2], (DEPTH, D_MODEL), 0.02)
    w_in = nrm(ks[3], (DEPTH, D_MODEL, 2 * D_LRU + 2 * D_CC), D_MODEL ** -0.5)
    lru_conv_w = nrm(ks[4], (DEPTH, LRU_CONV_W, D_LRU), LRU_CONV_W ** -0.5)
    lru_conv_b = nrm(ks[5], (DEPTH, D_LRU), 0.01)
    lru_gate_a_w = nrm(ks[6], (DEPTH, LRU_HEADS, LRU_HEAD_DIM, LRU_HEAD_DIM), LRU_HEAD_DIM ** -0.5)
    lru_gate_a_b = nrm(ks[7], (DEPTH, D_LRU), 0.01)
    lru_gate_x_w = nrm(ks[8], (DEPTH, LRU_HEADS, LRU_HEAD_DIM, LRU_HEAD_DIM), LRU_HEAD_DIM ** -0.5)
    lru_gate_x_b = nrm(ks[9], (DEPTH, D_LRU), 0.01)
    a_c = jax.random.uniform(ks[10], (DEPTH, D_LRU), f32, minval=0.9, maxval=0.999)
    a_base = jnp.power(a_c, 1.0 / LRU_C)
    lru_a_param = jnp.log(a_base) - jnp.log1p(-a_base)
    cc_conv_w = nrm(ks[11], (DEPTH, CC_CONV_W, D_CC), CC_CONV_W ** -0.5)
    cc_conv_b = nrm(ks[12], (DEPTH, D_CC), 0.01)
    cc_ln_g = 1.0 + nrm(ks[13], (DEPTH, D_CC), 0.02)
    cc_ln_b = nrm(ks[14], (DEPTH, D_CC), 0.01)
    out_norm_lru_g = 1.0 + nrm(ks[15], (DEPTH, D_LRU), 0.02)
    out_norm_cc_g = 1.0 + nrm(ks[16], (DEPTH, D_CC), 0.02)
    w_out = nrm(ks[17], (DEPTH, D_MIX, D_MODEL), D_MIX ** -0.5)
    norm_mlp_g = 1.0 + nrm(ks[18], (DEPTH, D_MODEL), 0.02)
    w_mlp_up = nrm(ks[19], (DEPTH, D_MODEL, D_FF), D_MODEL ** -0.5)
    w_mlp_down = nrm(ks[20], (DEPTH, D_FF, D_MODEL), D_FF ** -0.5)
    norm_final_g = 1.0 + nrm(ks[21], (D_MODEL,), 0.02)
    return {
        "x": x, "meta_tokens": meta_tokens, "norm_mix_g": norm_mix_g, "w_in": w_in,
        "lru_conv_w": lru_conv_w, "lru_conv_b": lru_conv_b,
        "lru_gate_a_w": lru_gate_a_w, "lru_gate_a_b": lru_gate_a_b,
        "lru_gate_x_w": lru_gate_x_w, "lru_gate_x_b": lru_gate_x_b,
        "lru_a_param": lru_a_param, "cc_conv_w": cc_conv_w, "cc_conv_b": cc_conv_b,
        "cc_ln_g": cc_ln_g, "cc_ln_b": cc_ln_b,
        "out_norm_lru_g": out_norm_lru_g, "out_norm_cc_g": out_norm_cc_g, "w_out": w_out,
        "norm_mlp_g": norm_mlp_g, "w_mlp_up": w_mlp_up, "w_mlp_down": w_mlp_down,
        "norm_final_g": norm_final_g,
    }

def first_block(x, meta_tokens, norm_mix_g, w_in, lru_conv_w, lru_conv_b, lru_gate_a_w,
              lru_gate_a_b, lru_gate_x_w, lru_gate_x_b, lru_a_param, cc_conv_w, cc_conv_b,
              cc_ln_g, cc_ln_b, out_norm_lru_g, out_norm_cc_g, w_out, norm_mlp_g,
              w_mlp_up, w_mlp_down, norm_final_g):
    B = x.shape[0]
    meta = jnp.broadcast_to(meta_tokens[None].astype(x.dtype), (B, N_META, D_MODEL))
    h = jnp.concatenate([meta, x], axis=1)

    for l in range(DEPTH):
        u = rmsnorm(h, norm_mix_g[l])
        proj = u @ w_in[l].astype(u.dtype)
        x_lru, g_lru, v_cc, g_cc = jnp.split(
            proj, [D_LRU, 2 * D_LRU, 2 * D_LRU + D_CC], axis=-1)

        xc = causal_depthwise_conv(x_lru, lru_conv_w[l], lru_conv_b[l])
        y_lru = rg_lru(xc, lru_gate_a_w[l], lru_gate_a_b[l], lru_gate_x_w[l],
                       lru_gate_x_b[l], lru_a_param[l]) * jax.nn.gelu(g_lru)

        c = v_cc * jax.nn.sigmoid(g_cc)
        c = causal_depthwise_conv(c, cc_conv_w[l], cc_conv_b[l])
        y_cc = jax.nn.silu(layernorm(c, cc_ln_g[l], cc_ln_b[l]))

        y = jnp.concatenate([rmsnorm(y_lru, out_norm_lru_g[l]),
                             rmsnorm(y_cc, out_norm_cc_g[l])], axis=-1)
        h = h + y @ w_out[l].astype(y.dtype)

        m = rmsnorm(h, norm_mlp_g[l]) @ w_mlp_up[l].astype(h.dtype)
        h = h + jnp.square(jax.nn.relu(m)) @ w_mlp_down[l].astype(h.dtype)

    out = rmsnorm(h, norm_final_g)
    return out[:, N_META:]


_first_inputs = first_inputs


def first_inputs(seed=0):
    import zlib

    import numpy as np

    out = dict(_first_inputs(seed))
    spreads = {}
    factors = {'norm_mix_g': 2.914,
     'lru_gate_a_b': 41.134,
     'lru_gate_x_b': 37.685,
     'cc_conv_b': 5.613,
     'cc_ln_g': 63.618,
     'cc_ln_b': 131.547,
     'out_norm_lru_g': 80.359,
     'out_norm_cc_g': 73.299,
     'norm_mlp_g': 14.561,
     'norm_final_g': 21.57,
     'lru_conv_b': 3.528}
    for name, (base, spread) in spreads.items():
        noise = np.random.default_rng([zlib.crc32(name.encode()), seed]).standard_normal(out[name].shape)
        drawn = base * np.exp(spread * noise) if base else spread * noise
        out[name] = __import__('jax').numpy.asarray(drawn.astype(out[name].dtype))
    for name, factor in factors.items():
        out[name] = (out[name] * factor).astype(out[name].dtype)
    return out


_narrow_inputs = first_inputs


def first_inputs(seed=0):

    out = dict(_narrow_inputs(seed))
    wider = {'cc_ln_g': 4.17,
     'cc_ln_b': 4.15,
     'out_norm_lru_g': 4.06,
     'out_norm_cc_g': 4.06,
     'norm_final_g': 3.14}
    for name, times in wider.items():
        mean = out[name].mean()
        out[name] = (mean + times * (out[name] - mean)).astype(out[name].dtype)
    return out


CHUNK = 64
HEAD_DIM = 64
M_HEADS = 4
R_HEADS = 6
W_HEADS = 6
M_WIDTH = M_HEADS * HEAD_DIM
R_WIDTH = R_HEADS * HEAD_DIM
W_WIDTH = W_HEADS * HEAD_DIM
MIX_WIDTH = M_WIDTH + R_WIDTH + W_WIDTH
CONV_WIDTH = 4
W_LORA = 64
A_LORA = 64
G_LORA = 128
D_FF_2 = -(-8 * D_MODEL // (3 * 256)) * 256
M_COLS = 4 * M_WIDTH + 2 * M_HEADS
R_COLS = 4 * R_WIDTH
W_COLS = 3 * W_WIDTH + W_LORA + A_LORA + G_LORA
P_COLS = M_COLS + R_COLS + W_COLS
RMS_EPS = 1e-6
HEAD_LN_EPS = 1e-5
RWKV_LN_EPS = 64e-5
ROPE_BASE = 10000.0
M_INIT = -1e30


def rmsnorm_2(x, g):
    xf = x.astype(jnp.float32)
    y = xf * lax.rsqrt(jnp.mean(xf * xf, axis=-1, keepdims=True) + RMS_EPS) * g.astype(jnp.float32)
    return y.astype(x.dtype)

def head_layernorm(x, n_heads, eps):
    B, T, C = x.shape
    xh = x.astype(jnp.float32).reshape(B, T, n_heads, C // n_heads)
    mu = jnp.mean(xh, axis=-1, keepdims=True)
    var = jnp.mean(jnp.square(xh - mu), axis=-1, keepdims=True)
    return ((xh - mu) * lax.rsqrt(var + eps)).reshape(B, T, C)

def causal_depthwise_conv_2(x, w):
    K, C = w.shape
    return lax.conv_general_dilated(
        x, w.astype(x.dtype)[:, None, :], window_strides=(1,), padding=[(K - 1, 0)],
        dimension_numbers=("NWC", "WIO", "NWC"), feature_group_count=C)

def to_chunks(x, n_heads):
    B, T, C = x.shape
    return x.reshape(B, T // CHUNK, CHUNK, n_heads, C // n_heads).transpose(1, 0, 3, 2, 4)

def from_chunks(y):
    NC, B, H, L, d = y.shape
    return y.transpose(1, 0, 3, 2, 4).reshape(B, NC * L, H * d)

def gate_chunks(g):
    B, T, H = g.shape
    return g.reshape(B, T // CHUNK, CHUNK, H).transpose(1, 0, 3, 2)

def mlstm_chunkwise(q, k, v, i_pre, log_f):
    B, T, _ = q.shape
    H, d = M_HEADS, HEAD_DIM
    causal = jnp.tril(jnp.ones((CHUNK, CHUNK), dtype=bool))

    def step(carry, inp):
        C, n, m = carry
        qc, kc, vc, ic, lfc = inp
        b = jnp.cumsum(lfc, axis=-1)
        dlog = jnp.where(causal, b[..., :, None] - b[..., None, :] + ic[..., None, :], -jnp.inf)
        inter = b + m[..., None]
        m_row = jnp.maximum(inter, jnp.max(dlog, axis=-1))
        s = jnp.einsum('bhjd,bhsd->bhjs', qc, kc) * jnp.exp(dlog - m_row[..., None])
        inter_w = jnp.exp(inter - m_row)
        num = jnp.einsum('bhjs,bhse->bhje', s, vc) + inter_w[..., None] * jnp.einsum('bhjd,bhde->bhje', qc, C)
        den = jnp.sum(s, axis=-1) + inter_w * jnp.einsum('bhjd,bhd->bhj', qc, n)
        h = num / jnp.maximum(jnp.abs(den), jnp.exp(-m_row))[..., None]
        bL = b[..., -1]
        src = bL[..., None] - b + ic
        m_new = jnp.maximum(bL + m, jnp.max(src, axis=-1))
        sw = jnp.exp(src - m_new[..., None])
        dec = jnp.exp(bL + m - m_new)
        C_new = dec[..., None, None] * C + jnp.einsum('bhs,bhsd,bhse->bhde', sw, kc, vc)
        n_new = dec[..., None] * n + jnp.einsum('bhs,bhsd->bhd', sw, kc)
        return (C_new, n_new, m_new), h

    init = (jnp.zeros((B, H, d, d), jnp.float32), jnp.zeros((B, H, d), jnp.float32),
            jnp.full((B, H), M_INIT, jnp.float32))
    xs = (to_chunks(q, H), to_chunks(k, H), to_chunks(v, H), gate_chunks(i_pre), gate_chunks(log_f))
    _, h = lax.scan(step, init, xs)
    return from_chunks(h)

def mlstm_group(p, conv_w, b_i, b_f, ln_g):
    p = p.astype(jnp.float32)
    qk, v, o, gi, gf = jnp.split(p, [2 * M_WIDTH, 3 * M_WIDTH, 4 * M_WIDTH, 4 * M_WIDTH + M_HEADS], axis=-1)
    qk = jax.nn.silu(causal_depthwise_conv_2(qk, conv_w))
    q, k = jnp.split(qk, 2, axis=-1)
    i_pre = gi + b_i.astype(jnp.float32)
    log_f = jax.nn.log_sigmoid(gf + b_f.astype(jnp.float32))
    h = mlstm_chunkwise(q, k * HEAD_DIM ** -0.5, v, i_pre, log_f)
    h = head_layernorm(h, M_HEADS, HEAD_LN_EPS) * ln_g.astype(jnp.float32)
    return jax.nn.sigmoid(o) * h

def rotary(x, cos, sin):
    x1, x2 = jnp.split(x, 2, axis=-1)
    c, s = cos[None, :, None, :], sin[None, :, None, :]
    return jnp.concatenate([x1 * c - x2 * s, x1 * s + x2 * c], axis=-1)

def retention_group(p):
    p = p.astype(jnp.float32)
    B, T, _ = p.shape
    H, d = R_HEADS, HEAD_DIM
    q, k, v, g = jnp.split(p, 4, axis=-1)
    pos = jnp.arange(T, dtype=jnp.float32)
    theta = 1.0 / (ROPE_BASE ** jnp.linspace(0.0, 1.0, d // 2, dtype=jnp.float32))
    ang = pos[:, None] * theta[None, :]
    cos, sin = jnp.cos(ang), jnp.sin(ang)
    q = rotary(q.reshape(B, T, H, d), cos, sin).reshape(B, T, H * d)
    k = rotary(k.reshape(B, T, H, d), cos, sin).reshape(B, T, H * d) * d ** -0.5
    log_g = jnp.log(1.0 - 2.0 ** (-5.0 - jnp.arange(H, dtype=jnp.float32)))
    idx = jnp.arange(CHUNK, dtype=jnp.float32)
    diff = idx[:, None] - idx[None, :]
    dmat = jnp.where(diff >= 0, jnp.exp(jnp.maximum(diff, 0.0)[None] * log_g[:, None, None]), 0.0)
    q_dec = jnp.exp((idx[None, :] + 1.0) * log_g[:, None])[None, :, :, None]
    k_dec = jnp.exp((CHUNK - 1.0 - idx[None, :]) * log_g[:, None])[None, :, :, None]
    c_dec = jnp.exp(CHUNK * log_g)[None, :, None, None]

    def step(R, inp):
        qc, kc, vc = inp
        s = jnp.einsum('bhjd,bhsd->bhjs', qc, kc) * dmat
        out = jnp.einsum('bhjs,bhse->bhje', s, vc) + jnp.einsum('bhjd,bhde->bhje', qc, R) * q_dec
        R_new = c_dec * R + jnp.einsum('bhsd,bhse->bhde', kc * k_dec, vc)
        return R_new, out

    R0 = jnp.zeros((B, H, d, d), jnp.float32)
    _, y = lax.scan(step, R0, (to_chunks(q, H), to_chunks(k, H), to_chunks(v, H)))
    y = head_layernorm(from_chunks(y), H, HEAD_LN_EPS)
    return jax.nn.silu(g) * y

def rwkv7_group(p, mu, w0, w_up, a0, a_up, g_up, k_k, k_a, r_k, ln_g, ln_b):
    p = p.astype(jnp.float32)
    B, T, _ = p.shape
    H, d = W_HEADS, HEAD_DIM
    p_prev = jnp.pad(p, ((0, 0), (1, 0), (0, 0)))[:, :-1]
    p = p + mu.astype(jnp.float32) * (p_prev - p)
    r, k, v, wl, al, gl = jnp.split(
        p, [W_WIDTH, 2 * W_WIDTH, 3 * W_WIDTH, 3 * W_WIDTH + W_LORA, 3 * W_WIDTH + W_LORA + A_LORA], axis=-1)
    w_log = -jax.nn.softplus(-(w0 + jnp.tanh(wl) @ w_up.astype(jnp.float32))) - 0.5
    decay = jnp.exp(-jnp.exp(w_log))
    a = jax.nn.sigmoid(a0 + al @ a_up.astype(jnp.float32))
    g = jax.nn.sigmoid(gl) @ g_up.astype(jnp.float32)
    kk = (k * k_k).reshape(B, T, H, d)
    kk = kk / jnp.maximum(jnp.sqrt(jnp.sum(kk * kk, axis=-1, keepdims=True)), 1e-12)
    k = k * (1.0 + (a - 1.0) * k_a)

    def heads_t(z):
        return z.reshape(B, T, H, d).transpose(1, 0, 2, 3)

    def step(S, inp):
        r_t, w_t, k_t, v_t, kk_t, a_t = inp
        S = (S * w_t[:, :, None, :]
             - jnp.einsum('bhvk,bhk->bhv', S, kk_t)[..., None] * (kk_t * a_t)[:, :, None, :]
             + v_t[..., :, None] * k_t[..., None, :])
        return S, jnp.einsum('bhvk,bhk->bhv', S, r_t)

    S0 = jnp.zeros((B, H, d, d), jnp.float32)
    xs = (heads_t(r), heads_t(decay), heads_t(k), heads_t(v), kk.transpose(1, 0, 2, 3), heads_t(a))
    _, y = lax.scan(step, S0, xs)
    y = y.transpose(1, 0, 2, 3).reshape(B, T, H * d)
    y = head_layernorm(y, H, RWKV_LN_EPS) * ln_g + ln_b
    bonus = jnp.sum(r.reshape(B, T, H, d) * k.reshape(B, T, H, d) * r_k.reshape(H, d), axis=-1, keepdims=True)
    y = y + (bonus * v.reshape(B, T, H, d)).reshape(B, T, H * d)
    return y * g

def second_inputs(seed: int = 0) -> dict:
    key = jax.random.key(seed)
    ks = jax.random.split(key, 24)
    f32 = jnp.float32
    nrm = lambda k, shape, s: jax.random.normal(k, shape, f32) * s
    w0_base = jnp.linspace(-5.5, 0.5, W_WIDTH, dtype=f32)
    bf_base = jnp.linspace(3.0, 6.0, M_HEADS, dtype=f32)
    return {
        "x": nrm(ks[0], (BATCH, SEQ, D_MODEL), 1.0),
        "w_in": nrm(ks[1], (DEPTH, D_MODEL, P_COLS), D_MODEL ** -0.5),
        "ln1_g": 1.0 + nrm(ks[2], (DEPTH, D_MODEL), 0.02),
        "ln2_g": 1.0 + nrm(ks[3], (DEPTH, D_MODEL), 0.02),
        "lnf_g": 1.0 + nrm(ks[4], (D_MODEL,), 0.02),
        "m_conv": nrm(ks[5], (DEPTH, CONV_WIDTH, 2 * M_WIDTH), CONV_WIDTH ** -0.5),
        "m_b_i": nrm(ks[6], (DEPTH, M_HEADS), 0.1),
        "m_b_f": bf_base + nrm(ks[7], (DEPTH, M_HEADS), 0.1),
        "m_ln_g": 1.0 + nrm(ks[8], (DEPTH, M_WIDTH), 0.02),
        "rw_mu": jax.random.uniform(ks[9], (DEPTH, W_COLS), f32),
        "rw_w0": w0_base + nrm(ks[10], (DEPTH, W_WIDTH), 0.1),
        "rw_w_up": nrm(ks[11], (DEPTH, W_LORA, W_WIDTH), 0.1),
        "rw_a0": nrm(ks[12], (DEPTH, W_WIDTH), 0.1),
        "rw_a_up": nrm(ks[13], (DEPTH, A_LORA, W_WIDTH), 0.1),
        "rw_g_up": nrm(ks[14], (DEPTH, G_LORA, W_WIDTH), G_LORA ** -0.5),
        "rw_k_k": 0.85 + nrm(ks[15], (DEPTH, W_WIDTH), 0.02),
        "rw_k_a": 1.0 + nrm(ks[16], (DEPTH, W_WIDTH), 0.02),
        "rw_r_k": nrm(ks[17], (DEPTH, W_WIDTH), 0.1),
        "rw_ln_g": 1.0 + nrm(ks[18], (DEPTH, W_WIDTH), 0.02),
        "rw_ln_b": nrm(ks[19], (DEPTH, W_WIDTH), 0.01),
        "w_out": nrm(ks[20], (DEPTH, MIX_WIDTH, D_MODEL), MIX_WIDTH ** -0.5),
        "w_gate": nrm(ks[21], (DEPTH, D_MODEL, D_FF_2), D_MODEL ** -0.5),
        "w_up": nrm(ks[22], (DEPTH, D_MODEL, D_FF_2), D_MODEL ** -0.5),
        "w_down": nrm(ks[23], (DEPTH, D_FF_2, D_MODEL), D_FF_2 ** -0.5),
    }

def second_block(x, w_in, ln1_g, ln2_g, lnf_g, m_conv, m_b_i, m_b_f, m_ln_g, rw_mu, rw_w0, rw_w_up,
              rw_a0, rw_a_up, rw_g_up, rw_k_k, rw_k_a, rw_r_k, rw_ln_g, rw_ln_b, w_out, w_gate,
              w_up, w_down):
    for l in range(DEPTH):
        h = rmsnorm_2(x, ln1_g[l])
        p = h @ w_in[l]
        pm, pr, pw = jnp.split(p, [M_COLS, M_COLS + R_COLS], axis=-1)
        ym = mlstm_group(pm, m_conv[l], m_b_i[l], m_b_f[l], m_ln_g[l])
        yr = retention_group(pr)
        yw = rwkv7_group(pw, rw_mu[l], rw_w0[l], rw_w_up[l], rw_a0[l], rw_a_up[l], rw_g_up[l],
                         rw_k_k[l], rw_k_a[l], rw_r_k[l], rw_ln_g[l], rw_ln_b[l])
        y = jnp.concatenate([ym, yr, yw], axis=-1).astype(x.dtype)
        x = x + y @ w_out[l]
        h = rmsnorm_2(x, ln2_g[l])
        x = x + (jax.nn.silu(h @ w_gate[l]) * (h @ w_up[l])) @ w_down[l]
    return rmsnorm_2(x, lnf_g)


_first_inputs_2 = second_inputs


def second_inputs(seed=0):
    import zlib

    import numpy as np

    out = dict(_first_inputs_2(seed))
    spreads = {}
    factors = {'ln2_g': 4.509,
     'lnf_g': 8.28,
     'm_b_i': 64.0,
     'm_ln_g': 27.832,
     'rw_a0': 4.285,
     'rw_k_k': 34.165,
     'rw_k_a': 7.87,
     'rw_ln_g': 21.413,
     'rw_ln_b': 44.492}
    for name, (base, spread) in spreads.items():
        noise = np.random.default_rng([zlib.crc32(name.encode()), seed]).standard_normal(out[name].shape)
        drawn = base * np.exp(spread * noise) if base else spread * noise
        out[name] = __import__('jax').numpy.asarray(drawn.astype(out[name].dtype))
    for name, factor in factors.items():
        out[name] = (out[name] * factor).astype(out[name].dtype)
    return out


_narrow_inputs_2 = second_inputs


def second_inputs(seed=0):

    out = dict(_narrow_inputs_2(seed))
    wider = {'lnf_g': 3.24, 'm_ln_g': 3.6, 'rw_k_k': 5.55, 'rw_ln_g': 3.47, 'rw_ln_b': 3.47}
    for name, times in wider.items():
        mean = out[name].mean()
        out[name] = (mean + times * (out[name] - mean)).astype(out[name].dtype)
    return out


MIX_WIDTH_3 = D_MODEL
GDN_WIDTH = MIX_WIDTH_3 // 2
GDN_HEAD_DIM = 64
GDN_HEADS = GDN_WIDTH // GDN_HEAD_DIM
GDN_CHUNK = 64
CONV_K = 5
SGU_WIDTH = MIX_WIDTH_3 - GDN_WIDTH
SGU_GROUPS = 4
SGU_GROUP_DIM = SGU_WIDTH // SGU_GROUPS
SGU_CHUNK = 128
FF_DIM = 4 * D_MODEL

SPLIT_SIZES = (GDN_WIDTH, GDN_WIDTH, GDN_WIDTH, GDN_WIDTH,
               GDN_HEADS, GDN_HEADS, GDN_HEADS, GDN_HEADS,
               SGU_WIDTH, SGU_WIDTH)
SPLIT_POINTS = tuple(int(s) for s in np.cumsum(SPLIT_SIZES)[:-1])
IN_COLS = sum(SPLIT_SIZES)


def rms_norm(x, gain):
    xf = x.astype(jnp.float32)
    y = xf * lax.rsqrt(jnp.mean(xf * xf, axis=-1, keepdims=True) + EPS)
    return (y * gain.astype(jnp.float32)).astype(x.dtype)

def l2_normalize(x):
    return x * lax.rsqrt(jnp.sum(x * x, axis=-1, keepdims=True) + EPS)

def short_conv(x, w):
    c = x.shape[-1]
    return lax.conv_general_dilated(
        x, w[:, None, :].astype(x.dtype), window_strides=(1,),
        padding=[(CONV_K // 2, CONV_K // 2)],
        dimension_numbers=("NWC", "WIO", "NWC"), feature_group_count=c)

def gated_delta_rule_chunked(q, k, v, g, beta):
    bsz, nh, s, dk = q.shape
    dv = v.shape[-1]
    n = s // GDN_CHUNK
    q = q * (dk ** -0.5)

    def chunks(t):
        return t.reshape(bsz, nh, n, GDN_CHUNK, *t.shape[3:])

    q, k, v, g, beta = chunks(q), chunks(k), chunks(v), chunks(g), chunks(beta)
    g = jnp.cumsum(g, axis=-1)
    tri_incl = jnp.tril(jnp.ones((GDN_CHUNK, GDN_CHUNK), dtype=bool))
    tri_strict = jnp.tril(jnp.ones((GDN_CHUNK, GDN_CHUNK), dtype=bool), -1)
    diff = g[..., :, None] - g[..., None, :]
    decay = jnp.exp(jnp.where(tri_incl, diff, -jnp.inf))

    k_beta = k * beta[..., None]
    v_beta = v * beta[..., None]
    lower = jnp.where(tri_strict, jnp.einsum("bhnid,bhnjd->bhnij", k_beta, k) * decay, 0.0)
    a_mat = jnp.eye(GDN_CHUNK, dtype=jnp.float32) + lower
    rhs = jnp.concatenate([v_beta, k_beta * jnp.exp(g)[..., None]], axis=-1)
    sol = lax.linalg.triangular_solve(a_mat, rhs, left_side=True, lower=True, unit_diagonal=True)
    u_c, w_c = sol[..., :dv], sol[..., dv:]

    attn_intra = jnp.einsum("bhnid,bhnjd->bhnij", q, k) * decay
    q_dec = q * jnp.exp(g)[..., None]
    k_dec = k * jnp.exp(g[..., -1:] - g)[..., None]
    g_last = jnp.exp(g[..., -1])

    def step(state, inp):
        u_i, w_i, q_i, k_i, a_i, gl = inp
        v_new = u_i - jnp.einsum("bhid,bhde->bhie", w_i, state)
        o_i = jnp.einsum("bhid,bhde->bhie", q_i, state) + jnp.einsum("bhij,bhje->bhie", a_i, v_new)
        state = state * gl[..., None, None] + jnp.einsum("bhid,bhie->bhde", k_i, v_new)
        return state, o_i

    xs = tuple(jnp.moveaxis(t, 2, 0) for t in (u_c, w_c, q_dec, k_dec, attn_intra, g_last))
    state0 = jnp.zeros((bsz, nh, dk, dv), jnp.float32)
    _, o = lax.scan(step, state0, xs)
    return jnp.moveaxis(o, 0, 2).reshape(bsz, nh, s, dv)

def bidir_gated_deltanet(qkv, z, b_f, b_b, a_f, a_b, a_log_f, dt_bias_f, a_log_b, dt_bias_b, norm_gain):
    bsz, s, _ = qkv.shape
    q, k, v = jnp.split(qkv.astype(jnp.float32), 3, axis=-1)

    def heads(t):
        return t.reshape(bsz, s, GDN_HEADS, GDN_HEAD_DIM).transpose(0, 2, 1, 3)

    q, k, v = l2_normalize(heads(q)), l2_normalize(heads(k)), heads(v)

    def gates(b, a, a_log, dt_bias):
        beta = jax.nn.sigmoid(b.astype(jnp.float32)).transpose(0, 2, 1)
        g = -jnp.exp(a_log.astype(jnp.float32)) * jax.nn.softplus(
            a.astype(jnp.float32) + dt_bias.astype(jnp.float32))
        return g.transpose(0, 2, 1), beta

    g_f, beta_f = gates(b_f, a_f, a_log_f, dt_bias_f)
    g_b, beta_b = gates(b_b, a_b, a_log_b, dt_bias_b)
    o_fwd = gated_delta_rule_chunked(q, k, v, g_f, beta_f)
    flip = lambda t: jnp.flip(t, axis=2)
    o_bwd = flip(gated_delta_rule_chunked(flip(q), flip(k), flip(v), flip(g_b), flip(beta_b)))
    o = (o_fwd + o_bwd).transpose(0, 2, 1, 3)
    zf = z.astype(jnp.float32).reshape(bsz, s, GDN_HEADS, GDN_HEAD_DIM)
    o = rms_norm(o, norm_gain) * jax.nn.silu(zf)
    return o.reshape(bsz, s, GDN_WIDTH).astype(z.dtype)

def spatial_gating(u, v, v_gain, w_s, b_s, out_gain):
    bsz, s, _ = u.shape
    u = jax.nn.gelu(u, approximate=False).reshape(bsz, s, SGU_GROUPS, SGU_GROUP_DIM)
    v = jax.nn.gelu(v, approximate=False).reshape(bsz, s, SGU_GROUPS, SGU_GROUP_DIM)
    v = rms_norm(v, v_gain).reshape(bsz, s // SGU_CHUNK, SGU_CHUNK, SGU_GROUPS, SGU_GROUP_DIM)
    mixed = jnp.einsum("gts,bnsgc->bntgc", w_s, v) + b_s.T[:, :, None]
    gated = u * mixed.reshape(bsz, s, SGU_GROUPS, SGU_GROUP_DIM)
    return rms_norm(gated, out_gain).reshape(bsz, s, SGU_WIDTH)

def third_inputs(seed: int = 0) -> dict:
    key = jax.random.key(seed)
    ks = jax.random.split(key, 20)
    f32 = jnp.float32
    L = DEPTH
    x = jax.random.normal(ks[0], (BATCH, SEQ, D_MODEL), f32)
    norm_mix = 1.0 + 0.02 * jax.random.normal(ks[1], (L, D_MODEL), f32)
    w_in = jax.random.normal(ks[2], (L, D_MODEL, IN_COLS), f32) * D_MODEL ** -0.5
    conv_w = jax.random.normal(ks[3], (L, CONV_K, 3 * GDN_WIDTH), f32) * CONV_K ** -0.5

    def decay_params(k_a, k_dt):
        a_log = jnp.log(jax.random.uniform(k_a, (L, GDN_HEADS), f32, 1.0, 16.0))
        dt = jnp.exp(jax.random.uniform(k_dt, (L, GDN_HEADS), f32, math.log(1e-3), math.log(1e-1)))
        dt_bias = dt + jnp.log(-jnp.expm1(-dt))
        return a_log, dt_bias

    a_log_fwd, dt_bias_fwd = decay_params(ks[4], ks[5])
    a_log_bwd, dt_bias_bwd = decay_params(ks[6], ks[7])
    gdn_norm = 1.0 + 0.02 * jax.random.normal(ks[8], (L, GDN_HEAD_DIM), f32)
    sgu_v_norm = 1.0 + 0.02 * jax.random.normal(ks[9], (L, SGU_GROUPS, SGU_GROUP_DIM), f32)
    sgu_w = jax.random.normal(ks[10], (L, SGU_GROUPS, SGU_CHUNK, SGU_CHUNK), f32) * SGU_CHUNK ** -0.5
    sgu_b = 1.0 + 0.02 * jax.random.normal(ks[11], (L, SGU_GROUPS, SGU_CHUNK), f32)
    sgu_out_norm = 1.0 + 0.02 * jax.random.normal(ks[12], (L, SGU_GROUPS, SGU_GROUP_DIM), f32)
    w_out = jax.random.normal(ks[13], (L, MIX_WIDTH_3, D_MODEL), f32) * MIX_WIDTH_3 ** -0.5
    norm_ffn = 1.0 + 0.02 * jax.random.normal(ks[14], (L, D_MODEL), f32)
    w_ff1 = jax.random.normal(ks[15], (L, D_MODEL, FF_DIM), f32) * D_MODEL ** -0.5
    w_ff2 = jax.random.normal(ks[16], (L, FF_DIM, D_MODEL), f32) * FF_DIM ** -0.5
    norm_final = 1.0 + 0.02 * jax.random.normal(ks[17], (D_MODEL,), f32)
    return {"x": x, "norm_mix": norm_mix, "w_in": w_in, "conv_w": conv_w,
            "a_log_fwd": a_log_fwd, "dt_bias_fwd": dt_bias_fwd,
            "a_log_bwd": a_log_bwd, "dt_bias_bwd": dt_bias_bwd,
            "gdn_norm": gdn_norm, "sgu_v_norm": sgu_v_norm, "sgu_w": sgu_w, "sgu_b": sgu_b,
            "sgu_out_norm": sgu_out_norm, "w_out": w_out, "norm_ffn": norm_ffn,
            "w_ff1": w_ff1, "w_ff2": w_ff2, "norm_final": norm_final}

def third_block(x, norm_mix, w_in, conv_w, a_log_fwd, dt_bias_fwd, a_log_bwd, dt_bias_bwd,
              gdn_norm, sgu_v_norm, sgu_w, sgu_b, sgu_out_norm, w_out, norm_ffn,
              w_ff1, w_ff2, norm_final):
    for l in range(DEPTH):
        h = rms_norm(x, norm_mix[l])
        proj = jnp.einsum("bsd,dc->bsc", h, w_in[l])
        q, k, v, z, b_f, b_b, a_f, a_b, su, sv = jnp.split(proj, SPLIT_POINTS, axis=-1)
        qkv = jax.nn.silu(short_conv(jnp.concatenate([q, k, v], axis=-1), conv_w[l]))
        o_a = bidir_gated_deltanet(qkv, z, b_f, b_b, a_f, a_b, a_log_fwd[l], dt_bias_fwd[l],
                                   a_log_bwd[l], dt_bias_bwd[l], gdn_norm[l])
        o_b = spatial_gating(su, sv, sgu_v_norm[l], sgu_w[l], sgu_b[l], sgu_out_norm[l])
        mix = jnp.concatenate([o_a, o_b], axis=-1)
        x = x + jnp.einsum("bsc,cd->bsd", mix, w_out[l])
        h = rms_norm(x, norm_ffn[l])
        ff = jnp.square(jax.nn.relu(jnp.einsum("bsd,df->bsf", h, w_ff1[l])))
        x = x + jnp.einsum("bsf,fd->bsd", ff, w_ff2[l])
    return rms_norm(x, norm_final)


_first_inputs_3 = third_inputs


def third_inputs(seed=0):
    import zlib

    import numpy as np

    out = dict(_first_inputs_3(seed))
    spreads = {}
    factors = {'gdn_norm': 8.0,
     'sgu_v_norm': 6.292,
     'sgu_b': 7.79,
     'sgu_out_norm': 4.892,
     'norm_ffn': 3.634,
     'norm_final': 2.865}
    for name, (base, spread) in spreads.items():
        noise = np.random.default_rng([zlib.crc32(name.encode()), seed]).standard_normal(out[name].shape)
        drawn = base * np.exp(spread * noise) if base else spread * noise
        out[name] = __import__('jax').numpy.asarray(drawn.astype(out[name].dtype))
    for name, factor in factors.items():
        out[name] = (out[name] * factor).astype(out[name].dtype)
    return out


_narrow_inputs_3 = third_inputs


def third_inputs(seed=0):

    out = dict(_narrow_inputs_3(seed))
    wider = {'gdn_norm': 4.4,
     'sgu_v_norm': 5.69,
     'sgu_b': 6.55,
     'sgu_out_norm': 4.03,
     'norm_final': 3.2}
    for name, times in wider.items():
        mean = out[name].mean()
        out[name] = (mean + times * (out[name] - mean)).astype(out[name].dtype)
    return out


def setup_inputs(seed=0):
    out = dict(first_inputs(seed))
    for name, value in second_inputs(seed + 1).items():
        if name != "x":
            out[name + "_2"] = value
    for name, value in third_inputs(seed + 2).items():
        if name != "x":
            out[name + "_3"] = value
    return out


def reference(
    x, meta_tokens, norm_mix_g, w_in, lru_conv_w, lru_conv_b, lru_gate_a_w, lru_gate_a_b,
    lru_gate_x_w, lru_gate_x_b, lru_a_param, cc_conv_w, cc_conv_b, cc_ln_g, cc_ln_b,
    out_norm_lru_g, out_norm_cc_g, w_out, norm_mlp_g, w_mlp_up, w_mlp_down, norm_final_g,
    w_in_2, ln1_g_2, ln2_g_2, lnf_g_2, m_conv_2, m_b_i_2, m_b_f_2, m_ln_g_2, rw_mu_2, rw_w0_2,
    rw_w_up_2, rw_a0_2, rw_a_up_2, rw_g_up_2, rw_k_k_2, rw_k_a_2, rw_r_k_2, rw_ln_g_2,
    rw_ln_b_2, w_out_2, w_gate_2, w_up_2, w_down_2, norm_mix_3, w_in_3, conv_w_3, a_log_fwd_3,
    dt_bias_fwd_3, a_log_bwd_3, dt_bias_bwd_3, gdn_norm_3, sgu_v_norm_3, sgu_w_3, sgu_b_3,
    sgu_out_norm_3, w_out_3, norm_ffn_3, w_ff1_3, w_ff2_3, norm_final_3,
):
    x = first_block(
        x, meta_tokens, norm_mix_g, w_in, lru_conv_w, lru_conv_b, lru_gate_a_w, lru_gate_a_b,
        lru_gate_x_w, lru_gate_x_b, lru_a_param, cc_conv_w, cc_conv_b, cc_ln_g, cc_ln_b,
        out_norm_lru_g, out_norm_cc_g, w_out, norm_mlp_g, w_mlp_up, w_mlp_down, norm_final_g,
    )
    x = second_block(
        x, w_in_2, ln1_g_2, ln2_g_2, lnf_g_2, m_conv_2, m_b_i_2, m_b_f_2, m_ln_g_2, rw_mu_2,
        rw_w0_2, rw_w_up_2, rw_a0_2, rw_a_up_2, rw_g_up_2, rw_k_k_2, rw_k_a_2, rw_r_k_2,
        rw_ln_g_2, rw_ln_b_2, w_out_2, w_gate_2, w_up_2, w_down_2,
    )
    return third_block(
        x, norm_mix_3, w_in_3, conv_w_3, a_log_fwd_3, dt_bias_fwd_3, a_log_bwd_3, dt_bias_bwd_3,
        gdn_norm_3, sgu_v_norm_3, sgu_w_3, sgu_b_3, sgu_out_norm_3, w_out_3, norm_ffn_3,
        w_ff1_3, w_ff2_3, norm_final_3,
    )


_drawn_inputs = setup_inputs


def setup_inputs(seed=0):
    import zlib

    import numpy as np

    out = dict(_drawn_inputs(seed))
    spreads = {}
    factors = {'ln2_g_2': 2.879, 'norm_mix_3': 3.129, 'norm_ffn_3': 3.077, 'sgu_out_norm_3': 2.799}
    for name, (base, spread) in spreads.items():
        noise = np.random.default_rng([zlib.crc32(name.encode()), seed]).standard_normal(out[name].shape)
        drawn = base * np.exp(spread * noise) if base else spread * noise
        out[name] = __import__('jax').numpy.asarray(drawn.astype(out[name].dtype))
    for name, factor in factors.items():
        out[name] = (out[name] * factor).astype(out[name].dtype)
    return out
```

```python
from contextlib import ExitStack, contextmanager

import numpy as np
import concourse.bass as bass
from concourse import mybir

F32 = mybir.dt.float32
F32R = mybir.dt.float32r
ACT = mybir.ActivationFunctionType
ALU = mybir.AluOpType
ds = bass.ds

P = 128
D = 1024
KD = D // P
SEQ = 1024
META = 16
EPS = 1e-6
CH = 64
NCH = SEQ // CH
M_Q, M_K, M_V, M_O, R_Q, R_K, R_V, R_G, W_R, W_K, W_V, W_WA, W_GL, M_GATE = (
    0, 2, 4, 6, 8, 11, 14, 17, 20, 23, 26, 29, 30, 31)
G_Q, G_K, G_V, G_Z, G_SU, G_SV, G_GATE = 0, 4, 8, 12, 16, 20, 24
TILES_1, TILES_2, TILES_3 = 16, 32, 26


class Stage(dict):
    pass


class Shared:
    pass


@contextmanager
def stage(nc, name, *names):
    with ExitStack() as ctx:
        s = Stage((n, ctx.enter_context(nc.semaphore(f"{name}_{n}"))) for n in names)
        s.sb = lambda n, shape, dt=F32: ctx.enter_context(nc.sbuf_tensor(f"{name}_{n}", shape, dt))
        s.ps = lambda n, shape, dt=F32: ctx.enter_context(nc.psum_tensor(f"{name}_{n}", shape, dt))
        yield s
        clear(nc, s)


def clear(nc, s):
    with nc.Block() as block:
        @block.gpsimd
        def _(pool):
            for sem in list(s.values())[0::2]:
                pool.sem_clear(sem)

        @block.sync
        def _(sp):
            for sem in list(s.values())[1::2]:
                sp.sem_clear(sem)


def chain(eng, own):
    count = {}

    def link(ins, sem=None):
        sem = own if sem is None else sem
        count[id(sem)] = count.get(id(sem), 0) + 1
        ins.then_inc(sem, 1)
        eng.wait_ge(sem, count[id(sem)])

    return link


def own_chain(eng, s):
    eng.sem_clear(s["own"])
    return chain(eng, s["own"])


def cuts(T):
    n = 4 if T == SEQ + META else 2
    return n, T // n


def flat(ps, T):
    n, w = cuts(T)
    return ps[:, 0:n, 0:w]


def sliced(ap, T):
    n, w = cuts(T)
    return ap.rearrange("p (n w) -> p n w", n=n)


DENSE = ("landed0", "landed1", "hi0", "hi1", "lo0", "lo1", "done0", "done1", "free0", "free1",
         "stored0", "stored1", "own", "act")


def weight_buffers(s):
    s.raw = [s.sb(f"raw{b}", [P, KD, P]) for b in range(2)]
    s.whi = [s.sb(f"whi{b}", [P, KD, P], F32R) for b in range(2)]
    s.wlo = [s.sb(f"wlo{b}", [P, KD, P], F32R) for b in range(2)]
    s.psum = s.ps("acc", [P, 8, 512])
    s.landed, s.hi, s.lo = [s["landed0"], s["landed1"]], [s["hi0"], s["hi1"]], [s["lo0"], s["lo1"]]
    s.done, s.free, s.stored = [s["done0"], s["done1"]], [s["free0"], s["free1"]], [s["stored0"], s["stored1"]]


def grant(nc, s):
    with nc.Block() as block:
        @block.gpsimd
        def _(pool):
            for sem in (*s.lo, *s.done, *s.free, s["act"]):
                pool.sem_inc(sem, 1)
            for sem in s.stored:
                pool.sem_inc(sem, 16)


def load_tile(sp, s, b, it, src, kt):
    sp.wait_ge(s.lo[b], it + 1)
    sp.dma_start(s.raw[b][:, 0:kt, :], src).then_inc(s.landed[b], 16)


def split_hi(act, s, b, it, kt):
    act.wait_ge(s.landed[b], (it + 1) * 16)
    act.wait_ge(s.done[b], it + 1)
    act.activation(s.whi[b][:, 0:kt, :], s.raw[b][:, 0:kt, :], ACT.Copy).then_inc(s.hi[b], 1)


def split_lo(pool, s, b, it, kt):
    pool.wait_ge(s.hi[b], it + 1)
    pool.tensor_tensor(s.wlo[b][:, 0:kt, :], s.raw[b][:, 0:kt, :], s.whi[b][:, 0:kt, :].bitcast(F32),
                       ALU.subtract).then_inc(s.lo[b], 1)


def product(pe, s, b, it, hi, lo, T, kt):
    n, w = cuts(T)
    pe.wait_ge(s.lo[b], it + 2)
    pe.wait_ge(s.free[b], it + 1)
    for k in range(kt):
        for j in range(n):
            out = s.psum[:, 4 * b + j, 0:w]
            x_hi, x_lo = hi[:, k, j * w:j * w + w], lo[:, k, j * w:j * w + w]
            pe.matmul(out, s.whi[b][:, k, :], x_hi, start=(k == 0), stop=False)
            pe.matmul(out, s.whi[b][:, k, :], x_lo, start=False, stop=False)
            mm = pe.matmul(out, s.wlo[b][:, k, :], x_hi, start=False, stop=(k == kt - 1))
    mm.then_inc(s.done[b], 1)


def dense(nc, name, g, W, tiles, T, store=None):
    Wt = W.rearrange("(k p) c -> p k c", p=P)
    pairs = tiles // 2
    with stage(nc, name, *DENSE) as s:
        weight_buffers(s)
        stg = [s.sb(f"stg{b}", [P, T]) for b in range(2)] if store is not None else None
        grant(nc, s)
        with nc.Block() as block:
            @block.sync
            def _(sp):
                with sp.Fori(0, pairs) as i:
                    for b in range(2):
                        load_tile(sp, s, b, i, Wt[:, :, ds(i * (2 * P) + b * P, P)], KD)

            @block.scalar
            def _(act):
                def put(b, i):
                    act.wait_ge(s.free[b], i + 2)
                    act.dma_start(store[ds(i * (2 * P) + b * P, P), :], stg[b][:, :]).then_inc(s.stored[b], 16)

                if store is None:
                    with act.Fori(0, pairs) as i:
                        for b in range(2):
                            split_hi(act, s, b, i, KD)
                else:
                    for b in range(2):
                        split_hi(act, s, b, 0, KD)
                    with act.Fori(0, pairs - 1) as i:
                        for b in range(2):
                            put(b, i)
                            split_hi(act, s, b, i + 1, KD)
                    for b in range(2):
                        act.wait_ge(s.free[b], pairs + 1)
                        act.dma_start(store[((pairs - 1) * 2 + b) * P:((pairs - 1) * 2 + b + 1) * P, :],
                                      stg[b][:, :]).then_inc(s.stored[b], 16)
                    for b in range(2):
                        act.wait_ge(s.stored[b], 16 * pairs + 16)

            @block.gpsimd
            def _(pool):
                with pool.Fori(0, pairs) as i:
                    for b in range(2):
                        split_lo(pool, s, b, i, KD)

            @block.tensor
            def _(pe):
                with pe.Fori(0, pairs) as i:
                    for b in range(2):
                        product(pe, s, b, i, g.uhi, g.ulo, T, KD)

            @block.vector
            def _(dve):
                with dve.Fori(0, pairs) as i:
                    for b in range(2):
                        acc = flat(s.psum[:, 4 * b:4 * b + 4, :], T)
                        dve.wait_ge(s.done[b], i + 2)
                        if store is not None:
                            dve.wait_ge(s.stored[b], i * 16 + 16)
                            dve.tensor_copy(sliced(stg[b][:, :], T), acc).then_inc(s.free[b], 1)
                        else:
                            n, w = cuts(T)
                            h = g.h[:, ds(i * 2 + b, 1), 0:T].rearrange("p a (n w) -> p (a n) w", n=n)
                            dve.tensor_tensor(h, h, acc, ALU.add).then_inc(s.free[b], 1)


def ffn(nc, name, g, Wup, Wdown, groups, T, gated):
    up, down = (W.rearrange("(k p) c -> p k c", p=P) for W in (Wup, Wdown))
    n, w = cuts(T)
    with stage(nc, name, *DENSE) as s:
        weight_buffers(s)
        xhi = s.sb("xhi", [P, 8, T], F32R)
        xlo = s.sb("xlo", [P, 8, T], F32R)
        sq = s.sb("sq", [P, T])
        silu = s.sb("silu", [P, T]) if gated else None
        grant(nc, s)

        def walk(eng, do_up, do_down):
            before, tile = 0, 0
            for many, kt in groups:
                ups = kt if gated else kt // 2
                per = ups + KD // 2

                def one(o):
                    with eng.Fori(0, ups) as j:
                        do_up(j, o * per + before + j, o * kt + tile, kt, o)
                    with eng.Fori(0, KD // 2) as j:
                        do_down(j, o * per + before + ups + j, o * kt + tile, kt, o)

                if many > 1:
                    with eng.Fori(0, many) as o:
                        one(o)
                else:
                    one(0)
                before += many * per
                tile += many * kt

        with nc.Block() as block:
            @block.sync
            def _(sp):
                def do_up(j, it, tile, kt, o):
                    for b in range(2):
                        at = tile * (2 * P if gated else P) + j * (2 * P) + b * P
                        load_tile(sp, s, b, it, up[:, :, ds(at, P)], KD)

                def do_down(j, it, tile, kt, o):
                    for b in range(2):
                        load_tile(sp, s, b, it, down[:, ds(tile, kt), ds(j * (2 * P) + b * P, P)], kt)

                walk(sp, do_up, do_down)

            @block.scalar
            def _(act):
                def do_up(j, it, tile, kt, o):
                    for b in range(2):
                        split_hi(act, s, b, it, KD)
                    if gated:
                        act.wait_ge(s["done0"], it + 2)
                        act.wait_ge(s["free1"], it + 1)
                        act.activation(sliced(silu[:, :], T), flat(s.psum[:, 0:4, :], T), ACT.Silu)\
                           .then_inc(s["free0"], 1)

                def do_down(j, it, tile, kt, o):
                    for b in range(2):
                        split_hi(act, s, b, it, kt)

                walk(act, do_up, do_down)

            @block.gpsimd
            def _(pool):
                def do_up(j, it, tile, kt, o):
                    for b in range(2):
                        split_lo(pool, s, b, it, KD)

                def do_down(j, it, tile, kt, o):
                    for b in range(2):
                        split_lo(pool, s, b, it, kt)

                walk(pool, do_up, do_down)

            @block.tensor
            def _(pe):
                def do_up(j, it, tile, kt, o):
                    for b in range(2):
                        product(pe, s, b, it, g.uhi, g.ulo, T, KD)

                def do_down(j, it, tile, kt, o):
                    pe.wait_ge(s["act"], tile + (kt + 1))
                    for b in range(2):
                        product(pe, s, b, it, xhi, xlo, T, kt)

                walk(pe, do_up, do_down)

            @block.vector
            def _(dve):
                def split(link, m):
                    link(dve.tensor_copy(xhi[:, ds(m, 1), :], sq[:, None, :]))
                    dve.tensor_tensor(xlo[:, ds(m, 1), :], sq[:, None, :],
                                      xhi[:, ds(m, 1), :].bitcast(F32), ALU.subtract).then_inc(s["act"], 1)

                def do_up(j, it, tile, kt, o):
                    if gated:
                        link = own_chain(dve, s)
                        dve.wait_ge(s["free0"], it + 2)
                        dve.wait_ge(s["done1"], it + 2)
                        dve.wait_ge(s["act"], tile + j + 1)
                        dve.tensor_tensor(sliced(sq[:, :], T), sliced(silu[:, :], T),
                                          flat(s.psum[:, 4:8, :], T), ALU.mult).then_inc(s["free1"], 1)
                        dve.wait_ge(s["free1"], it + 2)
                        split(link, j)
                        return
                    for b in range(2):
                        link = own_chain(dve, s)
                        dve.wait_ge(s.done[b], it + 2)
                        dve.wait_ge(s["act"], tile + j * 2 + (b + 1))
                        dve.tensor_scalar(sliced(sq[:, :], T), flat(s.psum[:, 4 * b:4 * b + 4, :], T),
                                          0.0, None, ALU.max).then_inc(s.free[b], 1)
                        dve.wait_ge(s.free[b], it + 2)
                        link(dve.tensor_tensor(sq[:, :], sq[:, :], sq[:, :], ALU.mult))
                        split(link, j * 2 + b)

                def do_down(j, it, tile, kt, o):
                    for b in range(2):
                        dve.wait_ge(s.done[b], it + 2)
                        h = g.h[:, ds(j * 2 + b, 1), 0:T].rearrange("p a (n w) -> p (a n) w", n=n)
                        dve.tensor_tensor(h, h, flat(s.psum[:, 4 * b:4 * b + 4, :], T), ALU.add)\
                           .then_inc(s.free[b], 1)

                walk(dve, do_up, do_down)


def norm(nc, name, g, src, groups, gain, T, eps=EPS, first=0, dest="u"):
    with stage(nc, name, "squared", "summed", "shifted", "rooted", "own", "scaled", "upper", "lower", "out0",
               "out1") as s:
        sq = [s.sb(f"sq{b}", [P, T]) for b in range(2)]
        inv = s.sb("inv", [P, T])
        acc = s.ps("acc", [P, 8, 512])
        n, w = cuts(T)
        tiles = [(gi, k) for gi, (a, b) in enumerate(groups) for k in range(a, b)]
        x = lambda k: src[:, k, first:first + T]
        stored = [s["out0"], s["out1"]]
        with nc.Block() as block:
            @block.scalar
            def _(act):
                for gi, (a, b) in enumerate(groups):
                    for k in range(a, b):
                        if k >= 2:
                            act.wait_ge(s["summed"], k - 1)
                        if gi and k < a + 2:
                            act.wait_ge(s["scaled"], a)
                            act.wait_ge(s["upper"], a)
                            if dest == "u":
                                act.wait_ge(s["lower"], a)
                        act.activation(sq[k % 2][:, :], x(k), ACT.Square).then_inc(s["squared"], 1)
                    act.wait_ge(s["shifted"], gi + 1)
                    act.activation(inv[:, :], inv[:, :], ACT.Sqrt).then_inc(s["rooted"], 1)
                    for k in range(a, b):
                        if dest in ("u", "h"):
                            act.wait_ge(s["scaled"], k + 1)
                            out = g.uhi[:, k, 0:T] if dest == "u" else g.h[:, k, 0:T]
                            act.activation(out, sq[k % 2][:, :], ACT.Copy).then_inc(s["upper"], 1)

            @block.tensor
            def _(pe):
                for gi, (a, b) in enumerate(groups):
                    for k in range(a, b):
                        pe.wait_ge(s["squared"], k + 1)
                        for j in range(n):
                            mm = pe.matmul(acc[:, 4 * (gi % 2) + j, 0:w], g.ones[:, :], sq[k % 2][:, j * w:j * w + w],
                                           start=(k == a), stop=(k == b - 1))
                        mm.then_inc(s["summed"], 1)

            @block.vector
            def _(dve):
                link = chain(dve, s["own"])
                for gi, (a, b) in enumerate(groups):
                    dve.wait_ge(s["summed"], b)
                    dve.tensor_scalar(sliced(inv[:, :], T), flat(acc[:, 4 * (gi % 2):4 * (gi % 2) + 4, :], T),
                                      1.0 / ((b - a) * P), eps, ALU.mult, ALU.add).then_inc(s["shifted"], 1)
                    dve.wait_ge(s["rooted"], gi + 1)
                    link(dve.reciprocal(inv[:, :], inv[:, :]))
                    for k in range(a, b):
                        if dest == "u" and k - a >= 2:
                            dve.wait_ge(s["lower"], k - 1)
                        if dest == "h" and k - a >= 2:
                            dve.wait_ge(s["upper"], k - 1)
                        if dest not in ("u", "h") and k >= 2:
                            dve.wait_ge(stored[k % 2], 16 * (k // 2))
                        dve.scalar_tensor_tensor(sq[k % 2][:, :], x(k), g.par[:, gain + k:gain + k + 1],
                                                 inv[:, :], ALU.mult, ALU.mult).then_inc(s["scaled"], 1)
                    dve.wait_ge(s["scaled"], b)

            @block.gpsimd
            def _(pool):
                if dest == "u":
                    for gi, k in tiles:
                        pool.wait_ge(s["upper"], k + 1)
                        pool.tensor_tensor(g.ulo[:, k, 0:T], sq[k % 2][:, :], g.uhi[:, k, 0:T].bitcast(F32),
                                           ALU.subtract).then_inc(s["lower"], 1)

            @block.sync
            def _(sp):
                if dest not in ("u", "h"):
                    for gi, k in tiles:
                        sp.wait_ge(s["scaled"], k + 1)
                        sp.dma_start(dest[k * P:(k + 1) * P, :], sq[k % 2][:, :]).then_inc(stored[k % 2], 16)
                    for b in range(2):
                        sp.wait_ge(stored[b], 16 * (len(tiles) // 2))


T1 = SEQ + META
LRU_HALO, CC_HALO = 3, 30
LRU_PAR = 10


def lru(nc, g, proj, wa, wx):
    with stage(nc, "lru", "zero", "gated", "loaded", "par", "conv", "gates", "sig_a", "sig_x", "loga", "decay", "tanh", "gelu",
               "power", "root", "own", "y") as s:
        xl, xc = s.sb("xl", [P, LRU_HALO + T1]), s.sb("xc", [P, T1])
        gate, r, ig = s.sb("gate", [P, T1]), s.sb("r", [P, T1]), s.sb("ig", [P, T1])
        a, th = s.sb("a", [P, T1]), s.sb("th", [P, T1])
        w_a, w_x = s.sb("wa", [P, P]), s.sb("wx", [P, P])
        par, tiny = s.sb("par", [P, LRU_PAR]), s.sb("tiny", [P, 6])
        acc = s.ps("acc", [P, 8, 512])
        n, w = cuts(T1)
        with nc.Block() as block:
            @block.vector
            def _(dve):
                dve.memset(xl[:, 0:LRU_HALO], 0.0).then_inc(s["zero"], 1)
        with nc.Fori(0, 4) as i:
            with nc.Block() as block:
                @block.sync
                def _(sp):
                    sp.dma_start(xl[:, LRU_HALO:], proj[ds(i * P, P), :]).then_inc(s["loaded"], 16)
                    sp.dma_start(gate[:, :], proj[ds(i * P + 4 * P, P), :]).then_inc(s["loaded"], 16)
                    sp.dma_start(w_a[:, :], wa[ds(i * P, P), :]).then_inc(s["loaded"], 16)
                    sp.dma_start(w_x[:, :], wx[ds(i * P, P), :]).then_inc(s["loaded"], 16)

                @block.vector
                def _(dve):
                    link = chain(dve, s["own"])
                    link(dve.tensor_copy(par[:, :], g.par[:, ds(i * LRU_PAR + g.col["lru"], LRU_PAR)]), s["par"])
                    dve.wait_ge(s["loaded"], 64)
                    link(dve.tensor_scalar(xc[:, :], xl[:, 0:T1], par[:, 0:1], par[:, 4:5], ALU.mult, ALU.add))
                    for k in range(1, 4):
                        link(dve.scalar_tensor_tensor(xc[:, :], xl[:, k:k + T1], par[:, k:k + 1], xc[:, :],
                                                      ALU.mult, ALU.add), s["conv"] if k == 3 else None)
                    dve.wait_ge(s["power"], 1)
                    e, z, z2, q = tiny[:, 0:1], tiny[:, 1:2], tiny[:, 2:3], tiny[:, 3:4]
                    link(dve.tensor_scalar(z, e, 2.0, None, ALU.add))
                    link(dve.reciprocal(z, z))
                    link(dve.tensor_tensor(z, z, e, ALU.mult))
                    link(dve.tensor_tensor(z2, z, z, ALU.mult))
                    link(dve.tensor_scalar(q, z2, 1.0 / 15, 1.0 / 13, ALU.mult, ALU.add))
                    for m in (11, 9, 7, 5, 3, 1):
                        link(dve.tensor_tensor(q, q, z2, ALU.mult))
                        link(dve.tensor_scalar(q, q, 1.0 / m, None, ALU.add))
                    link(dve.tensor_tensor(q, q, z, ALU.mult))
                    link(dve.tensor_scalar(z, par[:, 7:8], -1.0, 0.0, ALU.mult, ALU.max))
                    link(dve.tensor_scalar(q, q, 2.0, z, ALU.mult, ALU.add))
                    link(dve.tensor_scalar(q, q, -8.0, None, ALU.mult))
                    dve.wait_ge(s["sig_a"], 1)
                    link(dve.tensor_scalar(r[:, :], r[:, :], q, None, ALU.mult), s["loga"])
                    dve.wait_ge(s["sig_x"], 1)
                    link(dve.tensor_tensor(ig[:, :], ig[:, :], xc[:, :], ALU.mult))
                    dve.wait_ge(s["decay"], 1)
                    link(dve.tensor_tensor(xc[:, :], a[:, :], a[:, :], ALU.mult))
                    dve.wait_ge(s["tanh"], 1)
                    link(dve.scalar_tensor_tensor(th[:, :], xc[:, :], 1.0, th[:, :], ALU.add, ALU.mult), s["gates"])
                    dve.wait_ge(s["root"], 1)
                    link(dve.tensor_tensor(ig[:, :], ig[:, :], th[:, :], ALU.mult))
                    link(dve.tensor_tensor_scan(xc[:, :], a[:, :], ig[:, :], 0.0, ALU.mult, ALU.add))
                    dve.wait_ge(s["gelu"], 1)
                    dve.tensor_tensor(g.y[:, ds(i, 1), :], xc[:, None, :], gate[:, None, :], ALU.mult)\
                       .then_inc(s["y"], 1)

                @block.tensor
                def _(pe):
                    pe.wait_ge(s["conv"], 1)
                    pe.wait_ge(s["loaded"], 64)
                    for b, wt in enumerate((w_a, w_x)):
                        for j in range(n):
                            mm = pe.matmul(acc[:, 4 * b + j, 0:w], wt[:, :], xc[:, j * w:j * w + w],
                                           start=True, stop=True)
                        mm.then_inc(s["gated"], 1)

                @block.scalar
                def _(act):
                    act.wait_ge(s["loaded"], 64)
                    act.activation(gate[:, :], gate[:, :], ACT.Gelu_apprx_tanh).then_inc(s["gelu"], 1)
                    act.wait_ge(s["par"], 1)
                    act.activation(tiny[:, 0:1], par[:, 7:8], ACT.Abs).then_inc(s["y"], 1)
                    act.wait_ge(s["y"], 1)
                    act.activation(tiny[:, 0:1], tiny[:, 0:1], ACT.Exp, scale=-1.0).then_inc(s["power"], 1)
                    act.wait_ge(s["gated"], 2)
                    act.activation(sliced(r[:, :], T1), flat(acc[:, 0:4, :], T1), ACT.Sigmoid,
                                   bias=par[:, 5:6]).then_inc(s["sig_a"], 1)
                    act.activation(sliced(ig[:, :], T1), flat(acc[:, 4:8, :], T1), ACT.Sigmoid,
                                   bias=par[:, 6:7]).then_inc(s["sig_x"], 1)
                    act.wait_ge(s["loga"], 1)
                    act.activation(a[:, :], r[:, :], ACT.Exp).then_inc(s["decay"], 1)
                    act.activation(th[:, :], r[:, :], ACT.Tanh, scale=-1.0).then_inc(s["tanh"], 1)
                    act.wait_ge(s["gates"], 1)
                    act.activation(th[:, :], th[:, :], ACT.Sqrt).then_inc(s["root"], 1)
            clear(nc, s)


CC_TAPS = 31
CC_PAR = CC_TAPS + 1


def conv_mixer(nc, g, proj):
    with stage(nc, "cc", "zero", "loaded", "par", "sig", "own", "y") as s:
        v, gate, par = s.sb("v", [P, CC_HALO + T1]), s.sb("gate", [P, T1]), s.sb("par", [P, CC_PAR])
        acc = s.sb("acc", [P, T1])
        with nc.Block() as block:
            @block.vector
            def _(dve):
                dve.memset(v[:, 0:CC_HALO], 0.0).then_inc(s["zero"], 1)
        with nc.Fori(0, 4) as i:
            with nc.Block() as block:
                @block.sync
                def _(sp):
                    sp.dma_start(v[:, CC_HALO:], proj[ds(i * P + 8 * P, P), :]).then_inc(s["loaded"], 16)
                    sp.dma_start(gate[:, :], proj[ds(i * P + 12 * P, P), :]).then_inc(s["loaded"], 16)

                @block.scalar
                def _(act):
                    act.wait_ge(s["loaded"], 32)
                    act.activation(gate[:, :], gate[:, :], ACT.Sigmoid).then_inc(s["sig"], 1)

                @block.vector
                def _(dve):
                    link = chain(dve, s["own"])
                    link(dve.tensor_copy(par[:, :], g.par[:, ds(i * CC_PAR + g.col["cc"], CC_PAR)]))
                    dve.wait_ge(s["loaded"], 32)
                    dve.wait_ge(s["sig"], 1)
                    link(dve.tensor_tensor(v[:, CC_HALO:], v[:, CC_HALO:], gate[:, :], ALU.mult))
                    link(dve.tensor_scalar(acc[:, :], v[:, 0:T1], par[:, 0:1], par[:, CC_TAPS:CC_TAPS + 1],
                                           ALU.mult, ALU.add))
                    for k in range(1, CC_TAPS):
                        last = k == CC_TAPS - 1
                        out = g.y[:, ds(i + 4, 1), :] if last else acc[:, None, :]
                        link(dve.scalar_tensor_tensor(out, v[:, None, k:k + T1], par[:, k:k + 1],
                                                      acc[:, None, :], ALU.mult, ALU.add))
            clear(nc, s)
    with stage(nc, "ccln", "summed", "centred", "squared", "shifted", "rooted", "scaled", "own", "silu") as s:
        acc = s.ps("acc", [P, 8, 512])
        mean, inv = s.sb("mean", [P, T1]), s.sb("inv", [P, T1])
        sq = [s.sb(f"sq{b}", [P, T1]) for b in range(2)]
        n, w = cuts(T1)
        with nc.Block() as block:
            @block.tensor
            def _(pe):
                for k in range(4):
                    for j in range(n):
                        mm = pe.matmul(acc[:, j, 0:w], g.ones[:, :], g.y[:, 4 + k, j * w:j * w + w],
                                       start=(k == 0), stop=(k == 3))
                mm.then_inc(s["summed"], 1)
                for k in range(4):
                    pe.wait_ge(s["squared"], k + 1)
                    for j in range(n):
                        mm = pe.matmul(acc[:, 4 + j, 0:w], g.ones[:, :], sq[k % 2][:, j * w:j * w + w],
                                       start=(k == 0), stop=(k == 3))
                    mm.then_inc(s["summed"], 1)

            @block.vector
            def _(dve):
                link = chain(dve, s["own"])
                dve.wait_ge(s["summed"], 1)
                link(dve.tensor_scalar(sliced(mean[:, :], T1), flat(acc[:, 0:4, :], T1), 1.0 / (4 * P), None,
                                       ALU.mult))
                for k in range(4):
                    dve.tensor_tensor(g.y[:, 4 + k, :], g.y[:, 4 + k, :], mean[:, :], ALU.subtract)\
                       .then_inc(s["centred"], 1)
                dve.wait_ge(s["centred"], 4)
                dve.wait_ge(s["summed"], 5)
                dve.tensor_scalar(sliced(inv[:, :], T1), flat(acc[:, 4:8, :], T1), 1.0 / (4 * P), EPS,
                                  ALU.mult, ALU.add).then_inc(s["shifted"], 1)
                dve.wait_ge(s["rooted"], 1)
                link(dve.reciprocal(inv[:, :], inv[:, :]))
                for k in range(4):
                    link(dve.scalar_tensor_tensor(g.y[:, 4 + k, :], g.y[:, 4 + k, :],
                                                  g.par[:, g.col["ccg"] + k:g.col["ccg"] + k + 1], inv[:, :],
                                                  ALU.mult, ALU.mult), s["scaled"])

            @block.scalar
            def _(act):
                for k in range(4):
                    act.wait_ge(s["centred"], k + 1)
                    if k >= 2:
                        act.wait_ge(s["summed"], k)
                    act.activation(sq[k % 2][:, :], g.y[:, 4 + k, :], ACT.Square).then_inc(s["squared"], 1)
                act.wait_ge(s["shifted"], 1)
                act.activation(inv[:, :], inv[:, :], ACT.Sqrt).then_inc(s["rooted"], 1)
                for k in range(4):
                    act.wait_ge(s["scaled"], k + 1)
                    act.activation(g.y[:, 4 + k, :], g.y[:, 4 + k, :], ACT.Silu,
                                   bias=g.par[:, g.col["ccb"] + k:g.col["ccb"] + k + 1]).then_inc(s["silu"], 1)


def block1(nc, g, a, proj):
    with g.parts("a1"):
        norm(nc, "n1", g, g.h, [(0, KD)], g.col["g1"], T1)
        dense(nc, "in1", g, a["w_in"], TILES_1, T1, proj)
    with nc.sbuf_tensor("y1", [P, KD, T1], F32) as y:
        g.y = y
        lru(nc, g, proj, a["lru_wa"], a["lru_wx"])
        conv_mixer(nc, g, proj)
        with g.parts("b1"):
            norm(nc, "no1", g, g.y, [(0, 4), (4, KD)], g.col["go1"], T1)
            dense(nc, "out1", g, a["w_out"], KD, T1)
    with g.parts("c1"):
        norm(nc, "nm1", g, g.h, [(0, KD)], g.col["gm1"], T1)
        ffn(nc, "ff1", g, a["w_mlp_up"], a["w_mlp_down"], [(4, KD)], T1, gated=False)
    norm(nc, "nf1", g, g.h, [(0, KD)], g.col["gf1"], SEQ, first=META, dest="h")


def halves(ap):
    return ap.rearrange("p (n w) -> p n w", n=2)


def conv_silu(nc, name, proj, tiles, taps, lead, g, col, par_cols):
    with stage(nc, name, "zero", "loaded", "own", "conv", "silu", "stored") as s:
        x, y, par = s.sb("x", [P, taps - 1 + SEQ]), s.sb("y", [P, SEQ]), s.sb("par", [P, par_cols])
        with nc.Block() as block:
            @block.vector
            def _(dve):
                dve.memset(x[:, :], 0.0).then_inc(s["zero"], 1)
        with nc.Fori(0, tiles) as i:
            with nc.Block() as block:
                @block.sync
                def _(sp):
                    sp.dma_start(x[:, lead:lead + SEQ], proj[ds(i * P, P), :]).then_inc(s["loaded"], 16)
                    sp.wait_ge(s["silu"], 1)
                    sp.dma_start(proj[ds(i * P, P), :], y[:, :]).then_inc(s["stored"], 16)
                    sp.wait_ge(s["stored"], 16)

                @block.vector
                def _(dve):
                    link = chain(dve, s["own"])
                    link(dve.tensor_copy(par[:, :], g.par[:, ds(i * par_cols + g.col[col], par_cols)]))
                    dve.wait_ge(s["loaded"], 16)
                    link(dve.tensor_scalar(y[:, :], x[:, 0:SEQ], par[:, 0:1], None, ALU.mult))
                    for k in range(1, taps):
                        link(dve.scalar_tensor_tensor(y[:, :], x[:, k:k + SEQ], par[:, k:k + 1], y[:, :],
                                                      ALU.mult, ALU.add), s["conv"] if k == taps - 1 else None)

                @block.scalar
                def _(act):
                    act.wait_ge(s["conv"], 1)
                    act.activation(y[:, :], y[:, :], ACT.Silu).then_inc(s["silu"], 1)
            clear(nc, s)


def rotate(nc, g, proj, cos, sin, swap):
    with stage(nc, "rot", "const", "loaded", "swapped", "own", "rotated", "stored") as s:
        c, sn, sw = s.sb("c", [P, SEQ]), s.sb("s", [P, SEQ]), s.sb("sw", [P, P])
        x, y = s.sb("x", [P, SEQ]), s.sb("y", [P, SEQ])
        acc = s.ps("acc", [P, 2, 512])
        with nc.Block() as block:
            @block.sync
            def _(sp):
                for t, src in ((c, cos), (sn, sin), (sw, swap)):
                    sp.dma_start(t[:, :], src).then_inc(s["const"], 16)
                sp.wait_ge(s["const"], 48)
        with nc.Fori(0, 6) as i:
            with nc.Block() as block:
                @block.sync
                def _(sp):
                    sp.dma_start(x[:, :], proj[ds(i * P + R_Q * P, P), :]).then_inc(s["loaded"], 16)
                    sp.wait_ge(s["rotated"], 1)
                    sp.dma_start(proj[ds(i * P + R_Q * P, P), :], y[:, :]).then_inc(s["stored"], 16)
                    sp.wait_ge(s["stored"], 16)

                @block.tensor
                def _(pe):
                    pe.wait_ge(s["loaded"], 16)
                    for j in range(2):
                        mm = pe.matmul(acc[:, j, :], sw[:, :], x[:, j * 512:j * 512 + 512], start=True, stop=True)
                    mm.then_inc(s["swapped"], 1)

                @block.vector
                def _(dve):
                    link = chain(dve, s["own"])
                    dve.wait_ge(s["swapped"], 1)
                    link(dve.tensor_tensor(halves(y[:, :]), acc[:, :, :], halves(sn[:, :]), ALU.mult))
                    link(dve.tensor_tensor(x[:, :], x[:, :], c[:, :], ALU.mult))
                    link(dve.tensor_tensor(y[:, :], y[:, :], x[:, :], ALU.add), s["rotated"])
            clear(nc, s)


def mlstm_gates(nc, g, proj, rows):
    with stage(nc, "mg", "loaded", "own", "abs", "power", "log", "sum", "em", "stored") as s:
        names = ("gi", "gf", "l", "m", "b", "c", "top", "one")
        gi, gf, l, m, b, c, top, one = (s.sb(n, [4, SEQ]) for n in names)
        with nc.Block() as block:
            @block.sync
            def _(sp):
                at = M_GATE * P
                sp.dma_start(gi[:, :], proj[at:at + 4, :]).then_inc(s["loaded"], 16)
                sp.dma_start(gf[:, :], proj[at + 4:at + 8, :]).then_inc(s["loaded"], 16)
                sp.wait_ge(s["sum"], 1)
                sp.dma_start(rows[0:4, :], top[:, :]).then_inc(s["stored"], 16)
                sp.dma_start(rows[8:12, :], c[:, :]).then_inc(s["stored"], 16)
                sp.wait_ge(s["em"], 1)
                sp.dma_start(rows[4:8, :], b[:, :]).then_inc(s["stored"], 16)
                sp.wait_ge(s["stored"], 48)

            @block.scalar
            def _(act):
                bf = g.par[0:4, g.col["mb"] + 1:g.col["mb"] + 2]
                act.wait_ge(s["loaded"], 32)
                act.activation(l[:, :], gf[:, :], ACT.Abs, bias=bf).then_inc(s["abs"], 1)
                act.wait_ge(s["abs"], 1)
                act.activation(l[:, :], l[:, :], ACT.Exp, scale=-1.0).then_inc(s["power"], 1)
                act.wait_ge(s["power"], 1)
                act.activation(l[:, :], l[:, :], ACT.Ln, bias=1.0).then_inc(s["log"], 1)
                act.wait_ge(s["sum"], 1)
                act.activation(b[:, :], m[:, :], ACT.Exp).then_inc(s["em"], 1)

            @block.vector
            def _(dve):
                link = chain(dve, s["own"])
                bi, bf = (g.par[0:4, g.col["mb"] + k:g.col["mb"] + k + 1] for k in range(2))
                link(dve.memset(one[:, :], 1.0))
                dve.wait_ge(s["loaded"], 32)
                link(dve.tensor_scalar(m[:, :], gf[:, :], bf, 0.0, ALU.add, ALU.min))
                dve.wait_ge(s["log"], 1)
                link(dve.tensor_tensor(m[:, :], m[:, :], l[:, :], ALU.subtract))
                link(dve.tensor_tensor_scan(b[:, :], one[:, :], m[:, :], 0.0, ALU.mult, ALU.add))
                link(dve.scalar_tensor_tensor(c[:, :], gi[:, :], bi, b[:, :], ALU.add, ALU.subtract))
                link(dve.tensor_tensor_scan(top[:, :], c[:, :], c[:, :], -3e38, ALU.max, ALU.max))
                link(dve.scalar_tensor_tensor(m[:, :], b[:, :], -1.0, top[:, :], ALU.mult, ALU.subtract))
                link(dve.tensor_scalar(top[:, :], top[:, :], -1.0, None, ALU.mult), s["sum"])


def attention(nc, name, g, proj, y, heads, q0, k0, v0, y0, rows=None, tri=None, ramps=None):
    lstm = rows is not None
    steps = []
    for n in range(2):
        for sb in range(4 * n + 4):
            j0 = max(sb * P, 512 * n)
            steps.append((n, sb, j0, 512 * (n + 1) - j0))
    last = [max(t for t, st in enumerate(steps) if st[0] == n) for n in range(2)]
    with stage(nc, name, "loaded", "turned", "values", "arg", "weight", "score", "prob", "out", "own", "result",
               "stored", "one") as s:
        q, k, v = (s.sb(n, [64, SEQ]) for n in "qkv")
        cv = 128 if lstm else 64
        vt = s.sb("vt", [P, 8, cv])
        e = [s.sb(f"e{b}", [P, 512]) for b in range(2)] if lstm else None
        pr = [s.sb(f"p{b}", [P, 512]) for b in range(2)]
        res = s.sb("res", [64, SEQ])
        turned = s.ps("turned", [P, 8, 64])
        sc = s.ps("score", [P, 2, 512])
        o = s.ps("o", [P, 2, 512])
        if lstm:
            mb, em, ck, tr = s.sb("mb", [P, SEQ]), s.sb("em", [P, SEQ]), s.sb("ck", [P, 8]), s.sb("tri", [P, 512])
            den, rec = s.sb("den", [P, 512]), s.sb("rec", [64, 512])
        else:
            ramp = s.sb("ramp", [P, SEQ])
        n_loads = 6 if lstm else 4
        with nc.Block() as block:
            @block.sync
            def _(sp):
                if lstm:
                    sp.dma_start(tr[:, :], tri).then_inc(s["loaded"], 16)
                    sp.wait_ge(s["loaded"], 16)

            @block.vector
            def _(dve):
                if lstm:
                    dve.memset(vt[:, :, 64:128], 1.0).then_inc(s["one"], 1)
        clear(nc, s)
        with nc.Fori(0, heads) as h:
            with nc.Block() as block:
                @block.sync
                def _(sp):
                    for t, at in ((v, v0), (k, k0), (q, q0)):
                        sp.dma_start(t[:, :], proj[ds(h * 64 + at, 64), :]).then_inc(s["loaded"], 16)
                    if lstm:
                        sp.dma_start(mb[:, :], rows[ds(h, 1), :].broadcast_to([P, SEQ])).then_inc(s["loaded"], 16)
                        sp.dma_start(em[64:128, :], rows[ds(h + 4, 1), :].broadcast_to([64, SEQ]))\
                          .then_inc(s["loaded"], 16)
                        sp.dma_start(ck[:, :], rows[ds(h + 8, 1), :].rearrange("a (s p) -> p (a s)", p=P),
                                     allow_slow_non_contiguous=True)\
                          .then_inc(s["loaded"], 16)
                    else:
                        sp.dma_start(ramp[:, :], ramps[ds(h * P, P), :]).then_inc(s["loaded"], 16)
                    sp.wait_ge(s["result"], 2)
                    sp.dma_start(y[ds(h * 64 + y0, 64), :], res[:, :]).then_inc(s["stored"], 16)
                    sp.wait_ge(s["stored"], 16)

                @block.tensor
                def _(pe):
                    pe.wait_ge(s["loaded"], 16 * n_loads)
                    for b in range(8):
                        mm = pe.transpose(turned[:, b, :], v[:, b * P:(b + 1) * P], g.ident[0:64, 0:64])
                    mm.then_inc(s["turned"], 1)

                    def values(t):
                        n, sb, j0, w = steps[t]
                        pe.wait_ge(s["values"], 1)
                        pe.wait_ge(s["prob"], t + 1)
                        mm = pe.matmul(o[0:cv, n, j0 - 512 * n:512], vt[:, sb, :], pr[t % 2][:, 0:w],
                                       start=(sb == 0), stop=(t == last[n]))
                        mm.then_inc(s["out"], 1)

                    for t, (n, sb, j0, w) in enumerate(steps):
                        if t >= 2:
                            pe.wait_ge(s["prob"], t - 1)
                        pe.matmul(sc[:, t % 2, 0:w], k[:, sb * P:(sb + 1) * P], q[:, j0:j0 + w],
                                  start=True, stop=True).then_inc(s["score"], 1)
                        if t:
                            values(t - 1)
                    values(len(steps) - 1)

                if lstm:
                    @block.scalar
                    def _(act):
                        for t, (n, sb, j0, w) in enumerate(steps):
                            act.wait_ge(s["arg"], t + 1)
                            act.activation(e[t % 2][:, 0:w], e[t % 2][:, 0:w], ACT.Exp).then_inc(s["weight"], 1)

                @block.vector
                def _(dve):
                    link = chain(dve, s["own"])
                    dve.wait_ge(s["loaded"], 16 * n_loads)
                    dve.wait_ge(s["turned"], 1)
                    dve.tensor_copy(vt[:, :, 0:64], turned[:, :, :]).then_inc(s["values"], 1)

                    def arg(t):
                        n, sb, j0, w = steps[t]
                        if t >= 2:
                            dve.wait_ge(s["prob"], t - 1)
                        if j0 == sb * P:
                            ins = dve.scalar_tensor_tensor(e[t % 2][:, 0:w], mb[:, j0:j0 + w], ck[:, sb:sb + 1],
                                                           tr[:, 0:w], ALU.add, ALU.min)
                        else:
                            ins = dve.tensor_scalar(e[t % 2][:, 0:w], mb[:, j0:j0 + w], ck[:, sb:sb + 1], 0.0,
                                                    ALU.add, ALU.min)
                        ins.then_inc(s["arg"], 1)

                    if lstm:
                        arg(0)
                    for t, (n, sb, j0, w) in enumerate(steps):
                        if lstm and t + 1 < len(steps):
                            arg(t + 1)
                        dve.wait_ge(s["score"], t + 1)
                        if t >= 2:
                            dve.wait_ge(s["out"], t - 1)
                        if lstm:
                            dve.wait_ge(s["weight"], t + 1)
                            dve.scalar_tensor_tensor(pr[t % 2][:, 0:w], sc[:, t % 2, 0:w], 0.125,
                                                     e[t % 2][:, 0:w], ALU.mult, ALU.mult).then_inc(s["prob"], 1)
                        else:
                            at = j0 - sb * P
                            dve.tensor_tensor(pr[t % 2][:, 0:w], sc[:, t % 2, 0:w], ramp[:, at:at + w],
                                              ALU.mult).then_inc(s["prob"], 1)
                        if t == last[n]:
                            dve.wait_ge(s["out"], t + 1)
                            r = res[:, 512 * n:512 * n + 512]
                            if lstm:
                                dn = den[64:128, :]
                                link(dve.scalar_tensor_tensor(dn, o[64:128, n, :], -1.0,
                                                              em[64:128, 512 * n:512 * n + 512],
                                                              ALU.mult, ALU.max))
                                link(dve.tensor_tensor(dn, o[64:128, n, :], dn, ALU.max))
                                link(dve.reciprocal(rec[:, :], den[64:128, :]))
                                dve.tensor_tensor(r, o[0:64, n, :], rec[:, :], ALU.mult).then_inc(s["result"], 1)
                            else:
                                dve.tensor_copy(r, o[0:64, n, :]).then_inc(s["result"], 1)
            clear(nc, s)


def head_norm(nc, name, g, src, tiles, y0, eps, gate_rows, act_gate, center=True, gain=None, bias=None,
              extra=None, src2=None):
    with stage(nc, name, "loaded", "summed", "centred", "squared", "var", "shifted", "rooted", "gate", "own",
               "par") as s:
        x, gt, sq, par = s.sb("x", [P, SEQ]), s.sb("gate", [P, SEQ]), s.sb("sq", [P, SEQ]), s.sb("par", [P, 2])
        ex = s.sb("ex", [P, SEQ])
        acc = s.ps("acc", [P, 4, 512])
        loads = [(x, src, y0 if src2 is None else 0), (gt, *gate_rows)]
        if extra is not None:
            loads.append((ex, extra, 0))
        if src2 is not None:
            loads.append((ex, src2, 0))
        with nc.Fori(0, tiles) as i:
            with nc.Block() as block:
                @block.sync
                def _(sp):
                    for t, a, at in loads:
                        sp.dma_start(t[:, :], a[ds(i * P + at * P, P), :]).then_inc(s["loaded"], 16)

                @block.tensor
                def _(pe):
                    pe.wait_ge(s["centred"], 1)
                    if center:
                        for j in range(2):
                            mm = pe.matmul(acc[:, j, :], g.mean64[:, :], x[:, j * 512:j * 512 + 512],
                                           start=True, stop=True)
                        mm.then_inc(s["summed"], 1)
                    pe.wait_ge(s["squared"], 1)
                    for j in range(2):
                        mm = pe.matmul(acc[:, 2 + j, :], g.mean64[:, :], sq[:, j * 512:j * 512 + 512],
                                       start=True, stop=True)
                    mm.then_inc(s["var"], 1)

                @block.vector
                def _(dve):
                    link = chain(dve, s["own"])
                    if gain is not None:
                        link(dve.tensor_copy(par[:, 0:1], g.par[:, ds(i + g.col[gain], 1)]))
                    if bias is not None:
                        link(dve.tensor_copy(par[:, 1:2], g.par[:, ds(i + g.col[bias], 1)]))
                    dve.wait_ge(s["loaded"], 16 * len(loads))
                    if src2 is not None:
                        link(dve.tensor_tensor(x[:, :], x[:, :], ex[:, :], ALU.add))
                    link(dve.tensor_copy(par[:, 0:1], par[:, 0:1] if gain is not None else g.ones[:, 0:1]),
                         s["centred"])
                    if center:
                        dve.wait_ge(s["summed"], 1)
                        link(dve.tensor_tensor(halves(x[:, :]), halves(x[:, :]), acc[:, 0:2, :], ALU.subtract))
                    link(dve.tensor_tensor(sq[:, :], x[:, :], x[:, :], ALU.mult), s["squared"])
                    dve.wait_ge(s["var"], 1)
                    link(dve.tensor_scalar(halves(sq[:, :]), acc[:, 2:4, :], eps, None, ALU.add), s["shifted"])
                    dve.wait_ge(s["rooted"], 1)
                    link(dve.reciprocal(sq[:, :], sq[:, :]))
                    if gain is not None:
                        link(dve.scalar_tensor_tensor(x[:, :], x[:, :], par[:, 0:1], sq[:, :],
                                                      ALU.mult, ALU.mult))
                    else:
                        link(dve.tensor_tensor(x[:, :], x[:, :], sq[:, :], ALU.mult))
                    if extra is not None:
                        link(dve.scalar_tensor_tensor(x[:, :], x[:, :], par[:, 1:2], ex[:, :],
                                                      ALU.add, ALU.add))
                    dve.wait_ge(s["gate"], 1)
                    link(dve.tensor_tensor(g.y[:, ds(i + y0, 1), 0:SEQ], x[:, None, :], gt[:, None, :],
                                           ALU.mult))

                @block.scalar
                def _(act):
                    act.wait_ge(s["loaded"], 16 * len(loads))
                    act.activation(gt[:, :], gt[:, :], act_gate).then_inc(s["gate"], 1)
                    act.wait_ge(s["shifted"], 1)
                    act.activation(sq[:, :], sq[:, :], ACT.Sqrt).then_inc(s["rooted"], 1)
            clear(nc, s)


W_PAR = 8


def shifted(link, dve, x, d, mu, out, sem=None):
    link(dve.tensor_tensor(d, x[:, 0:SEQ], x[:, 1:SEQ + 1], ALU.subtract))
    link(dve.scalar_tensor_tensor(out, d, mu, x[:, 1:SEQ + 1], ALU.mult, ALU.add), sem)


def rwkv_inputs(nc, g, a, proj, rw, gate, extra):
    with stage(nc, "wp", "const", "zero", "loaded", "shift", "own", "tanh", "sig", "proj", "sw", "sa", "g_out",
               "cum", "ep", "en", "diff", "el", "sqkk", "normed", "root", "prod", "bonus", "extra", "stored") as s:
        x = [s.sb(f"x{n}", [P, 1 + SEQ]) for n in range(3)]
        d, wa, gl = s.sb("d", [P, SEQ]), s.sb("wal", [P, SEQ]), s.sb("gll", [P, SEQ])
        lora = [s.sb(f"lora{n}", [P, P]) for n in range(3)]
        par, reset = s.sb("par", [P, W_PAR]), s.sb("reset", [P, SEQ])
        r, k, av, lw, cum, eP, eN = (s.sb(n, [P, SEQ]) for n in ("r", "k", "a", "lw", "cum", "eP", "eN"))
        acc = s.ps("acc", [P, 8, 512])
        with nc.Block() as block:
            @block.sync
            def _(sp):
                sp.dma_start(reset[:, :], a["reset"]).then_inc(s["const"], 16)
                sp.wait_ge(s["zero"], 3)
                sp.dma_start(x[0][:, 1:], proj[W_WA * P:W_WA * P + P, :]).then_inc(s["loaded"], 16)
                sp.dma_start(x[1][:, 1:], proj[W_GL * P:W_GL * P + P, :]).then_inc(s["loaded"], 16)
                sp.wait_ge(s["const"], 16)

            @block.vector
            def _(dve):
                link = chain(dve, s["own"])
                for n in range(3):
                    link(dve.memset(x[n][:, 0:1], 0.0), s["zero"])
                dve.wait_ge(s["loaded"], 32)
                c = g.col["wmu"]
                shifted(link, dve, x[0], d[:, :], g.par[:, c:c + 1], wa[:, :], s["shift"])
                shifted(link, dve, x[1], d[:, :], g.par[:, c + 1:c + 2], gl[:, :], s["shift"])

            @block.scalar
            def _(act):
                act.wait_ge(s["shift"], 1)
                act.activation(wa[0:64, :], wa[0:64, :], ACT.Tanh).then_inc(s["tanh"], 1)
                act.wait_ge(s["shift"], 2)
                act.activation(gl[:, :], gl[:, :], ACT.Sigmoid).then_inc(s["sig"], 1)
        clear(nc, s)
        with nc.Fori(0, 3) as i:
            with nc.Block() as block:
                @block.sync
                def _(sp):
                    for n, name in enumerate(("w_up", "a_up", "g_up")):
                        sp.dma_start(lora[n][:, :], a[name][ds(i * P, P), :]).then_inc(s["const"], 16)
                    for n, t in enumerate((W_R, W_K, W_V)):
                        sp.dma_start(x[n][:, 1:], proj[ds(i * P + t * P, P), :]).then_inc(s["loaded"], 16)
                    sp.wait_ge(s["g_out"], 1)
                    sp.dma_start(gate[ds(i * P, P), :], av[:, :]).then_inc(s["stored"], 16)
                    sp.wait_ge(s["extra"], 1)
                    sp.dma_start(extra[ds(i * P, P), :], lw[:, :]).then_inc(s["stored"], 16)
                    sp.wait_ge(s["stored"], 32)

                @block.tensor
                def _(pe):
                    pe.wait_ge(s["const"], 48)
                    for n, src in enumerate((wa, wa, gl)):
                        for j in range(2):
                            mm = pe.matmul(acc[:, 2 * n + j, :], lora[n][:, :], src[:, j * 512:j * 512 + 512],
                                           start=True, stop=True)
                        mm.then_inc(s["proj"], 1)
                    for sem in (s["sqkk"], s["prod"]):
                        pe.wait_ge(sem, 1)
                        for j in range(2):
                            mm = pe.matmul(acc[:, 6 + j, :], g.mean64[:, :], d[:, j * 512:j * 512 + 512],
                                           start=True, stop=True)
                        mm.then_inc(s["normed"], 1)

                @block.scalar
                def _(act):
                    act.wait_ge(s["loaded"], 48)
                    act.wait_ge(s["shift"], 1)
                    act.wait_ge(s["proj"], 1)
                    act.activation(halves(lw[:, :]), acc[:, 0:2, :], ACT.Sigmoid, bias=par[:, 3:4]).then_inc(s["sw"], 1)
                    act.wait_ge(s["proj"], 2)
                    act.activation(halves(av[:, :]), acc[:, 2:4, :], ACT.Sigmoid, bias=par[:, 4:5]).then_inc(s["sa"], 1)
                    act.wait_ge(s["cum"], 1)
                    act.activation(eP[:, :], cum[:, :], ACT.Exp).then_inc(s["ep"], 1)
                    act.activation(eN[:, :], cum[:, :], ACT.Exp, scale=-1.0).then_inc(s["en"], 1)
                    act.wait_ge(s["diff"], 1)
                    act.activation(lw[:, :], lw[:, :], ACT.Exp).then_inc(s["el"], 1)
                    act.wait_ge(s["normed"], 1)
                    act.activation(halves(d[:, :]), acc[:, 6:8, :], ACT.Sqrt, scale=64.0).then_inc(s["root"], 1)

                @block.vector
                def _(dve):
                    link = chain(dve, s["own"])
                    at = lambda t: t[:, ds(i, 1), :]
                    one = lambda t: t[:, None, :]
                    link(dve.tensor_copy(par[:, :], g.par[:, ds(i * W_PAR + g.col["w"], W_PAR)]), s["shift"])
                    dve.wait_ge(s["loaded"], 48)
                    shifted(link, dve, x[0], d[:, :], par[:, 0:1], r[:, :])
                    shifted(link, dve, x[1], d[:, :], par[:, 1:2], k[:, :])
                    link(dve.tensor_tensor(d[:, :], x[2][:, 0:SEQ], x[2][:, 1:], ALU.subtract))
                    link(dve.scalar_tensor_tensor(at(rw.arrays["v"]), one(d), par[:, 2:3], x[2][:, None, 1:],
                                                  ALU.mult, ALU.add))
                    dve.wait_ge(s["sw"], 1)
                    link(dve.tensor_scalar(lw[:, :], lw[:, :], -float(np.exp(-0.5)), None, ALU.mult))
                    link(dve.tensor_tensor_scan(cum[:, :], reset[:, :], lw[:, :], 0.0, ALU.mult, ALU.add), s["cum"])
                    link(dve.tensor_tensor(lw[:, :], cum[:, :], lw[:, :], ALU.subtract), s["diff"])
                    kk, k2 = x[0][:, 1:], x[1][:, 1:]
                    link(dve.tensor_scalar(kk, k[:, :], par[:, 5:6], None, ALU.mult))
                    link(dve.tensor_tensor(d[:, :], kk, kk, ALU.mult), s["sqkk"])
                    dve.wait_ge(s["sa"], 1)
                    link(dve.tensor_scalar(k2, av[:, :], -1.0, par[:, 6:7], ALU.add, ALU.mult))
                    link(dve.scalar_tensor_tensor(k2, k2, 1.0, k[:, :], ALU.add, ALU.mult))
                    dve.wait_ge(s["root"], 1)
                    link(dve.tensor_scalar(d[:, :], d[:, :], 1e-12, None, ALU.max))
                    link(dve.reciprocal(d[:, :], d[:, :]))
                    link(dve.tensor_tensor(kk, kk, d[:, :], ALU.mult))
                    dve.wait_ge(s["el"], 1)
                    link(dve.tensor_tensor(at(rw.arrays["alpha"]), x[0][:, None, 1:], one(lw), ALU.mult))
                    link(dve.tensor_tensor(kk, kk, av[:, :], ALU.mult))
                    dve.wait_ge(s["ep"], 1)
                    dve.wait_ge(s["en"], 1)
                    link(dve.scalar_tensor_tensor(at(rw.arrays["beta"]), x[0][:, None, 1:], -1.0, one(eN),
                                                  ALU.mult, ALU.mult))
                    link(dve.tensor_tensor(at(rw.arrays["kappa"]), x[1][:, None, 1:], one(eN), ALU.mult))
                    link(dve.tensor_tensor(at(rw.arrays["rho"]), one(r), one(eP), ALU.mult))
                    link(dve.tensor_copy(rw.last[:, ds(i, 1), :], eP[:, None, CH - 1::CH]))
                    link(dve.scalar_tensor_tensor(d[:, :], r[:, :], par[:, 7:8], k2, ALU.mult, ALU.mult), s["prod"])
                    dve.wait_ge(s["proj"], 3)
                    link(dve.tensor_copy(halves(av[:, :]), acc[:, 4:6, :]), s["g_out"])
                    dve.wait_ge(s["normed"], 2)
                    link(dve.tensor_scalar(halves(lw[:, :]), acc[:, 6:8, :], 64.0, None, ALU.mult))
                    link(dve.tensor_tensor(one(lw), one(lw), at(rw.arrays["v"]), ALU.mult), s["extra"])
            clear(nc, s)


def spread(link, eng, out, src, at, sem):
    link(eng.tensor_copy(out[0:64, :, 0:64], src[0:64, :, ds(at, CH)]), sem)
    link(eng.tensor_copy(out[64:P, :, 64:P], src[64:P, :, ds(at, CH)]), sem)


def rwkv_chunks(nc, g, a, rw, out):
    N = 3
    with stage(nc, "wc", "const", "zero", "bd", "gram", "b_ready", "x1", "own", "mk", "y_done", "yp", "x_done",
               "x_new", "xt_new", "kt", "vt", "rhs", "rhs_s", "z", "z_s", "yo", "ys", "s_mm", "s_new", "turn",
               "tok", "plc", "stored") as s:
        bd = {n: s.sb(n + "bd", [P, N, P]) for n in ("alpha", "beta", "kappa", "rho")}
        vs, plc = s.sb("vs", [P, N, CH]), s.sb("plc", [P, N, 1])
        low, upp = s.sb("low", [P, 8, P]), s.sb("upp", [P, 8, P])
        mk, yp, X, XT = (s.sb(n, [P, N, P]) for n in ("mk", "yp", "X", "XT"))
        B, C, Dm, kT, bT = (s.sb(n, [P, N, P]) for n in ("B", "C", "D", "kT", "bT"))
        V, rhs, Z, ys, S = (s.sb(n, [P, N, CH]) for n in ("V", "rhs", "Z", "ys", "S"))
        yT = s.sb("yT", [P, N, SEQ])
        b_ = [s.ps(f"b{n}", [P, 4, P]) for n in range(8)]
        mm_ = lambda bank: bank[:, 0:N, :]
        bc = lambda m, k: m[:, k:k + 1, :].broadcast_to([P, N, P])
        idb = g.ident[:, None, :].broadcast_to([P, N, P])
        with nc.Block() as block:
            @block.sync
            def _(sp):
                sp.dma_start(low[:, :, :], a["low"].rearrange("p (k c) -> p k c", k=8)).then_inc(s["const"], 16)
                sp.dma_start(upp[:, :, :], a["upp"].rearrange("p (k c) -> p k c", k=8)).then_inc(s["const"], 16)
                sp.wait_ge(s["const"], 32)

            @block.vector
            def _(dve):
                for t in bd.values():
                    dve.memset(t[:, :, :], 0.0).then_inc(s["zero"], 1)
                dve.memset(S[:, :, :], 0.0).then_inc(s["zero"], 1)
        clear(nc, s)
        with nc.Fori(0, NCH) as i:
            with nc.Block() as block:
                @block.gpsimd
                def _(pool):
                    link = chain(pool, s["tok"])
                    for n in ("alpha", "beta", "kappa", "rho"):
                        spread(link, pool, bd[n], rw.arrays[n], i * CH, s["bd"])
                    pool.tensor_copy(vs[:, :, :], rw.arrays["v"][:, :, ds(i * CH, CH)]).then_inc(s["bd"], 1)
                    pool.wait_ge(s["bd"], 9)
                    pool.tensor_copy(plc[:, :, :], rw.last[:, :, ds(i, 1)]).then_inc(s["plc"], 1)

                @block.tensor
                def _(pe):
                    def each(bank, lhsT, rhs_, sem, start=True, stop=True, cols=P):
                        for p in range(N):
                            mm = pe.matmul(bank[:, p, 0:cols], lhsT[:, p, :], rhs_[:, p, :], start=start, stop=stop)
                        if sem is not None:
                            mm.then_inc(sem, 1)

                    pe.wait_ge(s["bd"], 9)
                    al, be, ka, rh = (bd[n] for n in ("alpha", "beta", "kappa", "rho"))
                    each(b_[0], al, be, s["gram"])
                    each(b_[1], be, al, s["gram"])
                    each(b_[2], ka, al, s["gram"])
                    each(b_[3], ka, rh, s["gram"])
                    each(b_[4], be, rh, s["gram"])
                    for bank, src in ((b_[5], ka), (b_[6], be)):
                        for p in range(N):
                            mm = pe.transpose(bank[:, p, :], src[:, p, :], g.ident[:, :])
                        mm.then_inc(s["kt"], 1)
                    for p in range(N):
                        mm = pe.transpose(b_[7][0:64, p, :], vs[:, p, :], g.ident[:, :])
                    mm.then_inc(s["kt"], 1)
                    pe.wait_ge(s["b_ready"], 7)
                    for k in range(1, 6):
                        pe.wait_ge(s["mk"], k)
                        pe.wait_ge(s["x1"], 1)
                        if k > 1:
                            pe.wait_ge(s["x_new"], k - 1)
                        each(b_[0], mk, X, s["y_done"])
                        pe.wait_ge(s["yp"], k)
                        if k < 5:
                            each(b_[2], XT, yp, None)
                        each(b_[3], yp, XT, s["x_done"])
                    for p in range(N):
                        pe.matmul(b_[4][:, p, 0:CH], al[:, p, :], S[:, p, :], start=True, stop=False)
                        mm = pe.matmul(b_[4][:, p, 0:CH], B[:, p, :], V[:, p, :], start=False, stop=True)
                    mm.then_inc(s["rhs"], 1)
                    pe.wait_ge(s["xt_new"], 5)
                    pe.wait_ge(s["rhs_s"], 1)
                    each(b_[5], XT, rhs, s["z"], cols=CH)
                    pe.wait_ge(s["z_s"], 1)
                    for p in range(N):
                        pe.matmul(b_[6][:, p, 0:CH], kT[:, p, :], V[:, p, :], start=True, stop=False)
                        mm = pe.matmul(b_[6][:, p, 0:CH], bT[:, p, :], Z[:, p, :], start=False, stop=True)
                    mm.then_inc(s["s_mm"], 1)
                    for p in range(N):
                        pe.matmul(b_[7][:, p, 0:CH], rh[:, p, :], S[:, p, :], start=True, stop=False)
                        pe.matmul(b_[7][:, p, 0:CH], C[:, p, :], V[:, p, :], start=False, stop=False)
                        mm = pe.matmul(b_[7][:, p, 0:CH], Dm[:, p, :], Z[:, p, :], start=False, stop=True)
                    mm.then_inc(s["yo"], 1)
                    pe.wait_ge(s["ys"], 1)
                    for p in range(N):
                        mm = pe.transpose(b_[5][0:64, p, :], ys[:, p, :], g.ident[:, :])
                    mm.then_inc(s["turn"], 1)

                @block.vector
                def _(dve):
                    link = chain(dve, s["own"])
                    dve.wait_ge(s["gram"], 2)
                    link(dve.tensor_tensor(X[:, :, :], mm_(b_[0]), bc(low, 0), ALU.mult))
                    link(dve.tensor_tensor(XT[:, :, :], mm_(b_[1]), bc(upp, 0), ALU.mult))
                    link(dve.tensor_tensor(X[:, :, :], X[:, :, :], idb, ALU.add))
                    link(dve.tensor_tensor(mk[:, :, :], mm_(b_[1]), bc(upp, 1), ALU.mult), s["mk"])
                    link(dve.tensor_tensor(XT[:, :, :], XT[:, :, :], idb, ALU.add), s["x1"])
                    dve.wait_ge(s["gram"], 5)
                    dve.tensor_tensor(B[:, :, :], mm_(b_[2]), bc(upp, 6), ALU.mult).then_inc(s["b_ready"], 1)
                    dve.tensor_tensor(C[:, :, :], mm_(b_[3]), bc(upp, 7), ALU.mult).then_inc(s["b_ready"], 1)
                    dve.tensor_tensor(Dm[:, :, :], mm_(b_[4]), bc(upp, 7), ALU.mult).then_inc(s["b_ready"], 1)
                    for k in range(1, 6):
                        dve.wait_ge(s["y_done"], k)
                        link(dve.tensor_tensor(yp[:, :, :], mm_(b_[0]), idb, ALU.add), s["yp"])
                        if k < 5:
                            link(dve.tensor_tensor(mk[:, :, :], mm_(b_[1]), bc(upp, k + 1), ALU.mult), s["mk"])
                        dve.wait_ge(s["x_done"], k)
                        link(dve.tensor_copy(XT[:, :, :], mm_(b_[3])), s["xt_new"])
                        if k < 5:
                            link(dve.tensor_copy(X[:, :, :], mm_(b_[2])), s["x_new"])
                    dve.wait_ge(s["rhs"], 1)
                    dve.tensor_copy(rhs[:, :, :], b_[4][:, 0:N, 0:CH]).then_inc(s["rhs_s"], 1)
                    dve.wait_ge(s["z"], 1)
                    dve.tensor_copy(Z[:, :, :], b_[5][:, 0:N, 0:CH]).then_inc(s["z_s"], 1)
                    dve.wait_ge(s["yo"], 1)
                    dve.wait_ge(s["s_mm"], 1)
                    dve.wait_ge(s["plc"], 1)
                    link(dve.tensor_copy(ys[:, :, :], b_[7][:, 0:N, 0:CH]), s["ys"])
                    link(dve.tensor_tensor(S[:, :, :], S[:, :, :], b_[6][:, 0:N, 0:CH], ALU.add))
                    link(dve.tensor_tensor(S[:, :, :], S[:, :, :], plc[:, :, :].broadcast_to([P, N, CH]),
                                           ALU.mult), s["s_new"])
                    dve.wait_ge(s["turn"], 1)
                    for hh in range(2):
                        dve.tensor_copy(yT[64 * hh:64 * hh + 64, :, ds(i * CH, CH)],
                                        b_[5][0:64, 0:N, 64 * hh:64 * hh + 64]).then_inc(s["tok"], 1)

                @block.scalar
                def _(act):
                    act.wait_ge(s["kt"], 3)
                    act.activation(kT[:, :, :], mm_(b_[5]), ACT.Copy).then_inc(s["b_ready"], 1)
                    act.activation(bT[:, :, :], mm_(b_[6]), ACT.Copy).then_inc(s["b_ready"], 1)
                    for hh in range(2):
                        act.activation(V[64 * hh:64 * hh + 64, :, :], b_[7][0:64, 0:N, 64 * hh:64 * hh + 64],
                                       ACT.Copy).then_inc(s["b_ready"], 1)
            clear(nc, s)
        with nc.Block() as block:
            @block.sync
            def _(sp):
                sp.dma_start(out.rearrange("(k p) t -> p k t", p=P), yT[:, :, :]).then_inc(s["stored"], 16)
                sp.wait_ge(s["stored"], 16)


def block2(nc, g, a, dram):
    proj, y = dram("proj2", (TILES_2 * P, SEQ)), dram("mixed2", (D, SEQ))
    rows, gate, extra = dram("rows2", (12, SEQ)), dram("gate2", (3 * P, SEQ)), dram("extra2", (3 * P, SEQ))
    with g.parts("a2"):
        norm(nc, "n2", g, g.h, [(0, KD)], g.col["g2"], SEQ)
        dense(nc, "in2", g, a["w_in_2"], TILES_2, SEQ, proj)
    conv_silu(nc, "mc", proj, 4, 4, 3, g, "mconv", 4)
    mlstm_gates(nc, g, proj, rows)
    attention(nc, "ml", g, proj, y, 4, M_Q * P, M_K * P, M_V * P, 0, rows=rows, tri=a["tri"])
    rotate(nc, g, proj, a["cos"], a["sin"], a["swap"])
    attention(nc, "rt", g, proj, y, 6, R_Q * P, R_K * P, R_V * P, 2 * P, ramps=a["ramps"])
    with ExitStack() as ctx:
        arrays = {n: ctx.enter_context(nc.sbuf_tensor(f"rw_{n}", [P, 3, SEQ], F32))
                  for n in ("alpha", "beta", "kappa", "rho", "v")}
        rw = Shared()
        rw.arrays = arrays
        rw.last = ctx.enter_context(nc.sbuf_tensor("rw_last", [P, 3, NCH], F32))
        rwkv_inputs(nc, g, a, proj, rw, gate, extra)
        rwkv_chunks(nc, g, a, rw, y[5 * P:8 * P, :])
    with nc.sbuf_tensor("y2", [P, KD, SEQ], F32) as y_sb:
        g.y = y_sb
        head_norm(nc, "hm", g, y, 2, 0, 1e-5, (proj, M_O), ACT.Sigmoid, gain="mln")
        head_norm(nc, "hr", g, y, 3, 2, 1e-5, (proj, R_G), ACT.Silu)
        head_norm(nc, "hw", g, y, 3, 5, 64e-5, (gate, 0), ACT.Copy, gain="wlng", bias="wlnb", extra=extra)
        with g.parts("b2"):
            split_u(nc, "su2", g)
            dense(nc, "out2", g, a["w_out_2"], KD, SEQ)
    with g.parts("c2"):
        norm(nc, "nm2", g, g.h, [(0, KD)], g.col["gm2"], SEQ)
        ffn(nc, "ff2", g, a["w_gu_2"], a["w_down_2"], [(2, 8), (1, 6)], SEQ, gated=True)
    norm(nc, "nf2", g, g.h, [(0, KD)], g.col["gf2"], SEQ, dest="h")


def split_u(nc, name, g):
    with stage(nc, name, "upper", "lower") as s:
        with nc.Block() as block:
            @block.scalar
            def _(act):
                for k in range(KD):
                    act.activation(g.uhi[:, k, 0:SEQ], g.y[:, k, 0:SEQ], ACT.Copy).then_inc(s["upper"], 1)

            @block.vector
            def _(dve):
                for k in range(KD):
                    dve.wait_ge(s["upper"], k + 1)
                    dve.tensor_tensor(g.ulo[:, k, 0:SEQ], g.y[:, k, 0:SEQ], g.uhi[:, k, 0:SEQ].bitcast(F32),
                                      ALU.subtract).then_inc(s["lower"], 1)


def unit_heads(nc, name, g, proj, row0, out, scale):
    with stage(nc, name, "loaded", "squared", "summed", "shifted", "rooted", "own") as s:
        x, sq = s.sb("x", [P, SEQ]), s.sb("sq", [P, SEQ])
        acc = s.ps("acc", [P, 2, 512])
        with nc.Fori(0, 4) as i:
            with nc.Block() as block:
                @block.sync
                def _(sp):
                    sp.dma_start(x[:, :], proj[ds(i * P + row0, P), :]).then_inc(s["loaded"], 16)

                @block.scalar
                def _(act):
                    act.wait_ge(s["loaded"], 16)
                    act.activation(sq[:, :], x[:, :], ACT.Square).then_inc(s["squared"], 1)
                    act.wait_ge(s["shifted"], 1)
                    act.activation(sq[:, :], sq[:, :], ACT.Sqrt).then_inc(s["rooted"], 1)

                @block.tensor
                def _(pe):
                    pe.wait_ge(s["squared"], 1)
                    for j in range(2):
                        mm = pe.matmul(acc[:, j, :], g.mean64[:, :], sq[:, j * 512:j * 512 + 512],
                                       start=True, stop=True)
                    mm.then_inc(s["summed"], 1)

                @block.vector
                def _(dve):
                    link = chain(dve, s["own"])
                    dve.wait_ge(s["summed"], 1)
                    link(dve.tensor_scalar(halves(sq[:, :]), acc[:, :, :], 64.0, EPS, ALU.mult, ALU.add), s["shifted"])
                    dve.wait_ge(s["rooted"], 1)
                    link(dve.reciprocal(sq[:, :], sq[:, :]))
                    link(dve.scalar_tensor_tensor(out[:, ds(i, 1), :], x[:, None, :], scale, sq[:, None, :],
                                                  ALU.mult, ALU.mult))
            clear(nc, s)


GK = 6


def gdn_gates(nc, g, proj, gd):
    with stage(nc, "gg", "loaded", "own", "abs", "power", "log", "alog", "sig", "decay", "turned", "tok", "sum", "end",
               "exps", "arg") as s:
        x, l = s.sb("x", [48, SEQ]), s.sb("l", [16, SEQ])
        ea = s.sb("ea", [16, 1])
        low, upp = s.sb("low", [P, P]), s.sb("upp", [P, P])
        tok = s.sb("tok", [P, NCH, 24])
        turned = s.ps("turned", [P, 2, 8, 64])
        acc = s.ps("acc", [P, 2, 512])
        c = g.col["gates3"]
        sums = lambda d: acc[:, d, 0:NCH * 4].rearrange("p (c h) -> p c h", h=4)
        ends = lambda d: acc[:, d, 64:64 + NCH * 4].rearrange("p (c h) -> p c h", h=4)
        with nc.Block() as block:
            @block.sync
            def _(sp):
                sp.dma_start(x[:, :], proj[G_GATE * P:G_GATE * P + 48, :]).then_inc(s["loaded"], 16)
                sp.dma_start(low[:, :], gd.a["low"][:, 7 * P:8 * P]).then_inc(s["loaded"], 16)
                sp.dma_start(upp[:, :], gd.a["upp"][:, 7 * P:8 * P]).then_inc(s["loaded"], 16)

            @block.scalar
            def _(act):
                act.wait_ge(s["loaded"], 48)
                dt = g.par[0:16, c:c + 1]
                act.activation(l[:, :], x[0:16, :], ACT.Abs, bias=dt).then_inc(s["abs"], 1)
                act.activation(ea[:, :], g.par[0:16, c + 1:c + 2], ACT.Exp).then_inc(s["alog"], 1)
                act.wait_ge(s["abs"], 1)
                act.activation(l[:, :], l[:, :], ACT.Exp, scale=-1.0).then_inc(s["power"], 1)
                act.wait_ge(s["power"], 1)
                act.activation(l[:, :], l[:, :], ACT.Ln, bias=1.0).then_inc(s["log"], 1)
                act.activation(x[32:48, :], x[32:48, :], ACT.Sigmoid).then_inc(s["sig"], 1)
                for d in range(2):
                    act.wait_ge(s["arg"], d + 1)
                    for n in (1, 2, 3):
                        act.activation(gd.sc[:, d, :, n, :], gd.sc[:, d, :, n, :], ACT.Exp).then_inc(s["exps"], 1)

            @block.vector
            def _(dve):
                link = chain(dve, s["own"])
                dve.wait_ge(s["loaded"], 48)
                dve.wait_ge(s["abs"], 1)
                link(dve.tensor_scalar(x[0:16, :], x[0:16, :], g.par[0:16, c:c + 1], 0.0, ALU.add, ALU.max))
                dve.wait_ge(s["log"], 1)
                link(dve.tensor_tensor(x[0:16, :], x[0:16, :], l[:, :], ALU.add))
                dve.wait_ge(s["alog"], 1)
                link(dve.tensor_scalar(x[0:16, :], x[0:16, :], ea[:, 0:1], -1.0, ALU.mult, ALU.mult), s["decay"])
                dve.wait_ge(s["turned"], 1)
                for hh in range(2):
                    for b in range(2):
                        link(dve.tensor_copy(tok[64 * hh:64 * hh + 64, 8 * b:8 * b + 8, :],
                                             turned[0:64, b, :, hh:48:2]), s["tok"])
                dve.wait_ge(s["sum"], 1)
                for d in range(2):
                    sc = gd.sc[:, d, :, :, :]
                    link(dve.tensor_copy(sc[:, :, 0, :], sums(d)))
                    link(dve.tensor_copy(sc[:, :, 1, :], sums(d)))
                    link(dve.scalar_tensor_tensor(sc[:, :, 2, :], ends(d), 64.0, sc[:, :, 0, :],
                                                  ALU.mult, ALU.subtract))
                    link(dve.tensor_scalar(sc[:, :, 3, :], ends(d), 64.0, None, ALU.mult), s["arg"])
                    beta = tok[:, :, 16 + 4 * d:20 + 4 * d]
                    link(dve.tensor_scalar(sc[:, :, 4, :], beta, -1.0, None, ALU.mult))
                    link(dve.tensor_copy(sc[:, :, 5, :], beta))

            @block.tensor
            def _(pe):
                pe.wait_ge(s["decay"], 1)
                pe.wait_ge(s["sig"], 1)
                for n in range(NCH):
                    mm = pe.transpose(turned[0:64, n // 8, n % 8, 0:48], x[:, n * CH:n * CH + CH],
                                      g.ident[0:48, 0:48])
                mm.then_inc(s["turned"], 1)
                pe.wait_ge(s["tok"], 4)
                for d, mask in enumerate((upp, low)):
                    for c4 in range(NCH):
                        r = tok[:, c4, 4 * d:4 * d + 4]
                        pe.matmul(acc[:, d, 4 * c4:4 * c4 + 4], mask[:, :], r, start=True, stop=True)
                        mm = pe.matmul(acc[:, d, 64 + 4 * c4:68 + 4 * c4], g.mean64[:, :], r, start=True, stop=True)
                mm.then_inc(s["sum"], 1)


GDN_SEMS = ("bd", "vs", "sc", "diag", "dots", "turn", "rows", "diff", "ramp", "V", "kT", "bV", "CT", "AT", "x1",
            "mk", "Y", "yp", "XX", "X", "XT", "KS", "rhs", "Vn", "vn", "vd", "CV", "up", "S", "o", "oturn", "own",
            "xtc", "actv")


def gdn_chunks(nc, g, gd, out):
    N = 4
    with stage(nc, "gc", *[f"{n}{d}" for d in range(2) for n in GDN_SEMS], "const", "zero", "tok") as s:
        sem = [{n: s[f"{n}{d}"] for n in GDN_SEMS} for d in range(2)]
        low, upp = s.sb("low", [P, 7, CH]), s.sb("upp", [P, 7, CH])
        idc, ones64 = s.sb("idc", [P, CH]), s.sb("ones64", [P, P])

        dirs = []
        for d in range(2):
            t = Shared()
            wide = lambda n: s.sb(n + str(d), [P, N, P])
            compact = lambda n: s.sb(n + str(d), [P, N, CH])
            t.kbd, t.qbd, t.kT, t.CT, t.mk, t.ypd, t.XTd = (
                wide(n) for n in ("kbd", "qbd", "kT", "CT", "mk", "ypd", "XTd"))
            t.vs, t.dg, t.db, t.df, t.dfn, t.E, t.A, t.ATc, t.X, t.XTc, t.yp, t.V = (
                compact(n) for n in ("vs", "dg", "db", "df", "dfn", "E", "A", "ATc", "X", "XTc", "yp", "V"))
            t.rhs, t.vn, t.vd, t.o, t.S = (compact(n) for n in ("rhs", "vn", "vd", "o", "S"))
            t.sc = s.sb(f"sc{d}", [P, GK, N])
            t.b = [s.ps(f"b{n}_{d}", [P, 512]) for n in range(4)]
            t.half = lambda n, h, t=t: t.b[n][:, 256 * h:256 * h + 256].rearrange("p (n c) -> p n c", n=N)
            t.full = lambda n, t=t: t.b[n][:, :].rearrange("p (n c) -> p n c", n=N)
            t.s = sem[d]
            t.mA, t.mT = (low, upp) if d == 0 else (upp, low)
            dirs.append(t)
        m_ = lambda mask, k: mask[:, k:k + 1, :].broadcast_to([P, N, CH])
        idn = idc[:, None, :].broadcast_to([P, N, CH])
        sc_ = lambda t, n: t.sc[:, n, :].unsqueeze(2).broadcast_to([P, N, CH])
        q, k, v = gd.q, gd.k, gd.v
        both = lambda: enumerate(dirs)
        with nc.Block() as block:
            @block.sync
            def _(sp):
                for hh in range(2):
                    at = slice(64 * hh, 64 * hh + 64)
                    for t, n in ((low, "low"), (upp, "upp")):
                        src = gd.a[n].rearrange("p (k c) -> p k c", k=8)
                        sp.dma_start(t[at, 0:6, :], src[at, 0:6, at]).then_inc(s["const"], 16)
                        sp.dma_start(t[at, 6:7, :], src[at, 7:8, at]).then_inc(s["const"], 16)
                    sp.dma_start(idc[at, :], gd.a["ident"][at, at]).then_inc(s["const"], 16)
                sp.wait_ge(s["const"], 160)

            @block.vector
            def _(dve):
                dve.tensor_scalar(ones64[:, :], g.mean64[:, :], 64.0, None, ALU.mult).then_inc(s["zero"], 1)
                for t in dirs:
                    for x in (t.kbd, t.qbd, t.CT, t.mk, t.ypd, t.XTd, t.S):
                        dve.memset(x[:, :, :], 0.0).then_inc(s["zero"], 1)
        clear(nc, s)
        with nc.Fori(0, NCH) as i:
            at = lambda d: i * CH if d == 0 else i * (-CH) + (NCH - 1) * CH
            ci = lambda d: i if d == 0 else i * (-1) + (NCH - 1)
            with nc.Block() as block:
                @block.gpsimd
                def _(pool):
                    link = chain(pool, s["own1"])
                    for d, t in both():
                        link(pool.tensor_copy(t.sc[:, :, :], gd.sc[:, d, ds(ci(d), 1), :, :]
                                              .rearrange("p a k n -> p (a k) n")), t.s["sc"])
                        spread(link, pool, t.kbd, k, at(d), t.s["bd"])
                        link(pool.tensor_copy(t.vs[:, :, :], v[:, :, ds(at(d), CH)]), t.s["vs"])
                        spread(link, pool, t.qbd, q, at(d), t.s["bd"])
                    for lev in range(1, 6):
                        for d, t in both():
                            pool.wait_ge(t.s["AT"], 1)
                            if lev > 1:
                                pool.wait_ge(t.s["Y"], lev - 1)
                            for hh in range(2):
                                r = slice(64 * hh, 64 * hh + 64)
                                link(pool.tensor_tensor(t.mk[r, :, r], t.ATc[r, :, :],
                                                        t.mT[r, lev:lev + 1, :].broadcast_to([64, N, CH]),
                                                        ALU.mult), t.s["mk"])

                @block.tensor
                def _(pe):
                    def each(out, lhsT, rhs, start=True, stop=True):
                        for p in range(N):
                            mm = pe.matmul(out[:, p, :], lhsT[:, p, :], rhs[:, p, :], start=start, stop=stop)
                        return mm

                    for d, t in both():
                        pe.wait_ge(t.s["diag"], 2)
                        pe.matmul(t.half(1, 0), ones64[:, :], t.dg[:, :, :], start=True, stop=True)
                        pe.matmul(t.half(1, 1), ones64[:, :], t.db[:, :, :], start=True, stop=True)\
                          .then_inc(t.s["rows"], 1)
                        pe.wait_ge(t.s["bd"], 2)
                        each(t.half(0, 0), t.kbd, k[:, :, ds(at(d), CH)])
                        each(t.half(0, 1), t.kbd, q[:, :, ds(at(d), CH)]).then_inc(t.s["dots"], 1)
                        pe.wait_ge(t.s["vs"], 1)
                        for p in range(N):
                            mm = pe.transpose(t.full(2)[0:64, p, :], t.vs[:, p, :], g.ident[:, :])
                        mm.then_inc(t.s["turn"], 1)
                        for p in range(N):
                            mm = pe.transpose(t.full(3)[:, p, :], t.kbd[:, p, :], g.ident[:, :])
                        mm.then_inc(t.s["turn"], 1)
                    for d, t in both():
                        pe.wait_ge(t.s["V"], 2)
                        pe.wait_ge(t.s["bd"], 4)
                        each(t.half(2, 0), t.kbd, t.S)
                        each(t.half(2, 1), t.qbd, t.S).then_inc(t.s["KS"], 1)
                    for lev in range(1, 6):
                        for d, t in both():
                            pe.wait_ge(t.s["mk"], 2 * lev)
                            if lev == 1:
                                pe.wait_ge(t.s["x1"], 1)
                                pe.wait_ge(t.s["CT"], 1)
                            else:
                                pe.wait_ge(t.s["X"], lev - 1)
                            each(t.half(0, 0), t.mk, t.X).then_inc(t.s["Y"], 1)
                        for d, t in both():
                            pe.wait_ge(t.s["yp"], lev)
                            if lev > 1:
                                pe.wait_ge(t.s["XT"], 3 * (lev - 1))
                            if lev < 5:
                                each(t.half(1, 0), t.XTd, t.yp)
                            each(t.half(1, 1), t.ypd, t.XTc).then_inc(t.s["XX"], 1)
                    for d, t in both():
                        pe.wait_ge(t.s["XT"], 3 * 5)
                        pe.wait_ge(t.s["rhs"], 1)
                        pe.wait_ge(t.s["kT"], 1)
                        each(t.half(3, 0), t.XTd, t.rhs).then_inc(t.s["Vn"], 1)
                    for d, t in both():
                        pe.wait_ge(t.s["vd"], 1)
                        each(t.half(0, 1), t.kT, t.vd).then_inc(t.s["up"], 1)
                        pe.wait_ge(t.s["vn"], 1)
                        each(t.half(3, 1), t.CT, t.vn).then_inc(t.s["CV"], 1)
                    for d, t in both():
                        pe.wait_ge(t.s["o"], 1)
                        for p in range(N):
                            mm = pe.transpose(t.full(2)[0:64, p, :], t.o[:, p, :], g.ident[:, :])
                        mm.then_inc(t.s["oturn"], 1)

                @block.vector
                def _(dve):
                    link = chain(dve, s["own0"])
                    tt = dve.tensor_tensor
                    full = slice(None)
                    for d, t in both():
                        dve.wait_ge(t.s["sc"], 1)
                        tt(t.dg[:, :, :], idn, sc_(t, 0), ALU.mult).then_inc(t.s["diag"], 1)
                        tt(t.db[:, :, :], idn, sc_(t, 4), ALU.mult).then_inc(t.s["diag"], 1)
                    for d, t in both():
                        dve.wait_ge(t.s["rows"], 1)
                        link(tt(t.df[:, :, :], t.half(1, 0), sc_(t, 0), ALU.subtract))
                        link(dve.tensor_scalar(t.dfn[:, :, :], t.df[:, :, :], 0.0, None, ALU.max), t.s["diff"])
                        link(dve.tensor_scalar(t.df[:, :, :], t.df[:, :, :], 0.0, None, ALU.min), t.s["diff"])
                    for d, t in both():
                        dve.wait_ge(t.s["dots"], 1)
                        dve.wait_ge(t.s["ramp"], 2)
                        link(tt(t.ATc[:, :, :], t.half(0, 0), t.df[:, :, :], ALU.mult))
                        link(tt(t.ATc[:, :, :], t.half(1, 1), t.ATc[:, :, :], ALU.mult), t.s["AT"])
                        link(tt(t.df[:, :, :], t.df[:, :, :], m_(t.mT, 6), ALU.mult))
                        for hh in range(2):
                            r = slice(64 * hh, 64 * hh + 64)
                            link(tt(t.CT[r, :, r], t.half(0, 1)[r, :, :], t.df[r, :, :], ALU.mult))
                        link(tt(t.E[:, :, :], t.dfn[:, :, :], m_(t.mA, 0), ALU.mult))
                        link(tt(t.A[:, :, :], t.half(0, 0), t.E[:, :, :], ALU.mult), t.s["CT"])
                        link(tt(t.A[:, :, :], t.A[:, :, :], sc_(t, 4), ALU.mult))
                        link(tt(t.X[:, :, :], t.A[:, :, :], idn, ALU.add))
                        link(tt(t.XTc[:, :, :], t.ATc[:, :, :], m_(t.mT, 0), ALU.mult))
                        link(tt(t.XTc[:, :, :], t.XTc[:, :, :], idn, ALU.add))
                        for hh in range(2):
                            r = slice(64 * hh, 64 * hh + 64)
                            link(dve.tensor_copy(t.XTd[r, :, r], t.XTc[r, :, :]), t.s["x1"] if hh else None)
                    for lev in range(1, 6):
                        for d, t in both():
                            dve.wait_ge(t.s["Y"], lev)
                            if lev > 1:
                                dve.wait_ge(t.s["XX"], lev - 1)
                            link(tt(t.yp[:, :, :], t.half(0, 0), idn, ALU.add))
                            for hh in range(2):
                                r = slice(64 * hh, 64 * hh + 64)
                                link(dve.tensor_copy(t.ypd[r, :, r], t.yp[r, :, :]), t.s["yp"] if hh else None)
                        if lev == 1:
                            for d, t in both():
                                dve.wait_ge(t.s["V"], 2)
                                dve.wait_ge(t.s["KS"], 1)
                                link(tt(t.rhs[:, :, :], t.half(2, 0), sc_(t, 1), ALU.mult))
                                link(tt(t.rhs[:, :, :], t.rhs[:, :, :], t.V[:, :, :], ALU.subtract))
                                link(tt(t.rhs[:, :, :], t.rhs[:, :, :], sc_(t, 4), ALU.mult), t.s["rhs"])
                                link(tt(t.o[:, :, :], t.half(2, 1), sc_(t, 1), ALU.mult))
                                link(tt(t.S[:, :, :], t.S[:, :, :], sc_(t, 3), ALU.mult))
                    for d, t in both():
                        dve.wait_ge(t.s["Vn"], 1)
                        link(tt(t.vd[:, :, :], t.half(3, 0), sc_(t, 2), ALU.mult), t.s["vd"])
                        link(dve.tensor_copy(t.vn[:, :, :], t.half(3, 0)), t.s["vn"])
                    for d, t in both():
                        dve.wait_ge(t.s["up"], 1)
                        link(tt(t.S[:, :, :], t.S[:, :, :], t.half(0, 1), ALU.add))
                        dve.wait_ge(t.s["CV"], 1)
                        link(tt(t.o[:, :, :], t.o[:, :, :], t.half(3, 1), ALU.add), t.s["o"])

                @block.scalar
                def _(act):
                    for d, t in both():
                        act.wait_ge(t.s["diff"], 2)
                        act.activation(t.dfn[:, :, :], t.dfn[:, :, :], ACT.Exp, scale=-1.0).then_inc(t.s["ramp"], 1)
                        act.activation(t.df[:, :, :], t.df[:, :, :], ACT.Exp).then_inc(t.s["ramp"], 1)
                    for d, t in both():
                        act.wait_ge(t.s["turn"], 2)
                        for hh in range(2):
                            r = slice(64 * hh, 64 * hh + 64)
                            act.activation(t.V[r, :, :], t.full(2)[0:64, :, r], ACT.Copy).then_inc(t.s["V"], 1)
                        act.activation(t.kT[:, :, :], t.full(3), ACT.Copy).then_inc(t.s["kT"], 1)
                    for lev in range(1, 6):
                        for d, t in both():
                            act.wait_ge(t.s["XX"], lev)
                            if lev < 5:
                                act.activation(t.X[:, :, :], t.half(1, 0), ACT.Copy).then_inc(t.s["X"], 1)
                            for hh in range(2):
                                r = slice(64 * hh, 64 * hh + 64)
                                act.activation(t.XTd[r, :, r], t.half(1, 1)[r, :, :], ACT.Copy)\
                                   .then_inc(t.s["XT"], 1)
                            act.activation(t.XTc[:, :, :], t.half(1, 1), ACT.Copy).then_inc(t.s["XT"], 1)
                    for d, t in both():
                        act.wait_ge(t.s["oturn"], 1)
                        for hh in range(2):
                            r = slice(64 * hh, 64 * hh + 64)
                            act.activation(out[d][r, :, ds(at(d), CH)], t.full(2)[0:64, :, r], ACT.Copy)\
                               .then_inc(s["tok"], 1)
            clear(nc, s)


def spatial(nc, g, a, proj):
    with stage(nc, "sg", "loaded", "gelu", "own", "par", "squared", "summed", "shifted", "rooted", "normed",
               "turned", "tok", "mixed", "sq2", "y") as s:
        u, v, sq = s.sb("u", [P, SEQ]), s.sb("v", [P, SEQ]), s.sb("sq", [P, SEQ])
        wT, bias = s.sb("wT", [P, P]), s.sb("bias", [P, P])
        vt = s.sb("vt", [P, 8, P])
        par = s.sb("par", [P, 2])
        acc = s.ps("acc", [P, 2, 512])
        turned, mixed = s.ps("turned", [P, 8, P]), s.ps("mixed", [P, 8, P])
        with nc.Fori(0, 4) as i:
            with nc.Block() as block:
                @block.sync
                def _(sp):
                    sp.dma_start(u[:, :], proj[ds(i * P + G_SU * P, P), :]).then_inc(s["loaded"], 16)
                    sp.dma_start(v[:, :], proj[ds(i * P + G_SV * P, P), :]).then_inc(s["loaded"], 16)
                    sp.dma_start(wT[:, :], a["sgu_wt"][ds(i * P, P), :]).then_inc(s["loaded"], 16)
                    sp.dma_start(bias[:, :], a["sgu_b"][ds(i, 1), :].broadcast_to([P, P])).then_inc(s["loaded"], 16)

                @block.scalar
                def _(act):
                    act.wait_ge(s["loaded"], 64)
                    act.activation(v[:, :], v[:, :], ACT.Gelu).then_inc(s["gelu"], 1)
                    act.activation(u[:, :], u[:, :], ACT.Gelu).then_inc(s["gelu"], 1)
                    for n in range(2):
                        act.wait_ge(s["shifted"], n + 1)
                        act.activation(sq[:, :], sq[:, :], ACT.Sqrt).then_inc(s["rooted"], 1)

                @block.tensor
                def _(pe):
                    def total(sem):
                        pe.wait_ge(sem, 1)
                        for j in range(2):
                            mm = pe.matmul(acc[:, j, :], g.ones[:, :], sq[:, j * 512:j * 512 + 512],
                                           start=True, stop=True)
                        mm.then_inc(s["summed"], 1)

                    total(s["squared"])
                    pe.wait_ge(s["normed"], 1)
                    for c in range(8):
                        mm = pe.transpose(turned[:, c, :], v[:, c * P:(c + 1) * P], g.ident[:, :])
                    mm.then_inc(s["turned"], 1)
                    pe.wait_ge(s["tok"], 2)
                    for c in range(8):
                        mm = pe.matmul(mixed[:, c, :], vt[:, c, :], wT[:, :], start=True, stop=True)
                    mm.then_inc(s["mixed"], 1)
                    total(s["sq2"])

                @block.vector
                def _(dve):
                    link = chain(dve, s["own"])
                    link(dve.tensor_copy(par[:, 0:1], g.par[:, ds(i + g.col["sgv"], 1)]))
                    link(dve.tensor_copy(par[:, 1:2], g.par[:, ds(i + g.col["sgo"], 1)]))

                    def inverse(n):
                        dve.wait_ge(s["summed"], n)
                        link(dve.tensor_scalar(halves(sq[:, :]), acc[:, :, :], 1.0 / P, EPS, ALU.mult, ALU.add),
                             s["shifted"])
                        dve.wait_ge(s["rooted"], n)
                        link(dve.reciprocal(sq[:, :], sq[:, :]))

                    dve.wait_ge(s["gelu"], 1)
                    link(dve.tensor_tensor(sq[:, :], v[:, :], v[:, :], ALU.mult), s["squared"])
                    inverse(1)
                    link(dve.scalar_tensor_tensor(v[:, :], v[:, :], par[:, 0:1], sq[:, :], ALU.mult, ALU.mult),
                         s["normed"])
                    dve.wait_ge(s["turned"], 1)
                    for n in range(2):
                        link(dve.tensor_copy(vt[:, 4 * n:4 * n + 4, :], turned[:, 4 * n:4 * n + 4, :]), s["tok"])
                    dve.wait_ge(s["mixed"], 1)
                    dve.wait_ge(s["loaded"], 64)
                    v8 = v[:, :].rearrange("p (c t) -> p c t", c=8)
                    for n in range(2):
                        link(dve.tensor_tensor(v8[:, 4 * n:4 * n + 4, :], mixed[:, 4 * n:4 * n + 4, :],
                                               bias[:, None, :].broadcast_to([P, 4, P]), ALU.add))
                    dve.wait_ge(s["gelu"], 2)
                    link(dve.tensor_tensor(v[:, :], v[:, :], u[:, :], ALU.mult))
                    link(dve.tensor_tensor(sq[:, :], v[:, :], v[:, :], ALU.mult), s["sq2"])
                    inverse(2)
                    link(dve.scalar_tensor_tensor(g.y[:, ds(i + 4, 1), :], v[:, None, :], par[:, 1:2],
                                                  sq[:, None, :], ALU.mult, ALU.mult))
            clear(nc, s)


def block3(nc, g, a, dram, out):
    proj = dram("proj3", (TILES_3 * P, SEQ))
    o_dram = [dram(f"o3_{d}", (4 * P, SEQ)) for d in range(2)]
    with g.parts("a3"):
        norm(nc, "n3", g, g.h, [(0, KD)], g.col["g3"], SEQ)
        dense(nc, "in3", g, a["w_in_3"], TILES_3, SEQ, proj)
    conv_silu(nc, "gcv", proj, 12, 5, 2, g, "gconv", 5)
    with ExitStack() as ctx:
        sb = lambda n, shape: ctx.enter_context(nc.sbuf_tensor(n, shape, F32))
        gd = Shared()
        gd.a = a
        gd.q, gd.k, gd.v = (sb(f"gd_{n}", [P, 4, SEQ]) for n in "qkv")
        gd.sc = sb("gd_sc", [P, 2, NCH, GK, 4])
        o = [sb(f"gd_o{d}", [P, 4, SEQ]) for d in range(2)]
        unit_heads(nc, "uq", g, proj, G_Q * P, gd.q, 0.125)
        unit_heads(nc, "uk", g, proj, G_K * P, gd.k, 1.0)
        gdn_gates(nc, g, proj, gd)
        with stage(nc, "gv", "loaded") as s:
            with nc.Block() as block:
                @block.sync
                def _(sp):
                    sp.dma_start(gd.v[:, :, :], proj[G_V * P:G_Z * P, :].rearrange("(k p) t -> p k t", p=P))\
                      .then_inc(s["loaded"], 16)
                    sp.wait_ge(s["loaded"], 16)
        gdn_chunks(nc, g, gd, o)
        with stage(nc, "go", "stored") as s:
            with nc.Block() as block:
                @block.sync
                def _(sp):
                    for d in range(2):
                        sp.dma_start(o_dram[d].rearrange("(k p) t -> p k t", p=P), o[d][:, :, :])\
                          .then_inc(s["stored"], 16)
                    sp.wait_ge(s["stored"], 32)
    with nc.sbuf_tensor("y3", [P, KD, SEQ], F32) as y_sb:
        g.y = y_sb
        head_norm(nc, "hg", g, o_dram[0], 4, 0, EPS, (proj, G_Z), ACT.Silu, center=False, gain="gdng",
                  src2=o_dram[1])
        spatial(nc, g, a, proj)
        with g.parts("b3"):
            split_u(nc, "su3", g)
            dense(nc, "out3", g, a["w_out_3"], KD, SEQ)
    with g.parts("c3"):
        norm(nc, "nm3", g, g.h, [(0, KD)], g.col["gm3"], SEQ)
        ffn(nc, "ff3", g, a["w_ff1_3"], a["w_ff2_3"], [(4, KD)], SEQ, gated=False)
    norm(nc, "nf3", g, g.h, [(0, KD)], g.col["gf3"], SEQ, dest=out)


def cols(v):
    v = v.reshape(-1, v.shape[-1])
    K, C = v.shape
    return np.ascontiguousarray(v.reshape(K, C // P, P).transpose(2, 1, 0)).reshape(P, -1)


def block_diagonal(w):
    out = np.zeros((w.shape[0] // 2, P, P), w.dtype)
    out[:, 0:64, 0:64] = w[0::2]
    out[:, 64:, 64:] = w[1::2]
    return out.reshape(-1, P)


def layout(x):
    par, col = [], {}

    def put(name, block):
        col[name] = sum(b.shape[1] for b in par)
        par.append(block)

    z1 = lambda n: np.zeros((P, n), np.float32)
    put("g1", cols(x["norm_mix_g"][0]))
    put("lru", np.concatenate([np.concatenate(
        [cols(x["lru_conv_w"][0][:, t * P:(t + 1) * P])] +
        [cols(x[k][0][t * P:(t + 1) * P]) for k in ("lru_conv_b", "lru_gate_a_b", "lru_gate_x_b", "lru_a_param")] +
        [z1(LRU_PAR - 8)], 1) for t in range(4)], 1))
    put("cc", np.concatenate([np.concatenate(
        [cols(x["cc_conv_w"][0][:, t * P:(t + 1) * P]), cols(x["cc_conv_b"][0][t * P:(t + 1) * P])], 1)
        for t in range(4)], 1))
    put("ccg", cols(x["cc_ln_g"][0]))
    put("ccb", cols(x["cc_ln_b"][0]))
    put("go1", np.concatenate([cols(x["out_norm_lru_g"][0]), cols(x["out_norm_cc_g"][0])], 1))
    put("gm1", cols(x["norm_mlp_g"][0]))
    put("gf1", cols(x["norm_final_g"]))
    a = {
        "h0": np.ascontiguousarray(np.concatenate([x["meta_tokens"], x["x"][0]], 0).T),
        "w_in": x["w_in"][0], "w_out": x["w_out"][0], "w_mlp_up": x["w_mlp_up"][0], "w_mlp_down": x["w_mlp_down"][0],
        "lru_wa": block_diagonal(x["lru_gate_a_w"][0]), "lru_wx": block_diagonal(x["lru_gate_x_w"][0]),
    }
    layout2(x, a, put)
    layout3(x, a, put)
    a["par"] = np.ascontiguousarray(np.concatenate(par, 1))
    return a, col


def tiles_of(w, *spans):
    out = []
    for lo, hi in spans:
        out.append(w[:, lo:hi])
        if (hi - lo) % P:
            out.append(np.zeros((w.shape[0], -(hi - lo) % P), w.dtype))
    return np.concatenate(out, 1)


def level_masks():
    t, s_ = np.meshgrid(np.arange(P), np.arange(P), indexing="ij")
    same = t // CH == s_ // CH
    m = [same & (t >> (k + 1) == s_ >> (k + 1)) & ((t >> k) & 1 == 1) & ((s_ >> k) & 1 == 0) for k in range(6)]
    m += [same & (s_ < t), same & (s_ <= t)]
    low = np.stack(m, 1).astype(np.float32)
    return low.reshape(P, -1), np.ascontiguousarray(low.transpose(2, 1, 0)).reshape(P, -1)


def layout2(x, a, put):
    w = x["w_in_2"][0]
    m, r = 1032, 1032 + 1536
    a["w_in_2"] = tiles_of(w, (0, 1024), (m, m + 1536), (r, r + 1408), (1024, 1032))
    a["w_gu_2"] = np.stack([x["w_gate_2"][0].reshape(D, -1, P), x["w_up_2"][0].reshape(D, -1, P)], 2).reshape(D, -1)
    a["w_out_2"], a["w_down_2"] = x["w_out_2"][0], x["w_down_2"][0]
    put("g2", cols(x["ln1_g_2"][0]))
    put("gm2", cols(x["ln2_g_2"][0]))
    put("gf2", cols(x["lnf_g_2"]))
    put("mconv", cols(x["m_conv_2"][0]))
    mb = np.zeros((P, 2), np.float32)
    mb[0:4, 0], mb[0:4, 1] = x["m_b_i_2"][0], x["m_b_f_2"][0]
    put("mb", mb)
    put("mln", cols(x["m_ln_g_2"][0]))
    put("wlng", cols(x["rw_ln_g_2"][0]))
    put("wlnb", cols(x["rw_ln_b_2"][0]))
    mu = x["rw_mu_2"][0]
    put("wmu", cols(mu[1152:1408]))
    by_tile = [cols(v) for v in (mu[0:384], mu[384:768], mu[768:1152], x["rw_w0_2"][0], x["rw_a0_2"][0],
                                 x["rw_k_k_2"][0], x["rw_k_a_2"][0], x["rw_r_k_2"][0])]
    put("w", np.stack(by_tile, 2).reshape(P, -1))
    tile = lambda v: v.reshape(P, 3, P).transpose(1, 0, 2).reshape(3 * P, P)
    z = np.zeros((64, 384), np.float32)
    a["w_up"] = tile(np.concatenate([x["rw_w_up_2"][0], z]))
    a["a_up"] = tile(np.concatenate([z, x["rw_a_up_2"][0]]))
    a["g_up"] = tile(x["rw_g_up_2"][0])
    d = np.arange(P)
    theta = (1.0 / 10000.0 ** np.linspace(0.0, 1.0, 32, dtype=np.float32)).astype(np.float32)
    ang = np.arange(SEQ, dtype=np.float32)[None, :] * theta[d % 32][:, None]
    a["cos"] = np.cos(ang)
    a["sin"] = np.sin(ang) * np.where(d % 64 < 32, -1.0, 1.0).astype(np.float32)[:, None]
    a["swap"] = (d[:, None] == (d ^ 32)[None, :]).astype(np.float32)
    xx = np.arange(SEQ)[None, :] - d[:, None]
    log_g = np.log(1.0 - 2.0 ** (-5.0 - np.arange(6)))
    a["ramps"] = np.concatenate([np.where(xx >= 0, np.exp(np.maximum(xx, 0) * lg), 0.0) * 0.125
                                 for lg in log_g]).astype(np.float32)
    a["tri"] = np.where(xx[:, 0:512] >= 0, 0.0, -1e30).astype(np.float32)
    a["reset"] = np.broadcast_to((np.arange(SEQ) % CH != 0).astype(np.float32), (P, SEQ))
    a["low"], a["upp"] = level_masks()
    a["ident"] = np.eye(P, dtype=np.float32)
    a["mean64"] = np.kron(np.eye(2), np.full((64, 64), 1.0 / 64)).astype(np.float32)


def layout3(x, a, put):
    w = x["w_in_3"][0]
    gates = np.zeros((D, P), w.dtype)
    gates[:, 0:16], gates[:, 32:48] = w[:, 2064:2080], w[:, 2048:2064]
    a["w_in_3"] = np.concatenate([w[:, 0:2048], w[:, 2080:3104], gates, np.zeros((D, P), w.dtype)], 1)
    a["w_out_3"], a["w_ff1_3"], a["w_ff2_3"] = x["w_out_3"][0], x["w_ff1_3"][0], x["w_ff2_3"][0]
    put("g3", cols(x["norm_mix_3"][0]))
    put("gm3", cols(x["norm_ffn_3"][0]))
    put("gf3", cols(x["norm_final_3"]))
    put("gconv", cols(x["conv_w_3"][0]))
    gates3 = np.zeros((P, 2), np.float32)
    gates3[0:8, 0], gates3[8:16, 0] = x["dt_bias_fwd_3"][0], x["dt_bias_bwd_3"][0]
    gates3[0:8, 1], gates3[8:16, 1] = x["a_log_fwd_3"][0], x["a_log_bwd_3"][0]
    put("gates3", gates3)
    put("gdng", np.tile(x["gdn_norm_3"][0][:, None], (2, 4)))
    put("sgv", cols(x["sgu_v_norm_3"][0].reshape(-1)))
    put("sgo", cols(x["sgu_out_norm_3"][0].reshape(-1)))
    a["sgu_wt"] = x["sgu_w_3"][0].transpose(0, 2, 1).reshape(4 * P, P)
    a["sgu_b"] = x["sgu_b_3"][0]


def program(nc, a, out, col, blocks=(1, 2, 3)):
    g = Shared()
    g.col = col
    par_cols = a["par"].shape[1]
    dram = lambda n, shape: nc.dram_tensor(n, shape, F32, kind="Internal").ap()
    with ExitStack() as ctx:
        sb = lambda n, shape, dt=F32: ctx.enter_context(nc.sbuf_tensor(n, shape, dt))
        g.h = sb("h", [P, KD, T1])
        g.par = sb("par", [P, par_cols])
        g.ones, g.ident, g.mean64 = sb("ones", [P, P]), sb("ident", [P, P]), sb("mean64", [P, P])
        with stage(nc, "start", "loaded", "ones") as s:
            with nc.Block() as block:
                @block.sync
                def _(sp):
                    T = a["h0"].shape[1]
                    sp.dma_start(g.h[:, :, 0:T], a["h0"].rearrange("(k p) t -> p k t", p=P)).then_inc(s["loaded"], 16)
                    sp.dma_start(g.par[:, :], a["par"]).then_inc(s["loaded"], 16)
                    sp.dma_start(g.ident[:, :], a["ident"]).then_inc(s["loaded"], 16)
                    sp.dma_start(g.mean64[:, :], a["mean64"]).then_inc(s["loaded"], 16)
                    sp.wait_ge(s["loaded"], 64)

                @block.vector
                def _(dve):
                    dve.memset(g.ones[:, :], 1.0).then_inc(s["ones"], 1)

        @contextmanager
        def parts(name):
            with nc.sbuf_tensor(name + "_uhi", [P, KD, T1], F32R) as uhi, \
                 nc.sbuf_tensor(name + "_ulo", [P, KD, T1], F32R) as ulo:
                g.uhi, g.ulo = uhi, ulo
                yield

        g.parts = parts
        if 1 in blocks:
            block1(nc, g, a, dram("proj1", (TILES_1 * P, T1)))
        if 2 in blocks:
            block2(nc, g, a, dram)
        if 3 in blocks:
            block3(nc, g, a, dram, out)
        else:
            with stage(nc, "dump", "st") as s:
                with nc.Block() as block:
                    @block.sync
                    def _(sp):
                        sp.dma_start(out.rearrange("(k p) t -> p k t", p=P), g.h[:, :, 0:SEQ]).then_inc(s["st"], 16)
                        sp.wait_ge(s["st"], 16)


def kernel(**inputs):
    import concourse.bacc as bacc
    from concourse.bass_utils import run_bass_kernel_spmd

    arrays, col = layout({k: np.asarray(v) for k, v in inputs.items()})
    arrays = {k: np.ascontiguousarray(v) for k, v in arrays.items()}
    nc = bacc.Bacc("TRN2", target_bir_lowering=False, num_devices=1)
    a = {k: nc.dram_tensor(f"in_{k}", v.shape, F32, kind="ExternalInput").ap() for k, v in arrays.items()}
    out = nc.dram_tensor("out_t", (D, SEQ), F32, kind="ExternalOutput").ap()
    program(nc, a, out, col)
    r = run_bass_kernel_spmd(nc, [{f"in_{k}": v for k, v in arrays.items()}], core_ids=[0])
    return np.ascontiguousarray(r.results[0]["out_t"].T)[None]
```

```python
from contextlib import ExitStack, contextmanager

import numpy as np
import concourse.bass as bass
from concourse import mybir

F32 = mybir.dt.float32
F32R = mybir.dt.float32r
ACT = mybir.ActivationFunctionType
ALU = mybir.AluOpType
ds = bass.ds

P = 128
D = 1024
KD = D // P
SEQ = 1024
META = 16
EPS = 1e-6
CH = 64
NCH = SEQ // CH
M_Q, M_K, M_V, M_O, R_Q, R_K, R_V, R_G, W_R, W_K, W_V, W_WA, W_GL, M_GATE = (
    0, 2, 4, 6, 8, 11, 14, 17, 20, 23, 26, 29, 30, 31)
G_Q, G_K, G_V, G_Z, G_SU, G_SV, G_GATE = 0, 4, 8, 12, 16, 20, 24
TILES_1, TILES_2, TILES_3 = 16, 32, 26


class Stage(dict):
    pass


class Shared:
    pass


@contextmanager
def stage(nc, name, *names):
    with ExitStack() as ctx:
        s = Stage((n, ctx.enter_context(nc.semaphore(f"{name}_{n}"))) for n in names)
        s.sb = lambda n, shape, dt=F32: ctx.enter_context(nc.sbuf_tensor(f"{name}_{n}", shape, dt))
        s.ps = lambda n, shape, dt=F32: ctx.enter_context(nc.psum_tensor(f"{name}_{n}", shape, dt))
        yield s
        clear(nc, s)


def clear(nc, s):
    with nc.Block() as block:
        @block.gpsimd
        def _(pool):
            for sem in list(s.values())[0::2]:
                pool.sem_clear(sem)

        @block.sync
        def _(sp):
            for sem in list(s.values())[1::2]:
                sp.sem_clear(sem)


def chain(eng, own):
    count = {}

    def link(ins, sem=None):
        sem = own if sem is None else sem
        count[id(sem)] = count.get(id(sem), 0) + 1
        ins.then_inc(sem, 1)
        eng.wait_ge(sem, count[id(sem)])

    return link


def own_chain(eng, s):
    eng.sem_clear(s["own"])
    return chain(eng, s["own"])


def rsqrt(act, s, x, n):
    act.activation(x, x, ACT.Ln).then_inc(s["logged"], 1)
    act.wait_ge(s["logged"], n)
    act.activation(x, x, ACT.Exp, scale=-0.5).then_inc(s["rooted"], 1)


def cuts(T):
    n = 4 if T == SEQ + META else 2
    return n, T // n


def flat(ps, T):
    n, w = cuts(T)
    return ps[:, 0:n, 0:w]


def sliced(ap, T):
    n, w = cuts(T)
    return ap.rearrange("p (n w) -> p n w", n=n)


DENSE = ("landed0", "landed1", "hi0", "hi1", "lo0", "lo1", "done0", "done1", "free0", "free1",
         "stored0", "stored1", "own", "act", "conv0", "conv1", "silu0", "silu1")


def weight_buffers(s):
    s.raw = [s.sb(f"raw{b}", [P, KD, P]) for b in range(2)]
    s.whi = [s.sb(f"whi{b}", [P, KD, P], F32R) for b in range(2)]
    s.wlo = [s.sb(f"wlo{b}", [P, KD, P], F32R) for b in range(2)]
    s.psum = s.ps("acc", [P, 8, 512])
    s.landed, s.hi, s.lo = [s["landed0"], s["landed1"]], [s["hi0"], s["hi1"]], [s["lo0"], s["lo1"]]
    s.done, s.free, s.stored = [s["done0"], s["done1"]], [s["free0"], s["free1"]], [s["stored0"], s["stored1"]]


def grant(nc, s):
    with nc.Block() as block:
        @block.gpsimd
        def _(pool):
            for sem in (*s.lo, *s.done, *s.free, s["act"]):
                pool.sem_inc(sem, 1)
            for sem in s.stored:
                pool.sem_inc(sem, 16)


def load_tile(sp, s, b, it, src, kt):
    sp.wait_ge(s.lo[b], it + 1)
    sp.dma_start(s.raw[b][:, 0:kt, :], src).then_inc(s.landed[b], 16)


def split_hi(act, s, b, it, kt):
    act.wait_ge(s.landed[b], (it + 1) * 16)
    act.wait_ge(s.done[b], it + 1)
    act.activation(s.whi[b][:, 0:kt, :], s.raw[b][:, 0:kt, :], ACT.Copy).then_inc(s.hi[b], 1)


def split_lo(pool, s, b, it, kt):
    pool.wait_ge(s.hi[b], it + 1)
    pool.tensor_tensor(s.wlo[b][:, 0:kt, :], s.raw[b][:, 0:kt, :], s.whi[b][:, 0:kt, :].bitcast(F32),
                       ALU.subtract).then_inc(s.lo[b], 1)


def product(pe, s, b, it, hi, lo, T, kt):
    n, w = cuts(T)
    pe.wait_ge(s.lo[b], it + 2)
    pe.wait_ge(s.free[b], it + 1)
    for k in range(kt):
        for j in range(n):
            out = s.psum[:, 4 * b + j, 0:w]
            x_hi, x_lo = hi[:, k, j * w:j * w + w], lo[:, k, j * w:j * w + w]
            pe.matmul(out, s.whi[b][:, k, :], x_hi, start=(k == 0), stop=False)
            pe.matmul(out, s.whi[b][:, k, :], x_lo, start=False, stop=False)
            mm = pe.matmul(out, s.wlo[b][:, k, :], x_hi, start=False, stop=(k == kt - 1))
    mm.then_inc(s.done[b], 1)


def dense(nc, name, g, W, tiles, T, store=None, conv=None):
    Wt = W.rearrange("(k p) c -> p k c", p=P)
    pairs = tiles // 2
    with stage(nc, name, *DENSE) as s:
        weight_buffers(s)
        stg = [s.sb(f"stg{b}", [P, T]) for b in range(2)] if store is not None else None
        if conv:
            taps, lead, col = conv
            xs, par = s.sb("x", [P, taps - 1 + T]), s.sb("par", [P, taps])
            with nc.Block() as block:
                @block.vector
                def _(dve):
                    dve.memset(xs[:, :], 0.0).then_inc(s["own"], 1)
                    dve.wait_ge(s["own"], 1)
        grant(nc, s)
        with nc.Block() as block:
            @block.sync
            def _(sp):
                with sp.Fori(0, pairs) as i:
                    for b in range(2):
                        load_tile(sp, s, b, i, Wt[:, :, ds(i * (2 * P) + b * P, P)], KD)

            @block.scalar
            def _(act):
                def put(b, i):
                    if conv:
                        act.wait_ge(s[f"conv{b}"], i + 1)
                        act.activation(stg[b][:, :], stg[b][:, :], ACT.Silu).then_inc(s[f"silu{b}"], 1)
                        act.wait_ge(s[f"silu{b}"], i + 1)
                    else:
                        act.wait_ge(s.free[b], i + 2)
                    act.dma_start(store[ds(i * (2 * P) + b * P, P), :], stg[b][:, :]).then_inc(s.stored[b], 16)

                if store is None:
                    with act.Fori(0, pairs) as i:
                        for b in range(2):
                            split_hi(act, s, b, i, KD)
                else:
                    for b in range(2):
                        split_hi(act, s, b, 0, KD)
                    with act.Fori(0, pairs - 1) as i:
                        for b in range(2):
                            put(b, i)
                            split_hi(act, s, b, i + 1, KD)
                    for b in range(2):
                        put(b, pairs - 1)
                    for b in range(2):
                        act.wait_ge(s.stored[b], 16 * pairs + 16)

            @block.gpsimd
            def _(pool):
                with pool.Fori(0, pairs) as i:
                    for b in range(2):
                        split_lo(pool, s, b, i, KD)

            @block.tensor
            def _(pe):
                with pe.Fori(0, pairs) as i:
                    for b in range(2):
                        product(pe, s, b, i, g.uhi, g.ulo, T, KD)

            @block.vector
            def _(dve):
                with dve.Fori(0, pairs) as i:
                    for b in range(2):
                        acc = flat(s.psum[:, 4 * b:4 * b + 4, :], T)
                        dve.wait_ge(s.done[b], i + 2)
                        if conv:
                            dve.tensor_copy(sliced(xs[:, lead:lead + T], T), acc).then_inc(s.free[b], 1)
                            link = own_chain(dve, s)
                            link(dve.tensor_copy(par[:, :], g.par[:, ds(i * (2 * taps) + (b * taps + g.col[col]),
                                                                         taps)]))
                            dve.wait_ge(s.free[b], i + 2)
                            dve.wait_ge(s.stored[b], i * 16 + 16)
                            y = stg[b][:, :]
                            link(dve.tensor_scalar(y, xs[:, 0:T], par[:, 0:1], None, ALU.mult))
                            for k in range(1, taps - 1):
                                link(dve.scalar_tensor_tensor(y, xs[:, k:k + T], par[:, k:k + 1], y,
                                                              ALU.mult, ALU.add))
                            dve.scalar_tensor_tensor(y, xs[:, taps - 1:taps - 1 + T], par[:, taps - 1:taps], y,
                                                     ALU.mult, ALU.add).then_inc(s[f"conv{b}"], 1)
                            dve.wait_ge(s[f"conv{b}"], i + 1)
                        elif store is not None:
                            dve.wait_ge(s.stored[b], i * 16 + 16)
                            dve.tensor_copy(sliced(stg[b][:, :], T), acc).then_inc(s.free[b], 1)
                        else:
                            n, w = cuts(T)
                            h = g.h[:, ds(i * 2 + b, 1), 0:T].rearrange("p a (n w) -> p (a n) w", n=n)
                            dve.tensor_tensor(h, h, acc, ALU.add).then_inc(s.free[b], 1)


def ffn(nc, name, g, Wup, Wdown, groups, T, gated):
    up, down = (W.rearrange("(k p) c -> p k c", p=P) for W in (Wup, Wdown))
    n, w = cuts(T)
    with stage(nc, name, *DENSE) as s:
        weight_buffers(s)
        xhi = s.sb("xhi", [P, 8, T], F32R)
        xlo = s.sb("xlo", [P, 8, T], F32R)
        sq = s.sb("sq", [P, T])
        silu = s.sb("silu", [P, T]) if gated else None
        grant(nc, s)

        def walk(eng, do_up, do_down):
            before, tile = 0, 0
            for many, kt in groups:
                ups = kt if gated else kt // 2
                per = ups + KD // 2

                def one(o):
                    with eng.Fori(0, ups) as j:
                        do_up(j, o * per + before + j, o * kt + tile, kt, o)
                    with eng.Fori(0, KD // 2) as j:
                        do_down(j, o * per + before + ups + j, o * kt + tile, kt, o)

                if many > 1:
                    with eng.Fori(0, many) as o:
                        one(o)
                else:
                    one(0)
                before += many * per
                tile += many * kt

        with nc.Block() as block:
            @block.sync
            def _(sp):
                def do_up(j, it, tile, kt, o):
                    for b in range(2):
                        at = tile * (2 * P if gated else P) + j * (2 * P) + b * P
                        load_tile(sp, s, b, it, up[:, :, ds(at, P)], KD)

                def do_down(j, it, tile, kt, o):
                    for b in range(2):
                        load_tile(sp, s, b, it, down[:, ds(tile, kt), ds(j * (2 * P) + b * P, P)], kt)

                walk(sp, do_up, do_down)

            @block.scalar
            def _(act):
                def do_up(j, it, tile, kt, o):
                    for b in range(2):
                        split_hi(act, s, b, it, KD)
                    if gated:
                        act.wait_ge(s["done0"], it + 2)
                        act.wait_ge(s["free1"], it + 1)
                        act.activation(sliced(silu[:, :], T), flat(s.psum[:, 0:4, :], T), ACT.Silu)\
                           .then_inc(s["free0"], 1)

                def do_down(j, it, tile, kt, o):
                    for b in range(2):
                        split_hi(act, s, b, it, kt)

                walk(act, do_up, do_down)

            @block.gpsimd
            def _(pool):
                def do_up(j, it, tile, kt, o):
                    for b in range(2):
                        split_lo(pool, s, b, it, KD)

                def do_down(j, it, tile, kt, o):
                    for b in range(2):
                        split_lo(pool, s, b, it, kt)

                walk(pool, do_up, do_down)

            @block.tensor
            def _(pe):
                def do_up(j, it, tile, kt, o):
                    for b in range(2):
                        product(pe, s, b, it, g.uhi, g.ulo, T, KD)

                def do_down(j, it, tile, kt, o):
                    pe.wait_ge(s["act"], tile + (kt + 1))
                    for b in range(2):
                        product(pe, s, b, it, xhi, xlo, T, kt)

                walk(pe, do_up, do_down)

            @block.vector
            def _(dve):
                def split(link, m):
                    link(dve.tensor_copy(xhi[:, ds(m, 1), :], sq[:, None, :]))
                    dve.tensor_tensor(xlo[:, ds(m, 1), :], sq[:, None, :],
                                      xhi[:, ds(m, 1), :].bitcast(F32), ALU.subtract).then_inc(s["act"], 1)

                def do_up(j, it, tile, kt, o):
                    if gated:
                        link = own_chain(dve, s)
                        dve.wait_ge(s["free0"], it + 2)
                        dve.wait_ge(s["done1"], it + 2)
                        dve.wait_ge(s["act"], tile + j + 1)
                        dve.tensor_tensor(sliced(sq[:, :], T), sliced(silu[:, :], T),
                                          flat(s.psum[:, 4:8, :], T), ALU.mult).then_inc(s["free1"], 1)
                        dve.wait_ge(s["free1"], it + 2)
                        split(link, j)
                        return
                    for b in range(2):
                        link = own_chain(dve, s)
                        dve.wait_ge(s.done[b], it + 2)
                        dve.wait_ge(s["act"], tile + j * 2 + (b + 1))
                        dve.tensor_scalar(sliced(sq[:, :], T), flat(s.psum[:, 4 * b:4 * b + 4, :], T),
                                          0.0, None, ALU.max).then_inc(s.free[b], 1)
                        dve.wait_ge(s.free[b], it + 2)
                        link(dve.tensor_tensor(sq[:, :], sq[:, :], sq[:, :], ALU.mult))
                        split(link, j * 2 + b)

                def do_down(j, it, tile, kt, o):
                    for b in range(2):
                        dve.wait_ge(s.done[b], it + 2)
                        h = g.h[:, ds(j * 2 + b, 1), 0:T].rearrange("p a (n w) -> p (a n) w", n=n)
                        dve.tensor_tensor(h, h, flat(s.psum[:, 4 * b:4 * b + 4, :], T), ALU.add)\
                           .then_inc(s.free[b], 1)

                walk(dve, do_up, do_down)


def norm(nc, name, g, src, groups, gain, T, eps=EPS, first=0, dest="u"):
    NB = 4
    with stage(nc, name, "squared", "added", "summed", "shifted", "logged", "rooted", "scaled", "upper", "low_p",
               "low_d", "out0", "out1") as s:
        buf = [s.sb(f"buf{b}", [P, T]) for b in range(NB)]
        tot, inv = s.sb("tot", [P, T]), s.sb("inv", [P, T])
        acc = s.ps("acc", [P, 8, 512])
        n, w = cuts(T)
        tiles = [(gi, k) for gi, (a, b) in enumerate(groups) for k in range(a, b)]
        x = lambda k: src[:, k, first:first + T]
        stored = [s["out0"], s["out1"]]

        def free(eng, k):
            if isinstance(dest, str):
                eng.wait_ge(s["upper"], k + 1)
                if dest == "u":
                    eng.wait_ge(s["low_d"] if k % 2 else s["low_p"], k // 2 + 1)
            else:
                eng.wait_ge(stored[k % 2], 16 * (k // 2 + 1))

        with nc.Block() as block:
            @block.scalar
            def _(act):
                for gi, (a, b) in enumerate(groups):
                    for k in range(a, b):
                        if k - a >= NB:
                            act.wait_ge(s["added"], k - NB + 1)
                        elif gi:
                            free(act, k - NB)
                        act.activation(buf[k % NB][:, :], x(k), ACT.Square).then_inc(s["squared"], 1)
                    act.wait_ge(s["shifted"], gi + 1)
                    rsqrt(act, s, inv[:, :], gi + 1)
                    for k in range(a, b):
                        if isinstance(dest, str):
                            act.wait_ge(s["scaled"], k + 1)
                            out = g.uhi[:, k, 0:T] if dest == "u" else g.h[:, k, 0:T]
                            act.activation(out, buf[k % NB][:, :], ACT.Copy).then_inc(s["upper"], 1)

            @block.tensor
            def _(pe):
                for gi, (a, b) in enumerate(groups):
                    pe.wait_ge(s["added"], b)
                    for j in range(n):
                        mm = pe.matmul(acc[:, 4 * (gi % 2) + j, 0:w], g.ones[:, :], tot[:, j * w:j * w + w],
                                       start=True, stop=True)
                    mm.then_inc(s["summed"], 1)

            @block.vector
            def _(dve):
                def lower(k):
                    dve.wait_ge(s["upper"], k + 1)
                    dve.tensor_tensor(g.ulo[:, k, 0:T], buf[k % NB][:, :], g.uhi[:, k, 0:T].bitcast(F32),
                                      ALU.subtract).then_inc(s["low_d"], 1)

                for gi, (a, b) in enumerate(groups):
                    for k in range(a, b):
                        dve.wait_ge(s["squared"], k + 1)
                        if k == a:
                            if gi:
                                dve.wait_ge(s["summed"], gi)
                            ins = dve.tensor_copy(tot[:, :], buf[k % NB][:, :])
                        else:
                            dve.wait_ge(s["added"], k)
                            ins = dve.tensor_tensor(tot[:, :], tot[:, :], buf[k % NB][:, :], ALU.add)
                        ins.then_inc(s["added"], 1)
                    dve.wait_ge(s["summed"], gi + 1)
                    if gi:
                        dve.wait_ge(s["scaled"], a)
                    dve.tensor_scalar(sliced(inv[:, :], T), flat(acc[:, 4 * (gi % 2):4 * (gi % 2) + 4, :], T),
                                      1.0 / ((b - a) * P), eps, ALU.mult, ALU.add).then_inc(s["shifted"], 1)
                    dve.wait_ge(s["rooted"], gi + 1)
                    for k in range(a, b):
                        if k - a >= NB:
                            free(dve, k - NB)
                        dve.scalar_tensor_tensor(buf[k % NB][:, :], x(k), g.par[:, gain + k:gain + k + 1],
                                                 inv[:, :], ALU.mult, ALU.mult).then_inc(s["scaled"], 1)
                        if dest == "u" and k % 2 == 0 and k > a:
                            lower(k - 1)
                    if dest == "u":
                        lower(b - 1)

            @block.gpsimd
            def _(pool):
                if dest == "u":
                    for gi, k in tiles[0::2]:
                        pool.wait_ge(s["upper"], k + 1)
                        pool.tensor_tensor(g.ulo[:, k, 0:T], buf[k % NB][:, :], g.uhi[:, k, 0:T].bitcast(F32),
                                           ALU.subtract).then_inc(s["low_p"], 1)

            @block.sync
            def _(sp):
                if not isinstance(dest, str):
                    for gi, k in tiles:
                        sp.wait_ge(s["scaled"], k + 1)
                        if k >= 2:
                            sp.wait_ge(stored[k % 2], 16 * (k // 2))
                        sp.dma_start(dest[k * P:(k + 1) * P, :], buf[k % NB][:, :]).then_inc(stored[k % 2], 16)
                    for b in range(2):
                        sp.wait_ge(stored[b], 16 * (len(tiles) // 2))


T1 = SEQ + META
LRU_HALO, CC_HALO = 3, 30
LRU_PAR = 10


def lru(nc, g, proj, wa, wx):
    with stage(nc, "lru", "zero", "gated", "loaded", "par", "conv", "gates", "sig_a", "sig_x", "loga", "decay", "tanh", "gelu",
               "power", "root", "own", "y") as s:
        xl, xc = s.sb("xl", [P, LRU_HALO + T1]), s.sb("xc", [P, T1])
        gate, r, ig = s.sb("gate", [P, T1]), s.sb("r", [P, T1]), s.sb("ig", [P, T1])
        a, th = s.sb("a", [P, T1]), s.sb("th", [P, T1])
        w_a, w_x = s.sb("wa", [P, P]), s.sb("wx", [P, P])
        par, tiny = s.sb("par", [P, LRU_PAR]), s.sb("tiny", [P, 6])
        acc = s.ps("acc", [P, 8, 512])
        n, w = cuts(T1)
        with nc.Block() as block:
            @block.vector
            def _(dve):
                dve.memset(xl[:, 0:LRU_HALO], 0.0).then_inc(s["zero"], 1)
        with nc.Fori(0, 4) as i:
            with nc.Block() as block:
                @block.sync
                def _(sp):
                    sp.dma_start(xl[:, LRU_HALO:], proj[ds(i * P, P), :]).then_inc(s["loaded"], 16)
                    sp.dma_start(gate[:, :], proj[ds(i * P + 4 * P, P), :]).then_inc(s["loaded"], 16)
                    sp.dma_start(w_a[:, :], wa[ds(i * P, P), :]).then_inc(s["loaded"], 16)
                    sp.dma_start(w_x[:, :], wx[ds(i * P, P), :]).then_inc(s["loaded"], 16)

                @block.vector
                def _(dve):
                    link = chain(dve, s["own"])
                    link(dve.tensor_copy(par[:, :], g.par[:, ds(i * LRU_PAR + g.col["lru"], LRU_PAR)]), s["par"])
                    dve.wait_ge(s["loaded"], 64)
                    link(dve.tensor_scalar(xc[:, :], xl[:, 0:T1], par[:, 0:1], par[:, 4:5], ALU.mult, ALU.add))
                    for k in range(1, 4):
                        link(dve.scalar_tensor_tensor(xc[:, :], xl[:, k:k + T1], par[:, k:k + 1], xc[:, :],
                                                      ALU.mult, ALU.add), s["conv"] if k == 3 else None)
                    dve.wait_ge(s["power"], 1)
                    e, z, z2, q = tiny[:, 0:1], tiny[:, 1:2], tiny[:, 2:3], tiny[:, 3:4]
                    link(dve.tensor_scalar(z, e, 2.0, None, ALU.add))
                    link(dve.reciprocal(z, z))
                    link(dve.tensor_tensor(z, z, e, ALU.mult))
                    link(dve.tensor_tensor(z2, z, z, ALU.mult))
                    link(dve.tensor_scalar(q, z2, 1.0 / 15, 1.0 / 13, ALU.mult, ALU.add))
                    for m in (11, 9, 7, 5, 3, 1):
                        link(dve.tensor_tensor(q, q, z2, ALU.mult))
                        link(dve.tensor_scalar(q, q, 1.0 / m, None, ALU.add))
                    link(dve.tensor_tensor(q, q, z, ALU.mult))
                    link(dve.tensor_scalar(z, par[:, 7:8], -1.0, 0.0, ALU.mult, ALU.max))
                    link(dve.tensor_scalar(q, q, 2.0, z, ALU.mult, ALU.add))
                    link(dve.tensor_scalar(q, q, -8.0, None, ALU.mult))
                    dve.wait_ge(s["sig_a"], 1)
                    link(dve.tensor_scalar(r[:, :], r[:, :], q, None, ALU.mult), s["loga"])
                    dve.wait_ge(s["sig_x"], 1)
                    link(dve.tensor_tensor(ig[:, :], ig[:, :], xc[:, :], ALU.mult))
                    dve.wait_ge(s["decay"], 1)
                    link(dve.tensor_tensor(xc[:, :], a[:, :], a[:, :], ALU.mult))
                    dve.wait_ge(s["tanh"], 1)
                    link(dve.scalar_tensor_tensor(th[:, :], xc[:, :], 1.0, th[:, :], ALU.add, ALU.mult), s["gates"])
                    dve.wait_ge(s["root"], 1)
                    link(dve.tensor_tensor(ig[:, :], ig[:, :], th[:, :], ALU.mult))
                    link(dve.tensor_tensor_scan(xc[:, :], a[:, :], ig[:, :], 0.0, ALU.mult, ALU.add))
                    dve.wait_ge(s["gelu"], 1)
                    dve.tensor_tensor(g.y[:, ds(i, 1), :], xc[:, None, :], gate[:, None, :], ALU.mult)\
                       .then_inc(s["y"], 1)

                @block.tensor
                def _(pe):
                    pe.wait_ge(s["conv"], 1)
                    pe.wait_ge(s["loaded"], 64)
                    for b, wt in enumerate((w_a, w_x)):
                        for j in range(n):
                            mm = pe.matmul(acc[:, 4 * b + j, 0:w], wt[:, :], xc[:, j * w:j * w + w],
                                           start=True, stop=True)
                        mm.then_inc(s["gated"], 1)

                @block.scalar
                def _(act):
                    act.wait_ge(s["loaded"], 64)
                    act.activation(gate[:, :], gate[:, :], ACT.Gelu_apprx_tanh).then_inc(s["gelu"], 1)
                    act.wait_ge(s["par"], 1)
                    act.activation(tiny[:, 0:1], par[:, 7:8], ACT.Abs).then_inc(s["y"], 1)
                    act.wait_ge(s["y"], 1)
                    act.activation(tiny[:, 0:1], tiny[:, 0:1], ACT.Exp, scale=-1.0).then_inc(s["power"], 1)
                    act.wait_ge(s["gated"], 2)
                    act.activation(sliced(r[:, :], T1), flat(acc[:, 0:4, :], T1), ACT.Sigmoid,
                                   bias=par[:, 5:6]).then_inc(s["sig_a"], 1)
                    act.activation(sliced(ig[:, :], T1), flat(acc[:, 4:8, :], T1), ACT.Sigmoid,
                                   bias=par[:, 6:7]).then_inc(s["sig_x"], 1)
                    act.wait_ge(s["loga"], 1)
                    act.activation(a[:, :], r[:, :], ACT.Exp).then_inc(s["decay"], 1)
                    act.activation(th[:, :], r[:, :], ACT.Tanh, scale=-1.0).then_inc(s["tanh"], 1)
                    act.wait_ge(s["gates"], 1)
                    act.activation(th[:, :], th[:, :], ACT.Sqrt).then_inc(s["root"], 1)
            clear(nc, s)


CC_TAPS = 31
CC_PAR = CC_TAPS + 1


def conv_mixer(nc, g, proj):
    with stage(nc, "cc", "zero", "loaded", "par", "sig", "own", "y") as s:
        v, gate, par = s.sb("v", [P, CC_HALO + T1]), s.sb("gate", [P, T1]), s.sb("par", [P, CC_PAR])
        acc = s.sb("acc", [P, T1])
        with nc.Block() as block:
            @block.vector
            def _(dve):
                dve.memset(v[:, 0:CC_HALO], 0.0).then_inc(s["zero"], 1)
        with nc.Fori(0, 4) as i:
            with nc.Block() as block:
                @block.sync
                def _(sp):
                    sp.dma_start(v[:, CC_HALO:], proj[ds(i * P + 8 * P, P), :]).then_inc(s["loaded"], 16)
                    sp.dma_start(gate[:, :], proj[ds(i * P + 12 * P, P), :]).then_inc(s["loaded"], 16)

                @block.scalar
                def _(act):
                    act.wait_ge(s["loaded"], 32)
                    act.activation(gate[:, :], gate[:, :], ACT.Sigmoid).then_inc(s["sig"], 1)

                @block.vector
                def _(dve):
                    link = chain(dve, s["own"])
                    link(dve.tensor_copy(par[:, :], g.par[:, ds(i * CC_PAR + g.col["cc"], CC_PAR)]))
                    dve.wait_ge(s["loaded"], 32)
                    dve.wait_ge(s["sig"], 1)
                    link(dve.tensor_tensor(v[:, CC_HALO:], v[:, CC_HALO:], gate[:, :], ALU.mult))
                    link(dve.tensor_scalar(acc[:, :], v[:, 0:T1], par[:, 0:1], par[:, CC_TAPS:CC_TAPS + 1],
                                           ALU.mult, ALU.add))
                    for k in range(1, CC_TAPS):
                        last = k == CC_TAPS - 1
                        out = g.y[:, ds(i + 4, 1), :] if last else acc[:, None, :]
                        link(dve.scalar_tensor_tensor(out, v[:, None, k:k + T1], par[:, k:k + 1],
                                                      acc[:, None, :], ALU.mult, ALU.add))
            clear(nc, s)
    with stage(nc, "ccln", "summed", "centred", "squared", "shifted", "logged", "rooted", "scaled", "own", "silu") as s:
        acc = s.ps("acc", [P, 8, 512])
        mean, inv = s.sb("mean", [P, T1]), s.sb("inv", [P, T1])
        sq = [s.sb(f"sq{b}", [P, T1]) for b in range(2)]
        n, w = cuts(T1)
        with nc.Block() as block:
            @block.tensor
            def _(pe):
                for k in range(4):
                    for j in range(n):
                        mm = pe.matmul(acc[:, j, 0:w], g.ones[:, :], g.y[:, 4 + k, j * w:j * w + w],
                                       start=(k == 0), stop=(k == 3))
                mm.then_inc(s["summed"], 1)
                for k in range(4):
                    pe.wait_ge(s["squared"], k + 1)
                    for j in range(n):
                        mm = pe.matmul(acc[:, 4 + j, 0:w], g.ones[:, :], sq[k % 2][:, j * w:j * w + w],
                                       start=(k == 0), stop=(k == 3))
                    mm.then_inc(s["summed"], 1)

            @block.vector
            def _(dve):
                link = chain(dve, s["own"])
                dve.wait_ge(s["summed"], 1)
                link(dve.tensor_scalar(sliced(mean[:, :], T1), flat(acc[:, 0:4, :], T1), 1.0 / (4 * P), None,
                                       ALU.mult))
                for k in range(4):
                    dve.tensor_tensor(g.y[:, 4 + k, :], g.y[:, 4 + k, :], mean[:, :], ALU.subtract)\
                       .then_inc(s["centred"], 1)
                dve.wait_ge(s["centred"], 4)
                dve.wait_ge(s["summed"], 5)
                dve.tensor_scalar(sliced(inv[:, :], T1), flat(acc[:, 4:8, :], T1), 1.0 / (4 * P), EPS,
                                  ALU.mult, ALU.add).then_inc(s["shifted"], 1)
                dve.wait_ge(s["rooted"], 1)
                for k in range(4):
                    link(dve.scalar_tensor_tensor(g.y[:, 4 + k, :], g.y[:, 4 + k, :],
                                                  g.par[:, g.col["ccg"] + k:g.col["ccg"] + k + 1], inv[:, :],
                                                  ALU.mult, ALU.mult), s["scaled"])

            @block.scalar
            def _(act):
                for k in range(4):
                    act.wait_ge(s["centred"], k + 1)
                    if k >= 2:
                        act.wait_ge(s["summed"], k)
                    act.activation(sq[k % 2][:, :], g.y[:, 4 + k, :], ACT.Square).then_inc(s["squared"], 1)
                act.wait_ge(s["shifted"], 1)
                rsqrt(act, s, inv[:, :], 1)
                for k in range(4):
                    act.wait_ge(s["scaled"], k + 1)
                    act.activation(g.y[:, 4 + k, :], g.y[:, 4 + k, :], ACT.Silu,
                                   bias=g.par[:, g.col["ccb"] + k:g.col["ccb"] + k + 1]).then_inc(s["silu"], 1)


def block1(nc, g, a, proj):
    with g.parts("a1"):
        norm(nc, "n1", g, g.h, [(0, KD)], g.col["g1"], T1)
        dense(nc, "in1", g, a["w_in"], TILES_1, T1, proj)
    with nc.sbuf_tensor("y1", [P, KD, T1], F32) as y:
        g.y = y
        lru(nc, g, proj, a["lru_wa"], a["lru_wx"])
        conv_mixer(nc, g, proj)
        with g.parts("b1"):
            norm(nc, "no1", g, g.y, [(0, 4), (4, KD)], g.col["go1"], T1)
            dense(nc, "out1", g, a["w_out"], KD, T1)
    with g.parts("c1"):
        norm(nc, "nm1", g, g.h, [(0, KD)], g.col["gm1"], T1)
        ffn(nc, "ff1", g, a["w_mlp_up"], a["w_mlp_down"], [(4, KD)], T1, gated=False)
    norm(nc, "nf1", g, g.h, [(0, KD)], g.col["gf1"], SEQ, first=META, dest="h")


def halves(ap):
    return ap.rearrange("p (n w) -> p n w", n=2)


def rotate(nc, g, proj, cos, sin, swap):
    with stage(nc, "rot", "const", "loaded", "swapped", "own", "rotated", "stored") as s:
        c, sn, sw = s.sb("c", [P, SEQ]), s.sb("s", [P, SEQ]), s.sb("sw", [P, P])
        x, y = s.sb("x", [P, SEQ]), s.sb("y", [P, SEQ])
        acc = s.ps("acc", [P, 2, 512])
        with nc.Block() as block:
            @block.sync
            def _(sp):
                for t, src in ((c, cos), (sn, sin), (sw, swap)):
                    sp.dma_start(t[:, :], src).then_inc(s["const"], 16)
                sp.wait_ge(s["const"], 48)
        with nc.Fori(0, 6) as i:
            with nc.Block() as block:
                @block.sync
                def _(sp):
                    sp.dma_start(x[:, :], proj[ds(i * P + R_Q * P, P), :]).then_inc(s["loaded"], 16)
                    sp.wait_ge(s["rotated"], 1)
                    sp.dma_start(proj[ds(i * P + R_Q * P, P), :], y[:, :]).then_inc(s["stored"], 16)
                    sp.wait_ge(s["stored"], 16)

                @block.tensor
                def _(pe):
                    pe.wait_ge(s["loaded"], 16)
                    for j in range(2):
                        mm = pe.matmul(acc[:, j, :], sw[:, :], x[:, j * 512:j * 512 + 512], start=True, stop=True)
                    mm.then_inc(s["swapped"], 1)

                @block.vector
                def _(dve):
                    link = chain(dve, s["own"])
                    dve.wait_ge(s["swapped"], 1)
                    link(dve.tensor_tensor(halves(y[:, :]), acc[:, :, :], halves(sn[:, :]), ALU.mult))
                    link(dve.tensor_tensor(x[:, :], x[:, :], c[:, :], ALU.mult))
                    link(dve.tensor_tensor(y[:, :], y[:, :], x[:, :], ALU.add), s["rotated"])
            clear(nc, s)


def mlstm_gates(nc, g, proj, rows):
    with stage(nc, "mg", "loaded", "own", "abs", "power", "log", "sum", "em", "stored") as s:
        names = ("gi", "gf", "l", "m", "b", "c", "top", "one")
        gi, gf, l, m, b, c, top, one = (s.sb(n, [4, SEQ]) for n in names)
        with nc.Block() as block:
            @block.sync
            def _(sp):
                at = M_GATE * P
                sp.dma_start(gi[:, :], proj[at:at + 4, :]).then_inc(s["loaded"], 16)
                sp.dma_start(gf[:, :], proj[at + 4:at + 8, :]).then_inc(s["loaded"], 16)
                sp.wait_ge(s["sum"], 1)
                sp.dma_start(rows[0:4, :], top[:, :]).then_inc(s["stored"], 16)
                sp.dma_start(rows[8:12, :], c[:, :]).then_inc(s["stored"], 16)
                sp.wait_ge(s["em"], 1)
                sp.dma_start(rows[4:8, :], b[:, :]).then_inc(s["stored"], 16)
                sp.wait_ge(s["stored"], 48)

            @block.scalar
            def _(act):
                bf = g.par[0:4, g.col["mb"] + 1:g.col["mb"] + 2]
                act.wait_ge(s["loaded"], 32)
                act.activation(l[:, :], gf[:, :], ACT.Abs, bias=bf).then_inc(s["abs"], 1)
                act.wait_ge(s["abs"], 1)
                act.activation(l[:, :], l[:, :], ACT.Exp, scale=-1.0).then_inc(s["power"], 1)
                act.wait_ge(s["power"], 1)
                act.activation(l[:, :], l[:, :], ACT.Ln, bias=1.0).then_inc(s["log"], 1)
                act.wait_ge(s["sum"], 1)
                act.activation(b[:, :], m[:, :], ACT.Exp).then_inc(s["em"], 1)

            @block.vector
            def _(dve):
                link = chain(dve, s["own"])
                bi, bf = (g.par[0:4, g.col["mb"] + k:g.col["mb"] + k + 1] for k in range(2))
                link(dve.memset(one[:, :], 1.0))
                dve.wait_ge(s["loaded"], 32)
                link(dve.tensor_scalar(m[:, :], gf[:, :], bf, 0.0, ALU.add, ALU.min))
                dve.wait_ge(s["log"], 1)
                link(dve.tensor_tensor(m[:, :], m[:, :], l[:, :], ALU.subtract))
                link(dve.tensor_tensor_scan(b[:, :], one[:, :], m[:, :], 0.0, ALU.mult, ALU.add))
                link(dve.scalar_tensor_tensor(c[:, :], gi[:, :], bi, b[:, :], ALU.add, ALU.subtract))
                link(dve.tensor_tensor_scan(top[:, :], c[:, :], c[:, :], -3e38, ALU.max, ALU.max))
                link(dve.scalar_tensor_tensor(m[:, :], b[:, :], -1.0, top[:, :], ALU.mult, ALU.subtract))
                link(dve.tensor_scalar(top[:, :], top[:, :], -1.0, None, ALU.mult), s["sum"])


def attention(nc, name, g, proj, y, heads, q0, k0, v0, y0, rows=None, tri=None, ramps=None):
    lstm = rows is not None
    steps = []
    for n in range(2):
        for sb in range(4 * n + 4):
            j0 = max(sb * P, 512 * n)
            steps.append((n, sb, j0, 512 * (n + 1) - j0))
    last = [max(t for t, st in enumerate(steps) if st[0] == n) for n in range(2)]
    with stage(nc, name, "loaded", "turned", "values", "arg", "weight", "score", "prob", "out", "own", "result",
               "stored", "one") as s:
        q, k, v = (s.sb(n, [64, SEQ]) for n in "qkv")
        cv = 128 if lstm else 64
        vt = s.sb("vt", [P, 8, cv])
        e = [s.sb(f"e{b}", [P, 512]) for b in range(2)] if lstm else None
        pr = [s.sb(f"p{b}", [P, 512]) for b in range(2)]
        res = s.sb("res", [64, SEQ])
        turned = s.ps("turned", [P, 8, 64])
        sc = s.ps("score", [P, 2, 512])
        o = s.ps("o", [P, 2, 512])
        if lstm:
            mb, em, ck, tr = s.sb("mb", [P, SEQ]), s.sb("em", [P, SEQ]), s.sb("ck", [P, 8]), s.sb("tri", [P, 512])
            den, rec = s.sb("den", [P, 512]), s.sb("rec", [64, 512])
        else:
            ramp = s.sb("ramp", [P, SEQ])
        n_loads = 6 if lstm else 4
        with nc.Block() as block:
            @block.sync
            def _(sp):
                if lstm:
                    sp.dma_start(tr[:, :], tri).then_inc(s["loaded"], 16)
                    sp.wait_ge(s["loaded"], 16)

            @block.vector
            def _(dve):
                if lstm:
                    dve.memset(vt[:, :, 64:128], 1.0).then_inc(s["one"], 1)
        clear(nc, s)
        with nc.Fori(0, heads) as h:
            with nc.Block() as block:
                @block.sync
                def _(sp):
                    for t, at in ((v, v0), (k, k0), (q, q0)):
                        sp.dma_start(t[:, :], proj[ds(h * 64 + at, 64), :]).then_inc(s["loaded"], 16)
                    if lstm:
                        sp.dma_start(mb[:, :], rows[ds(h, 1), :].broadcast_to([P, SEQ])).then_inc(s["loaded"], 16)
                        sp.dma_start(em[64:128, :], rows[ds(h + 4, 1), :].broadcast_to([64, SEQ]))\
                          .then_inc(s["loaded"], 16)
                        sp.dma_start(ck[:, :], rows[ds(h + 8, 1), :].rearrange("a (s p) -> p (a s)", p=P),
                                     allow_slow_non_contiguous=True)\
                          .then_inc(s["loaded"], 16)
                    else:
                        sp.dma_start(ramp[:, :], ramps[ds(h * P, P), :]).then_inc(s["loaded"], 16)
                    sp.wait_ge(s["result"], 2)
                    sp.dma_start(y[ds(h * 64 + y0, 64), :], res[:, :]).then_inc(s["stored"], 16)
                    sp.wait_ge(s["stored"], 16)

                @block.tensor
                def _(pe):
                    pe.wait_ge(s["loaded"], 16 * n_loads)
                    for b in range(8):
                        mm = pe.transpose(turned[:, b, :], v[:, b * P:(b + 1) * P], g.ident[0:64, 0:64])
                    mm.then_inc(s["turned"], 1)

                    def values(t):
                        n, sb, j0, w = steps[t]
                        pe.wait_ge(s["values"], 1)
                        pe.wait_ge(s["prob"], t + 1)
                        mm = pe.matmul(o[0:cv, n, j0 - 512 * n:512], vt[:, sb, :], pr[t % 2][:, 0:w],
                                       start=(sb == 0), stop=(t == last[n]))
                        mm.then_inc(s["out"], 1)

                    for t, (n, sb, j0, w) in enumerate(steps):
                        if t >= 2:
                            pe.wait_ge(s["prob"], t - 1)
                        pe.matmul(sc[:, t % 2, 0:w], k[:, sb * P:(sb + 1) * P], q[:, j0:j0 + w],
                                  start=True, stop=True).then_inc(s["score"], 1)
                        if t:
                            values(t - 1)
                    values(len(steps) - 1)

                if lstm:
                    @block.scalar
                    def _(act):
                        for t, (n, sb, j0, w) in enumerate(steps):
                            act.wait_ge(s["arg"], t + 1)
                            act.activation(e[t % 2][:, 0:w], e[t % 2][:, 0:w], ACT.Exp).then_inc(s["weight"], 1)

                @block.vector
                def _(dve):
                    link = chain(dve, s["own"])
                    dve.wait_ge(s["loaded"], 16 * n_loads)
                    dve.wait_ge(s["turned"], 1)
                    dve.tensor_copy(vt[:, :, 0:64], turned[:, :, :]).then_inc(s["values"], 1)

                    def arg(t):
                        n, sb, j0, w = steps[t]
                        if t >= 2:
                            dve.wait_ge(s["prob"], t - 1)
                        if j0 == sb * P:
                            ins = dve.scalar_tensor_tensor(e[t % 2][:, 0:w], mb[:, j0:j0 + w], ck[:, sb:sb + 1],
                                                           tr[:, 0:w], ALU.add, ALU.min)
                        else:
                            ins = dve.tensor_scalar(e[t % 2][:, 0:w], mb[:, j0:j0 + w], ck[:, sb:sb + 1], 0.0,
                                                    ALU.add, ALU.min)
                        ins.then_inc(s["arg"], 1)

                    if lstm:
                        arg(0)
                    for t, (n, sb, j0, w) in enumerate(steps):
                        if lstm and t + 1 < len(steps):
                            arg(t + 1)
                        dve.wait_ge(s["score"], t + 1)
                        if t >= 2:
                            dve.wait_ge(s["out"], t - 1)
                        if lstm:
                            dve.wait_ge(s["weight"], t + 1)
                            dve.scalar_tensor_tensor(pr[t % 2][:, 0:w], sc[:, t % 2, 0:w], 0.125,
                                                     e[t % 2][:, 0:w], ALU.mult, ALU.mult).then_inc(s["prob"], 1)
                        else:
                            at = j0 - sb * P
                            dve.tensor_tensor(pr[t % 2][:, 0:w], sc[:, t % 2, 0:w], ramp[:, at:at + w],
                                              ALU.mult).then_inc(s["prob"], 1)
                        if t == last[n]:
                            dve.wait_ge(s["out"], t + 1)
                            r = res[:, 512 * n:512 * n + 512]
                            if lstm:
                                dn = den[64:128, :]
                                link(dve.scalar_tensor_tensor(dn, o[64:128, n, :], -1.0,
                                                              em[64:128, 512 * n:512 * n + 512],
                                                              ALU.mult, ALU.max))
                                link(dve.tensor_tensor(dn, o[64:128, n, :], dn, ALU.max))
                                link(dve.reciprocal(rec[:, :], den[64:128, :]))
                                dve.tensor_tensor(r, o[0:64, n, :], rec[:, :], ALU.mult).then_inc(s["result"], 1)
                            else:
                                dve.tensor_copy(r, o[0:64, n, :]).then_inc(s["result"], 1)
            clear(nc, s)


def head_norm(nc, name, g, src, tiles, y0, eps, gate_rows, act_gate, center=True, gain=None, bias=None,
              extra=None, src2=None):
    with stage(nc, name, "loaded", "summed", "centred", "squared", "var", "shifted", "logged", "rooted", "gate", "own",
               "par") as s:
        x, gt, sq, par = s.sb("x", [P, SEQ]), s.sb("gate", [P, SEQ]), s.sb("sq", [P, SEQ]), s.sb("par", [P, 2])
        ex = s.sb("ex", [P, SEQ])
        acc = s.ps("acc", [P, 4, 512])
        loads = [(x, src, y0 if src2 is None else 0), (gt, *gate_rows)]
        if extra is not None:
            loads.append((ex, extra, 0))
        if src2 is not None:
            loads.append((ex, src2, 0))
        with nc.Fori(0, tiles) as i:
            with nc.Block() as block:
                @block.sync
                def _(sp):
                    for t, a, at in loads:
                        sp.dma_start(t[:, :], a[ds(i * P + at * P, P), :]).then_inc(s["loaded"], 16)

                @block.tensor
                def _(pe):
                    pe.wait_ge(s["centred"], 1)
                    if center:
                        for j in range(2):
                            mm = pe.matmul(acc[:, j, :], g.mean64[:, :], x[:, j * 512:j * 512 + 512],
                                           start=True, stop=True)
                        mm.then_inc(s["summed"], 1)
                    pe.wait_ge(s["squared"], 1)
                    for j in range(2):
                        mm = pe.matmul(acc[:, 2 + j, :], g.mean64[:, :], sq[:, j * 512:j * 512 + 512],
                                       start=True, stop=True)
                    mm.then_inc(s["var"], 1)

                @block.vector
                def _(dve):
                    link = chain(dve, s["own"])
                    if gain is not None:
                        link(dve.tensor_copy(par[:, 0:1], g.par[:, ds(i + g.col[gain], 1)]))
                    if bias is not None:
                        link(dve.tensor_copy(par[:, 1:2], g.par[:, ds(i + g.col[bias], 1)]))
                    dve.wait_ge(s["loaded"], 16 * len(loads))
                    if src2 is not None:
                        link(dve.tensor_tensor(x[:, :], x[:, :], ex[:, :], ALU.add))
                    link(dve.tensor_copy(par[:, 0:1], par[:, 0:1] if gain is not None else g.ones[:, 0:1]),
                         s["centred"])
                    if center:
                        dve.wait_ge(s["summed"], 1)
                        link(dve.tensor_tensor(halves(x[:, :]), halves(x[:, :]), acc[:, 0:2, :], ALU.subtract))
                    link(dve.tensor_tensor(sq[:, :], x[:, :], x[:, :], ALU.mult), s["squared"])
                    dve.wait_ge(s["var"], 1)
                    link(dve.tensor_scalar(halves(sq[:, :]), acc[:, 2:4, :], eps, None, ALU.add), s["shifted"])
                    dve.wait_ge(s["rooted"], 1)
                    if gain is not None:
                        link(dve.scalar_tensor_tensor(x[:, :], x[:, :], par[:, 0:1], sq[:, :],
                                                      ALU.mult, ALU.mult))
                    else:
                        link(dve.tensor_tensor(x[:, :], x[:, :], sq[:, :], ALU.mult))
                    if extra is not None:
                        link(dve.scalar_tensor_tensor(x[:, :], x[:, :], par[:, 1:2], ex[:, :],
                                                      ALU.add, ALU.add))
                    dve.wait_ge(s["gate"], 1)
                    link(dve.tensor_tensor(g.y[:, ds(i + y0, 1), 0:SEQ], x[:, None, :], gt[:, None, :],
                                           ALU.mult))

                @block.scalar
                def _(act):
                    act.wait_ge(s["loaded"], 16 * len(loads))
                    act.activation(gt[:, :], gt[:, :], act_gate).then_inc(s["gate"], 1)
                    act.wait_ge(s["shifted"], 1)
                    rsqrt(act, s, sq[:, :], 1)
            clear(nc, s)


W_PAR = 8


def shifted(link, dve, x, d, mu, out, sem=None):
    link(dve.tensor_tensor(d, x[:, 0:SEQ], x[:, 1:SEQ + 1], ALU.subtract))
    link(dve.scalar_tensor_tensor(out, d, mu, x[:, 1:SEQ + 1], ALU.mult, ALU.add), sem)


def rwkv_inputs(nc, g, a, proj, rw, gate, extra):
    with stage(nc, "wp", "const", "zero", "loaded", "shift", "own", "tanh", "sig", "proj", "sw", "sa", "g_out",
               "cum", "ep", "en", "diff", "el", "sqkk", "normed", "root", "prod", "bonus", "extra", "stored") as s:
        x = [s.sb(f"x{n}", [P, 1 + SEQ]) for n in range(3)]
        d, wa, gl = s.sb("d", [P, SEQ]), s.sb("wal", [P, SEQ]), s.sb("gll", [P, SEQ])
        lora = [s.sb(f"lora{n}", [P, P]) for n in range(3)]
        par, reset = s.sb("par", [P, W_PAR]), s.sb("reset", [P, SEQ])
        r, k, av, lw, cum, eP, eN = (s.sb(n, [P, SEQ]) for n in ("r", "k", "a", "lw", "cum", "eP", "eN"))
        acc = s.ps("acc", [P, 8, 512])
        with nc.Block() as block:
            @block.sync
            def _(sp):
                sp.dma_start(reset[:, :], a["reset"]).then_inc(s["const"], 16)
                sp.wait_ge(s["zero"], 3)
                sp.dma_start(x[0][:, 1:], proj[W_WA * P:W_WA * P + P, :]).then_inc(s["loaded"], 16)
                sp.dma_start(x[1][:, 1:], proj[W_GL * P:W_GL * P + P, :]).then_inc(s["loaded"], 16)
                sp.wait_ge(s["const"], 16)

            @block.vector
            def _(dve):
                link = chain(dve, s["own"])
                for n in range(3):
                    link(dve.memset(x[n][:, 0:1], 0.0), s["zero"])
                dve.wait_ge(s["loaded"], 32)
                c = g.col["wmu"]
                shifted(link, dve, x[0], d[:, :], g.par[:, c:c + 1], wa[:, :], s["shift"])
                shifted(link, dve, x[1], d[:, :], g.par[:, c + 1:c + 2], gl[:, :], s["shift"])

            @block.scalar
            def _(act):
                act.wait_ge(s["shift"], 1)
                act.activation(wa[0:64, :], wa[0:64, :], ACT.Tanh).then_inc(s["tanh"], 1)
                act.wait_ge(s["shift"], 2)
                act.activation(gl[:, :], gl[:, :], ACT.Sigmoid).then_inc(s["sig"], 1)
        clear(nc, s)
        with nc.Fori(0, 3) as i:
            with nc.Block() as block:
                @block.sync
                def _(sp):
                    for n, name in enumerate(("w_up", "a_up", "g_up")):
                        sp.dma_start(lora[n][:, :], a[name][ds(i * P, P), :]).then_inc(s["const"], 16)
                    for n, t in enumerate((W_R, W_K, W_V)):
                        sp.dma_start(x[n][:, 1:], proj[ds(i * P + t * P, P), :]).then_inc(s["loaded"], 16)
                    sp.wait_ge(s["g_out"], 1)
                    sp.dma_start(gate[ds(i * P, P), :], av[:, :]).then_inc(s["stored"], 16)
                    sp.wait_ge(s["extra"], 1)
                    sp.dma_start(extra[ds(i * P, P), :], lw[:, :]).then_inc(s["stored"], 16)
                    sp.wait_ge(s["stored"], 32)

                @block.tensor
                def _(pe):
                    pe.wait_ge(s["const"], 48)
                    for n, src in enumerate((wa, wa, gl)):
                        for j in range(2):
                            mm = pe.matmul(acc[:, 2 * n + j, :], lora[n][:, :], src[:, j * 512:j * 512 + 512],
                                           start=True, stop=True)
                        mm.then_inc(s["proj"], 1)
                    for sem in (s["sqkk"], s["prod"]):
                        pe.wait_ge(sem, 1)
                        for j in range(2):
                            mm = pe.matmul(acc[:, 6 + j, :], g.mean64[:, :], d[:, j * 512:j * 512 + 512],
                                           start=True, stop=True)
                        mm.then_inc(s["normed"], 1)

                @block.scalar
                def _(act):
                    act.wait_ge(s["loaded"], 48)
                    act.wait_ge(s["shift"], 1)
                    act.wait_ge(s["proj"], 1)
                    act.activation(halves(lw[:, :]), acc[:, 0:2, :], ACT.Sigmoid, bias=par[:, 3:4]).then_inc(s["sw"], 1)
                    act.wait_ge(s["proj"], 2)
                    act.activation(halves(av[:, :]), acc[:, 2:4, :], ACT.Sigmoid, bias=par[:, 4:5]).then_inc(s["sa"], 1)
                    act.wait_ge(s["cum"], 1)
                    act.activation(eP[:, :], cum[:, :], ACT.Exp).then_inc(s["ep"], 1)
                    act.activation(eN[:, :], cum[:, :], ACT.Exp, scale=-1.0).then_inc(s["en"], 1)
                    act.wait_ge(s["diff"], 1)
                    act.activation(lw[:, :], lw[:, :], ACT.Exp).then_inc(s["el"], 1)
                    act.wait_ge(s["normed"], 1)
                    act.activation(halves(d[:, :]), acc[:, 6:8, :], ACT.Sqrt, scale=64.0).then_inc(s["root"], 1)

                @block.vector
                def _(dve):
                    link = chain(dve, s["own"])
                    at = lambda t: t[:, ds(i, 1), :]
                    one = lambda t: t[:, None, :]
                    link(dve.tensor_copy(par[:, :], g.par[:, ds(i * W_PAR + g.col["w"], W_PAR)]), s["shift"])
                    dve.wait_ge(s["loaded"], 48)
                    shifted(link, dve, x[0], d[:, :], par[:, 0:1], r[:, :])
                    shifted(link, dve, x[1], d[:, :], par[:, 1:2], k[:, :])
                    link(dve.tensor_tensor(d[:, :], x[2][:, 0:SEQ], x[2][:, 1:], ALU.subtract))
                    link(dve.scalar_tensor_tensor(at(rw.arrays["v"]), one(d), par[:, 2:3], x[2][:, None, 1:],
                                                  ALU.mult, ALU.add))
                    dve.wait_ge(s["sw"], 1)
                    link(dve.tensor_scalar(lw[:, :], lw[:, :], -float(np.exp(-0.5)), None, ALU.mult))
                    link(dve.tensor_tensor_scan(cum[:, :], reset[:, :], lw[:, :], 0.0, ALU.mult, ALU.add), s["cum"])
                    link(dve.tensor_tensor(lw[:, :], cum[:, :], lw[:, :], ALU.subtract), s["diff"])
                    kk, k2 = x[0][:, 1:], x[1][:, 1:]
                    link(dve.tensor_scalar(kk, k[:, :], par[:, 5:6], None, ALU.mult))
                    link(dve.tensor_tensor(d[:, :], kk, kk, ALU.mult), s["sqkk"])
                    dve.wait_ge(s["sa"], 1)
                    link(dve.tensor_scalar(k2, av[:, :], -1.0, par[:, 6:7], ALU.add, ALU.mult))
                    link(dve.scalar_tensor_tensor(k2, k2, 1.0, k[:, :], ALU.add, ALU.mult))
                    dve.wait_ge(s["root"], 1)
                    link(dve.tensor_scalar(d[:, :], d[:, :], 1e-12, None, ALU.max))
                    link(dve.reciprocal(d[:, :], d[:, :]))
                    link(dve.tensor_tensor(kk, kk, d[:, :], ALU.mult))
                    dve.wait_ge(s["el"], 1)
                    link(dve.tensor_tensor(at(rw.arrays["alpha"]), x[0][:, None, 1:], one(lw), ALU.mult))
                    link(dve.tensor_tensor(kk, kk, av[:, :], ALU.mult))
                    dve.wait_ge(s["ep"], 1)
                    dve.wait_ge(s["en"], 1)
                    link(dve.scalar_tensor_tensor(at(rw.arrays["beta"]), x[0][:, None, 1:], -1.0, one(eN),
                                                  ALU.mult, ALU.mult))
                    link(dve.tensor_tensor(at(rw.arrays["kappa"]), x[1][:, None, 1:], one(eN), ALU.mult))
                    link(dve.tensor_tensor(at(rw.arrays["rho"]), one(r), one(eP), ALU.mult))
                    link(dve.tensor_copy(rw.last[:, ds(i, 1), :], eP[:, None, CH - 1::CH]))
                    link(dve.scalar_tensor_tensor(d[:, :], r[:, :], par[:, 7:8], k2, ALU.mult, ALU.mult), s["prod"])
                    dve.wait_ge(s["proj"], 3)
                    link(dve.tensor_copy(halves(av[:, :]), acc[:, 4:6, :]), s["g_out"])
                    dve.wait_ge(s["normed"], 2)
                    link(dve.tensor_scalar(halves(lw[:, :]), acc[:, 6:8, :], 64.0, None, ALU.mult))
                    link(dve.tensor_tensor(one(lw), one(lw), at(rw.arrays["v"]), ALU.mult), s["extra"])
            clear(nc, s)


def spread(link, eng, out, src, at, sem):
    link(eng.tensor_copy(out[0:64, :, 0:64], src[0:64, :, ds(at, CH)]), sem)
    link(eng.tensor_copy(out[64:P, :, 64:P], src[64:P, :, ds(at, CH)]), sem)


HEAD = (slice(0, 64), slice(64, P))


def rwkv_chunks(nc, g, a, rw, out):
    N, U = 3, 4
    names = ("al", "be", "ka", "v", "gram", "x_low", "x1", "xt1", "at", "d_t", "b_bd", "c_t", "k_t", "b_t", "v_d",
             "v_t", "bv", "kv", "mk", "y_done", "yp", "x_done", "x_new", "xt_done", "xt_new")
    with stage(nc, "wc", *[f"{n}{u}" for u in range(U) for n in names], "const", "zero", "zero_p", "own", "pown",
               "plc", "rhs", "rhs_s", "z", "z_s", "z_bd", "s_mm", "s_new", "s_bd", "yo", "tok", "stored") as s:
        low, upp = s.sb("low", [P, P]), s.sb("upp", [P, 8, CH])
        units = []
        for u in range(U):
            t = Shared()
            t.s = {n: s[f"{n}{u}"] for n in names}
            t.al, t.be, t.ka, t.v, t.B, t.kT, t.bT, t.Vd, t.X, t.XT, t.yp, t.mk = (
                s.sb(n + str(u), [P, N, P]) for n in ("al", "be", "ka", "v", "B", "kT", "bT", "Vd", "X", "XT",
                                                      "yp", "mk"))
            t.ATc, t.CT, t.DT, t.V, t.BV, t.kV = (
                s.sb(n + str(u), [P, N, CH]) for n in ("ATc", "CT", "DT", "V", "BV", "kV"))
            t.b = [s.ps(f"b{n}_{u}", [P, 512]) for n in range(2)]
            t.wide = lambda n, t=t: t.b[n][:, 0:N * P].rearrange("p (n c) -> p n c", n=N)
            t.half = lambda n, h, t=t: t.b[n][:, h * N * CH:(h + 1) * N * CH].rearrange("p (n c) -> p n c", n=N)
            t.two = lambda n, t=t: t.b[n][:, 0:N * P].rearrange("p (n b c) -> p n b c", n=N, b=2)
            units.append(t)
        rhs, Z, S, SkV = (s.sb(n, [P, N, CH]) for n in ("rhs", "Z", "S", "SkV"))
        Zd, Sd = ([s.sb(n + str(b), [P, N, P]) for b in range(2)] for n in ("Zd", "Sd"))
        plc = s.sb("plc", [P, N, U])
        yT = s.sb("yT", [P, N, U * CH])
        m_ = lambda k: upp[:, k:k + 1, :].broadcast_to([P, N, CH])
        mh = lambda k, r: upp[r, k:k + 1, :].broadcast_to([64, N, CH])
        idb = g.ident[:, None, :].broadcast_to([P, N, P])
        arr = rw.arrays
        every = lambda: enumerate(units)
        with nc.Block() as block:
            @block.sync
            def _(sp):
                for r in HEAD:
                    sp.dma_start(upp[r, :, :], a["upp"].rearrange("p (k c) -> p k c", k=8)[r, :, r])\
                      .then_inc(s["const"], 16)
                sp.dma_start(low[:, :], a["low"][:, 0:P]).then_inc(s["const"], 16)
                sp.wait_ge(s["const"], 48)

            @block.vector
            def _(dve):
                for t in units:
                    for x in (t.al, t.be, t.ka, t.v):
                        dve.memset(x[:, :, :], 0.0).then_inc(s["zero"], 1)
                for x in (S, *Zd):
                    dve.memset(x[:, :, :], 0.0).then_inc(s["zero"], 1)

            @block.gpsimd
            def _(pool):
                for t in units:
                    for x in (t.B, t.XT, t.mk):
                        pool.memset(x[:, :, :], 0.0).then_inc(s["zero_p"], 1)
                for x in Sd:
                    pool.memset(x[:, :, :], 0.0).then_inc(s["zero_p"], 1)
        clear(nc, s)
        with nc.Fori(0, NCH // U) as i:
            at = lambda u: i * (U * CH) + u * CH
            with nc.Block() as block:
                @block.gpsimd
                def _(pool):
                    link = chain(pool, s["pown"])
                    for u, t in every():
                        spread(link, pool, t.ka, arr["kappa"], at(u), t.s["ka"])
                    for u, t in every():
                        spread(link, pool, t.v, arr["v"], at(u), t.s["v"])
                    link(pool.tensor_copy(plc[:, :, :], rw.last[:, :, ds(i * U, U)]), s["plc"])
                    for lev in range(1, 6):
                        for u, t in every():
                            if lev == 1:
                                pool.wait_ge(t.s["at"], 1)
                            else:
                                pool.wait_ge(t.s["y_done"], lev - 1)
                            for r in HEAD:
                                link(pool.tensor_tensor(t.mk[r, :, r], t.ATc[r, :, :], mh(lev, r), ALU.mult),
                                     t.s["mk"])

                @block.tensor
                def _(pe):
                    def each(out, lhsT, rhs_, sem):
                        for p in range(N):
                            mm = pe.matmul(out[:, p], lhsT[:, p, :], rhs_(p), start=True, stop=True)
                        mm.then_inc(sem, 1)

                    def turn(out, x, sem):
                        for p in range(N):
                            mm = pe.transpose(out[:, p, :], x[:, p, :], g.ident[:, :])
                        mm.then_inc(sem, 1)

                    of = lambda x: (lambda p: x[:, p, :])
                    both = lambda u: (lambda p: rw.all[:, 0:2, p, ds(at(u), CH)])
                    for u, t in every():
                        pe.wait_ge(t.s["al"], 2)
                        pe.wait_ge(t.s["be"], 2)
                        each(t.wide(0), t.al, of(t.be), t.s["gram"])
                        each(t.two(1), t.be, both(u), t.s["gram"])
                    for u, t in every():
                        pe.wait_ge(t.s["x_low"], 1)
                        pe.wait_ge(t.s["ka"], 2)
                        each(t.two(0), t.ka, both(u), t.s["gram"])
                        pe.wait_ge(t.s["at"], 1)
                        pe.wait_ge(t.s["d_t"], 1)
                        turn(t.wide(1), t.ka, t.s["gram"])
                    for u, t in every():
                        pe.wait_ge(t.s["b_bd"], 2)
                        pe.wait_ge(t.s["c_t"], 1)
                        turn(t.wide(0), t.be, t.s["gram"])
                        pe.wait_ge(t.s["v"], 2)
                        pe.wait_ge(t.s["k_t"], 1)
                        turn(t.wide(1), t.v, t.s["gram"])
                    for u, t in every():
                        pe.wait_ge(t.s["b_t"], 1)
                        pe.wait_ge(t.s["v_t"], 2)
                        each(t.half(0, 0), t.B, of(t.V), t.s["gram"])
                        each(t.half(1, 0), t.kT, of(t.V), t.s["gram"])
                    for lev in range(1, 6):
                        for u, t in every():
                            pe.wait_ge(t.s["mk"], 2 * lev)
                            if lev == 1:
                                pe.wait_ge(t.s["bv"], 1)
                                pe.wait_ge(t.s["x1"], 1)
                            else:
                                pe.wait_ge(t.s["x_new"], lev - 1)
                                pe.wait_ge(t.s["xt_new"], lev - 1)
                            each(t.wide(0), t.mk, of(t.X), t.s["y_done"])
                        for u, t in every():
                            pe.wait_ge(t.s["yp"], lev)
                            if lev == 1:
                                pe.wait_ge(t.s["kv"], 1)
                                pe.wait_ge(t.s["xt1"], 1)
                            if lev < 5:
                                each(t.wide(1), t.XT, of(t.yp), t.s["x_done"])
                            each(t.wide(0), t.yp, of(t.XT), t.s["xt_done"])

                    def outputs(c):
                        t = units[c]
                        pe.wait_ge(s["z_bd"], 2 * c + 2)
                        if c > 0:
                            pe.wait_ge(s["s_bd"], 2 * c)
                        for p in range(N):
                            o = t.half(1, 1)[:, p, :]
                            pe.matmul(o, t.Vd[:, p, :], t.CT[:, p, :], start=True, stop=False)
                            pe.matmul(o, Sd[c % 2][:, p, :], arr["rho"][:, p, ds(at(c), CH)], start=False, stop=False)
                            mm = pe.matmul(o, Zd[c % 2][:, p, :], t.DT[:, p, :], start=False, stop=True)
                        mm.then_inc(s["yo"], 1)

                    for c, t in every():
                        pe.wait_ge(t.s["xt_new"], 5)
                        if c > 0:
                            pe.wait_ge(s["s_new"], c)
                        each(t.half(0, 0), t.al, of(S), s["rhs"])
                        if c > 0:
                            outputs(c - 1)
                        pe.wait_ge(s["rhs_s"], c + 1)
                        each(t.half(1, 0), t.XT, of(rhs), s["z"])
                        pe.wait_ge(s["z_s"], c + 1)
                        each(t.half(0, 1), t.bT, of(Z), s["s_mm"])
                    outputs(U - 1)

                @block.vector
                def _(dve):
                    link = chain(dve, s["own"])
                    tt = dve.tensor_tensor
                    for u, t in every():
                        for r in HEAD:
                            dve.tensor_copy(t.al[r, :, r], arr["alpha"][r, :, ds(at(u), CH)]).then_inc(t.s["al"], 1)
                    for u, t in every():
                        dve.wait_ge(t.s["gram"], 1)
                        tt(t.X[:, :, :], t.wide(0), low[:, None, :].broadcast_to([P, N, P]), ALU.mult)\
                          .then_inc(t.s["x_low"], 1)
                        dve.wait_ge(t.s["at"], 1)
                        tt(t.DT[:, :, :], t.two(1)[:, :, 1, :], m_(7), ALU.mult).then_inc(t.s["d_t"], 1)
                    for u, t in every():
                        dve.wait_ge(t.s["gram"], 3)
                        for r in HEAD:
                            tt(t.B[r, :, r], t.two(0)[r, :, 0, :], mh(6, r), ALU.mult).then_inc(t.s["b_bd"], 1)
                        tt(t.CT[:, :, :], t.two(0)[:, :, 1, :], m_(7), ALU.mult).then_inc(t.s["c_t"], 1)
                        dve.wait_ge(t.s["x_low"], 1)
                        tt(t.X[:, :, :], t.X[:, :, :], idb, ALU.add).then_inc(t.s["x1"], 1)
                        for r in HEAD:
                            ins = tt(t.XT[r, :, r], t.ATc[r, :, :], mh(0, r), ALU.mult)
                            link(ins)
                        tt(t.XT[:, :, :], t.XT[:, :, :], idb, ALU.add).then_inc(t.s["xt1"], 1)
                    for u, t in every():
                        dve.wait_ge(t.s["gram"], 7)
                        dve.tensor_copy(t.BV[:, :, :], t.half(0, 0)).then_inc(t.s["bv"], 1)
                    for lev in range(1, 6):
                        for u, t in every():
                            dve.wait_ge(t.s["y_done"], lev)
                            if lev > 1:
                                dve.wait_ge(t.s["xt_done"], lev - 1)
                            tt(t.yp[:, :, :], t.wide(0), idb, ALU.add).then_inc(t.s["yp"], 1)
                    dve.wait_ge(s["plc"], 1)
                    for c, t in every():
                        dve.wait_ge(t.s["kv"], 1)
                        dve.wait_ge(t.s["bv"], 1)
                        link(tt(SkV[:, :, :], S[:, :, :], t.kV[:, :, :], ALU.add))
                        dve.wait_ge(s["rhs"], c + 1)
                        tt(rhs[:, :, :], t.half(0, 0), t.BV[:, :, :], ALU.add).then_inc(s["rhs_s"], 1)
                        dve.wait_ge(s["z"], c + 1)
                        if c > 0:
                            dve.wait_ge(s["z_bd"], 2 * c)
                            dve.wait_ge(s["s_bd"], 2 * c)
                        dve.tensor_copy(Z[:, :, :], t.half(1, 0)).then_inc(s["z_s"], 1)
                        dve.wait_ge(s["s_mm"], c + 1)
                        link(tt(S[:, :, :], SkV[:, :, :], t.half(0, 1), ALU.add))
                        link(tt(S[:, :, :], S[:, :, :], plc[:, :, c:c + 1].broadcast_to([P, N, CH]), ALU.mult),
                             s["s_new"])

                @block.scalar
                def _(act):
                    def copy(out, src, sem):
                        act.activation(out, src, ACT.Copy).then_inc(sem, 1)

                    for u, t in every():
                        for r in HEAD:
                            copy(t.be[r, :, r], arr["beta"][r, :, ds(at(u), CH)], t.s["be"])
                    for u, t in every():
                        act.wait_ge(t.s["gram"], 2)
                        copy(t.ATc[:, :, :], t.two(1)[:, :, 0, :], t.s["at"])
                    for u, t in every():
                        act.wait_ge(t.s["gram"], 4)
                        copy(t.kT[:, :, :], t.wide(1), t.s["k_t"])
                    for u, t in every():
                        act.wait_ge(t.s["gram"], 5)
                        copy(t.bT[:, :, :], t.wide(0), t.s["b_t"])
                        act.wait_ge(t.s["gram"], 6)
                        copy(t.Vd[:, :, :], t.wide(1), t.s["v_d"])
                        for r in HEAD:
                            copy(t.V[r, :, :], t.wide(1)[r, :, r], t.s["v_t"])
                    for u, t in every():
                        act.wait_ge(t.s["gram"], 8)
                        copy(t.kV[:, :, :], t.half(1, 0), t.s["kv"])
                    for lev in range(1, 6):
                        for u, t in every():
                            if lev < 5:
                                act.wait_ge(t.s["x_done"], lev)
                                copy(t.X[:, :, :], t.wide(1), t.s["x_new"])
                            act.wait_ge(t.s["xt_done"], lev)
                            copy(t.XT[:, :, :], t.wide(0), t.s["xt_new"])

                    def collect(c):
                        act.wait_ge(s["yo"], c + 1)
                        act.activation(yT[:, :, c * CH:c * CH + CH], units[c].half(1, 1), ACT.Copy)\
                           .then_inc(s["tok"], 1)

                    for c in range(U):
                        act.wait_ge(s["z_s"], c + 1)
                        for r in HEAD:
                            copy(Zd[c % 2][r, :, r], Z[r, :, :], s["z_bd"])
                        if c > 0:
                            collect(c - 1)
                        act.wait_ge(s["s_new"], c + 1)
                        for r in HEAD:
                            copy(Sd[(c + 1) % 2][r, :, r], S[r, :, :], s["s_bd"])
                    collect(U - 1)

                @block.sync
                def _(sp):
                    sp.wait_ge(s["tok"], U)
                    sp.dma_start(out[:, ds(i * (U * CH), U * CH)].rearrange("(k p) t -> p k t", p=P),
                                 yT[:, :, :]).then_inc(s["stored"], 16)
                    sp.wait_ge(s["stored"], 16)
            clear(nc, s)


def block2(nc, g, a, dram):
    proj, y = dram("proj2", (TILES_2 * P, SEQ)), dram("mixed2", (D, SEQ))
    rows, gate, extra = dram("rows2", (12, SEQ)), dram("gate2", (3 * P, SEQ)), dram("extra2", (3 * P, SEQ))
    with g.parts("a2"):
        norm(nc, "n2", g, g.h, [(0, KD)], g.col["g2"], SEQ)
        dense(nc, "in2a", g, a["w_in_2"][:, 0:M_V * P], M_V, SEQ, proj[0:M_V * P, :], conv=(4, 3, "mconv"))
        dense(nc, "in2", g, a["w_in_2"][:, M_V * P:], TILES_2 - M_V, SEQ, proj[M_V * P:, :])
    mlstm_gates(nc, g, proj, rows)
    attention(nc, "ml", g, proj, y, 4, M_Q * P, M_K * P, M_V * P, 0, rows=rows, tri=a["tri"])
    rotate(nc, g, proj, a["cos"], a["sin"], a["swap"])
    attention(nc, "rt", g, proj, y, 6, R_Q * P, R_K * P, R_V * P, 2 * P, ramps=a["ramps"])
    with ExitStack() as ctx:
        rw = Shared()
        rw.all = ctx.enter_context(nc.sbuf_tensor("rw_all", [P, 5, 3, SEQ], F32))
        rw.arrays = {n: rw.all[:, k, :, :] for k, n in enumerate(("alpha", "rho", "beta", "kappa", "v"))}
        rw.last = ctx.enter_context(nc.sbuf_tensor("rw_last", [P, 3, NCH], F32))
        rwkv_inputs(nc, g, a, proj, rw, gate, extra)
        rwkv_chunks(nc, g, a, rw, y[5 * P:8 * P, :])
    with nc.sbuf_tensor("y2", [P, KD, SEQ], F32) as y_sb:
        g.y = y_sb
        head_norm(nc, "hm", g, y, 2, 0, 1e-5, (proj, M_O), ACT.Sigmoid, gain="mln")
        head_norm(nc, "hr", g, y, 3, 2, 1e-5, (proj, R_G), ACT.Silu)
        head_norm(nc, "hw", g, y, 3, 5, 64e-5, (gate, 0), ACT.Copy, gain="wlng", bias="wlnb", extra=extra)
        with g.parts("b2"):
            split_u(nc, "su2", g)
            dense(nc, "out2", g, a["w_out_2"], KD, SEQ)
    with g.parts("c2"):
        norm(nc, "nm2", g, g.h, [(0, KD)], g.col["gm2"], SEQ)
        ffn(nc, "ff2", g, a["w_gu_2"], a["w_down_2"], [(2, 8), (1, 6)], SEQ, gated=True)
    norm(nc, "nf2", g, g.h, [(0, KD)], g.col["gf2"], SEQ, dest="h")


def split_u(nc, name, g):
    with stage(nc, name, "upper", "lower") as s:
        with nc.Block() as block:
            @block.scalar
            def _(act):
                for k in range(KD):
                    act.activation(g.uhi[:, k, 0:SEQ], g.y[:, k, 0:SEQ], ACT.Copy).then_inc(s["upper"], 1)

            @block.vector
            def _(dve):
                for k in range(KD):
                    dve.wait_ge(s["upper"], k + 1)
                    dve.tensor_tensor(g.ulo[:, k, 0:SEQ], g.y[:, k, 0:SEQ], g.uhi[:, k, 0:SEQ].bitcast(F32),
                                      ALU.subtract).then_inc(s["lower"], 1)


def unit_heads(nc, name, g, proj, row0, out, scale):
    with stage(nc, name, "loaded", "squared", "summed", "shifted", "logged", "rooted", "own") as s:
        x, sq = s.sb("x", [P, SEQ]), s.sb("sq", [P, SEQ])
        acc = s.ps("acc", [P, 2, 512])
        with nc.Fori(0, 4) as i:
            with nc.Block() as block:
                @block.sync
                def _(sp):
                    sp.dma_start(x[:, :], proj[ds(i * P + row0, P), :]).then_inc(s["loaded"], 16)

                @block.scalar
                def _(act):
                    act.wait_ge(s["loaded"], 16)
                    act.activation(sq[:, :], x[:, :], ACT.Square).then_inc(s["squared"], 1)
                    act.wait_ge(s["shifted"], 1)
                    rsqrt(act, s, sq[:, :], 1)

                @block.tensor
                def _(pe):
                    pe.wait_ge(s["squared"], 1)
                    for j in range(2):
                        mm = pe.matmul(acc[:, j, :], g.mean64[:, :], sq[:, j * 512:j * 512 + 512],
                                       start=True, stop=True)
                    mm.then_inc(s["summed"], 1)

                @block.vector
                def _(dve):
                    link = chain(dve, s["own"])
                    dve.wait_ge(s["summed"], 1)
                    link(dve.tensor_scalar(halves(sq[:, :]), acc[:, :, :], 64.0, EPS, ALU.mult, ALU.add), s["shifted"])
                    dve.wait_ge(s["rooted"], 1)
                    link(dve.scalar_tensor_tensor(out[:, ds(i, 1), :], x[:, None, :], scale, sq[:, None, :],
                                                  ALU.mult, ALU.mult))
            clear(nc, s)


GK = 6


def gdn_gates(nc, g, proj, gd):
    with stage(nc, "gg", "loaded", "own", "abs", "power", "log", "alog", "sig", "decay", "turned", "tok", "sum", "end",
               "exps", "arg") as s:
        x, l = s.sb("x", [48, SEQ]), s.sb("l", [16, SEQ])
        ea = s.sb("ea", [16, 1])
        low, upp = s.sb("low", [P, P]), s.sb("upp", [P, P])
        tok = s.sb("tok", [P, NCH, 24])
        turned = s.ps("turned", [P, 2, 8, 64])
        acc = s.ps("acc", [P, 2, 512])
        c = g.col["gates3"]
        sums = lambda d: acc[:, d, 0:NCH * 4].rearrange("p (c h) -> p c h", h=4)
        ends = lambda d: acc[:, d, 64:64 + NCH * 4].rearrange("p (c h) -> p c h", h=4)
        with nc.Block() as block:
            @block.sync
            def _(sp):
                sp.dma_start(x[:, :], proj[G_GATE * P:G_GATE * P + 48, :]).then_inc(s["loaded"], 16)
                sp.dma_start(low[:, :], gd.a["low"][:, 7 * P:8 * P]).then_inc(s["loaded"], 16)
                sp.dma_start(upp[:, :], gd.a["upp"][:, 7 * P:8 * P]).then_inc(s["loaded"], 16)

            @block.scalar
            def _(act):
                act.wait_ge(s["loaded"], 48)
                dt = g.par[0:16, c:c + 1]
                act.activation(l[:, :], x[0:16, :], ACT.Abs, bias=dt).then_inc(s["abs"], 1)
                act.activation(ea[:, :], g.par[0:16, c + 1:c + 2], ACT.Exp).then_inc(s["alog"], 1)
                act.wait_ge(s["abs"], 1)
                act.activation(l[:, :], l[:, :], ACT.Exp, scale=-1.0).then_inc(s["power"], 1)
                act.wait_ge(s["power"], 1)
                act.activation(l[:, :], l[:, :], ACT.Ln, bias=1.0).then_inc(s["log"], 1)
                act.activation(x[32:48, :], x[32:48, :], ACT.Sigmoid).then_inc(s["sig"], 1)
                for d in range(2):
                    act.wait_ge(s["arg"], d + 1)
                    for n in (1, 2, 3):
                        act.activation(gd.sc[:, d, :, n, :], gd.sc[:, d, :, n, :], ACT.Exp).then_inc(s["exps"], 1)

            @block.vector
            def _(dve):
                link = chain(dve, s["own"])
                dve.wait_ge(s["loaded"], 48)
                dve.wait_ge(s["abs"], 1)
                link(dve.tensor_scalar(x[0:16, :], x[0:16, :], g.par[0:16, c:c + 1], 0.0, ALU.add, ALU.max))
                dve.wait_ge(s["log"], 1)
                link(dve.tensor_tensor(x[0:16, :], x[0:16, :], l[:, :], ALU.add))
                dve.wait_ge(s["alog"], 1)
                link(dve.tensor_scalar(x[0:16, :], x[0:16, :], ea[:, 0:1], -1.0, ALU.mult, ALU.mult), s["decay"])
                dve.wait_ge(s["turned"], 1)
                for hh in range(2):
                    for b in range(2):
                        link(dve.tensor_copy(tok[64 * hh:64 * hh + 64, 8 * b:8 * b + 8, :],
                                             turned[0:64, b, :, hh:48:2]), s["tok"])
                dve.wait_ge(s["sum"], 1)
                for d in range(2):
                    sc = gd.sc[:, d, :, :, :]
                    link(dve.tensor_copy(sc[:, :, 0, :], sums(d)))
                    link(dve.tensor_copy(sc[:, :, 1, :], sums(d)))
                    link(dve.scalar_tensor_tensor(sc[:, :, 2, :], ends(d), 64.0, sc[:, :, 0, :],
                                                  ALU.mult, ALU.subtract))
                    link(dve.tensor_scalar(sc[:, :, 3, :], ends(d), 64.0, None, ALU.mult), s["arg"])
                    beta = tok[:, :, 16 + 4 * d:20 + 4 * d]
                    link(dve.tensor_scalar(sc[:, :, 4, :], beta, -1.0, None, ALU.mult))
                    link(dve.tensor_copy(sc[:, :, 5, :], beta))
                for d in range(2):
                    sc = gd.sc[:, d, :, :, :]
                    dve.wait_ge(s["exps"], 3 * d + 3)
                    link(dve.tensor_tensor(sc[:, :, 1, :], sc[:, :, 1, :], sc[:, :, 4, :], ALU.mult))

            @block.tensor
            def _(pe):
                pe.wait_ge(s["decay"], 1)
                pe.wait_ge(s["sig"], 1)
                for n in range(NCH):
                    mm = pe.transpose(turned[0:64, n // 8, n % 8, 0:48], x[:, n * CH:n * CH + CH],
                                      g.ident[0:48, 0:48])
                mm.then_inc(s["turned"], 1)
                pe.wait_ge(s["tok"], 4)
                for d, mask in enumerate((upp, low)):
                    for c4 in range(NCH):
                        r = tok[:, c4, 4 * d:4 * d + 4]
                        pe.matmul(acc[:, d, 4 * c4:4 * c4 + 4], mask[:, :], r, start=True, stop=True)
                        mm = pe.matmul(acc[:, d, 64 + 4 * c4:68 + 4 * c4], g.mean64[:, :], r, start=True, stop=True)
                mm.then_inc(s["sum"], 1)


def gdn_chunks(nc, g, gd, out):
    N, K2 = 4, 2
    names = ("sc", "kbd", "vs", "dg", "db", "rows", "dots", "turn", "x0", "eq", "diff", "ramp", "at", "em", "c_t",
             "xt1", "k_t", "v_t", "vb", "q_g", "mk", "y_done", "yp", "x_done", "x_new", "xt_done", "xt_new", "ks",
             "rhs", "vn", "vd", "vn_d", "up", "oo", "o")
    with stage(nc, "gc", *[f"{n}{u}" for u in range(2 * K2) for n in names], "const", "zero", "zero_p", "own",
               "pown", "s_new0", "s_new1", "s_bd0", "s_bd1", "stored") as s:
        low, upp = s.sb("low", [P, 7, CH]), s.sb("upp", [P, 7, CH])
        idc, ones64 = s.sb("idc", [P, CH]), s.sb("ones64", [P, P])
        dirs, units = [], []
        for d in range(2):
            t = Shared()
            t.S, t.SE, t.Sd = s.sb(f"S{d}", [P, N, CH]), s.sb(f"SE{d}", [P, N, CH]), s.sb(f"Sd{d}", [P, N, P])
            t.stg = s.sb(f"stg{d}", [P, N, K2 * CH])
            t.new, t.bd = s[f"s_new{d}"], s[f"s_bd{d}"]
            t.mT = (upp, low)[d]
            dirs.append(t)
        for u in range(2 * K2):
            t = Shared()
            t.k, t.d = u // 2, u % 2
            t.dir = dirs[t.d]
            t.s = {n: s[f"{n}{u}"] for n in names}
            t.kbd, t.kT, t.X, t.XT, t.yp, t.mk = (
                s.sb(n + str(u), [P, N, P]) for n in ("kbd", "kT", "X", "XT", "yp", "mk"))
            t.dg, t.db, t.E, t.ATc, t.CT, t.eq, t.V = (
                s.sb(n + str(u), [P, N, CH]) for n in ("dg", "db", "E", "ATc", "CT", "eq", "V"))
            t.rhs, t.vd, t.Vnd = t.dg, t.db, t.yp
            t.sc = s.sb(f"sc{u}", [P, GK, N])
            t.b = [s.ps(f"b{n}_{u}", [P, 512]) for n in range(2)]
            t.wide = lambda n, t=t: t.b[n][:, :].rearrange("p (n c) -> p n c", n=N)
            t.half = lambda n, h, t=t: t.b[n][:, 256 * h:256 * h + 256].rearrange("p (n c) -> p n c", n=N)
            t.two = lambda n, t=t: t.b[n][:, :].rearrange("p (n b c) -> p n b c", n=N, b=2)
            t.m = lambda k, t=t: t.dir.mT[:, k:k + 1, :].broadcast_to([P, N, CH])
            t.mh = lambda k, r, t=t: t.dir.mT[r, k:k + 1, :].broadcast_to([64, N, CH])
            t.f = lambda n, t=t: t.sc[:, n, :].unsqueeze(2).broadcast_to([P, N, CH])
            units.append(t)
        idn = idc[:, None, :].broadcast_to([P, N, CH])
        idb = g.ident[:, None, :].broadcast_to([P, N, P])
        with nc.Block() as block:
            @block.sync
            def _(sp):
                for r in HEAD:
                    for t, n in ((low, "low"), (upp, "upp")):
                        src = gd.a[n].rearrange("p (k c) -> p k c", k=8)
                        sp.dma_start(t[r, 0:6, :], src[r, 0:6, r]).then_inc(s["const"], 16)
                        sp.dma_start(t[r, 6:7, :], src[r, 7:8, r]).then_inc(s["const"], 16)
                    sp.dma_start(idc[r, :], gd.a["ident"][r, r]).then_inc(s["const"], 16)
                sp.wait_ge(s["const"], 160)

            @block.vector
            def _(dve):
                dve.tensor_scalar(ones64[:, :], g.mean64[:, :], 64.0, None, ALU.mult).then_inc(s["zero"], 1)
                for t in units:
                    dve.memset(t.kbd[:, :, :], 0.0).then_inc(s["zero"], 1)
                for t in dirs:
                    dve.memset(t.S[:, :, :], 0.0).then_inc(s["zero"], 1)

            @block.gpsimd
            def _(pool):
                for t in units:
                    for x in (t.XT, t.mk):
                        pool.memset(x[:, :, :], 0.0).then_inc(s["zero_p"], 1)
                for t in dirs:
                    pool.memset(t.Sd[:, :, :], 0.0).then_inc(s["zero_p"], 1)
        clear(nc, s)
        with nc.Fori(0, NCH // K2) as i:
            chunk = lambda t: i * K2 + t.k if t.d == 0 else i * (-K2) + (NCH - 1 - t.k)
            at = lambda t: i * (K2 * CH) + t.k * CH if t.d == 0 else i * (-K2 * CH) + (NCH - 1 - t.k) * CH
            with nc.Block() as block:
                @block.gpsimd
                def _(pool):
                    link = chain(pool, s["pown"])
                    tt = pool.tensor_tensor
                    for t in units:
                        link(pool.tensor_copy(t.sc[:, :, :], gd.sc[:, t.d, ds(chunk(t), 1), :, :]
                                              .rearrange("p a k n -> p (a k) n")), t.s["sc"])
                    for t in units:
                        link(tt(t.dg[:, :, :], idn, t.f(0), ALU.mult), t.s["dg"])
                    for t in units:
                        pool.wait_ge(t.s["ramp"], 1)
                        link(tt(t.CT[:, :, :], t.E[:, :, :], t.m(6), ALU.mult), t.s["em"])
                    for lev in range(1, 6):
                        for t in units:
                            if lev == 1:
                                pool.wait_ge(t.s["at"], 1)
                            else:
                                pool.wait_ge(t.s["y_done"], lev - 1)
                            for r in HEAD:
                                link(tt(t.mk[r, :, r], t.ATc[r, :, :], t.mh(lev, r), ALU.mult), t.s["mk"])
                        if lev == 1:
                            for t in units:
                                pool.wait_ge(t.s["eq"], 1)
                                link(tt(t.eq[:, :, :], t.eq[:, :, :], gd.q[:, :, ds(at(t), CH)], ALU.mult),
                                     t.s["q_g"])
                                pool.wait_ge(t.s["v_t"], 2)
                                link(tt(t.V[:, :, :], t.V[:, :, :], t.f(5), ALU.mult), t.s["vb"])

                @block.tensor
                def _(pe):
                    def each(out, lhsT, rhs_, sem):
                        for p in range(N):
                            mm = pe.matmul(out[:, p], lhsT[:, p, :], rhs_(p), start=True, stop=True)
                        mm.then_inc(sem, 1)

                    def turn(out, x, sem):
                        for p in range(N):
                            mm = pe.transpose(out[:, p, :], x[:, p, :], g.ident[:, :])
                        mm.then_inc(sem, 1)

                    of = lambda x: (lambda p: x[:, p, :])
                    for t in units:
                        pe.wait_ge(t.s["kbd"], 2)
                        each(t.two(1), t.kbd, lambda p: gd.all[:, 0:2, p, ds(at(t), CH)], t.s["dots"])
                        pe.wait_ge(t.s["dg"], 1)
                        pe.wait_ge(t.s["db"], 1)
                        pe.matmul(t.half(0, 0), ones64[:, :], t.dg[:, :, :], start=True, stop=True)
                        pe.matmul(t.half(0, 1), ones64[:, :], t.db[:, :, :], start=True, stop=True)\
                          .then_inc(t.s["rows"], 1)
                    for t in units:
                        pe.wait_ge(t.s["eq"], 1)
                        pe.wait_ge(t.s["at"], 1)
                        turn(t.wide(0), t.kbd, t.s["turn"])
                        pe.wait_ge(t.s["c_t"], 1)
                        pe.wait_ge(t.s["vs"], 1)
                        turn(t.wide(1)[0:64], t.V, t.s["turn"])
                    for t in units:
                        pe.wait_ge(t.s["k_t"], 1)
                        pe.wait_ge(t.s["xt1"], 1)
                        turn(t.wide(0), t.XT, t.s["x0"])
                    for lev in range(1, 6):
                        for t in units:
                            pe.wait_ge(t.s["mk"], 2 * lev)
                            pe.wait_ge(t.s["x_new"], lev)
                            if lev > 1:
                                pe.wait_ge(t.s["xt_new"], lev - 1)
                            each(t.wide(0), t.mk, of(t.X), t.s["y_done"])
                        for t in units:
                            pe.wait_ge(t.s["yp"], lev)
                            if lev == 1:
                                pe.wait_ge(t.s["v_t"], 2)
                            if lev < 5:
                                each(t.wide(1), t.XT, of(t.yp), t.s["x_done"])
                            each(t.wide(0), t.yp, of(t.XT), t.s["xt_done"])
                    for k in range(K2):
                        now = units[2 * k:2 * k + 2]
                        for t in now:
                            pe.wait_ge(t.s["xt_new"], 5)
                            if k > 0:
                                pe.wait_ge(t.dir.new, k)
                            each(t.half(0, 0), t.kbd, of(t.dir.S), t.s["ks"])
                        for t in now:
                            pe.wait_ge(t.s["rhs"], 1)
                            each(t.half(1, 0), t.XT, of(t.rhs), t.s["vn"])
                        for t in now:
                            pe.wait_ge(t.s["vd"], 1)
                            each(t.half(0, 1), t.kT, of(t.vd), t.s["up"])
                        for t in now:
                            pe.wait_ge(t.s["vn_d"], 2)
                            pe.wait_ge(t.s["q_g"], 1)
                            if k > 0:
                                pe.wait_ge(t.dir.bd, 2 * k)
                            for p in range(N):
                                o = t.half(1, 1)[:, p, :]
                                pe.matmul(o, t.dir.Sd[:, p, :], t.eq[:, p, :], start=True, stop=False)
                                mm = pe.matmul(o, t.Vnd[:, p, :], t.CT[:, p, :], start=False, stop=True)
                            mm.then_inc(t.s["oo"], 1)

                @block.vector
                def _(dve):
                    link = chain(dve, s["own"])
                    tt = dve.tensor_tensor
                    for t in units:
                        dve.wait_ge(t.s["sc"], 1)
                        tt(t.db[:, :, :], idn, t.f(4), ALU.mult).then_inc(t.s["db"], 1)
                    for t in units:
                        dve.wait_ge(t.s["eq"], 1)
                        link(tt(t.E[:, :, :], t.half(0, 0), t.f(0), ALU.subtract))
                        dve.tensor_scalar(t.E[:, :, :], t.E[:, :, :], 0.0, None, ALU.min).then_inc(t.s["diff"], 1)
                    for t in units:
                        dve.wait_ge(t.s["dots"], 1)
                        dve.wait_ge(t.s["ramp"], 1)
                        link(tt(t.ATc[:, :, :], t.two(1)[:, :, 0, :], t.E[:, :, :], ALU.mult))
                        link(tt(t.ATc[:, :, :], t.half(0, 1), t.ATc[:, :, :], ALU.mult), t.s["at"])
                        for r in HEAD:
                            link(tt(t.XT[r, :, r], t.ATc[r, :, :], t.mh(0, r), ALU.mult))
                        tt(t.XT[:, :, :], t.XT[:, :, :], idb, ALU.add).then_inc(t.s["xt1"], 1)
                        dve.wait_ge(t.s["em"], 1)
                        tt(t.CT[:, :, :], t.two(1)[:, :, 1, :], t.CT[:, :, :], ALU.mult).then_inc(t.s["c_t"], 1)
                    for lev in range(1, 6):
                        for t in units:
                            dve.wait_ge(t.s["y_done"], lev)
                            if lev > 1:
                                dve.wait_ge(t.s["xt_done"], lev - 1)
                            tt(t.yp[:, :, :], t.wide(0), idb, ALU.add).then_inc(t.s["yp"], 1)
                    for k in range(K2):
                        now = units[2 * k:2 * k + 2]
                        for t in now:
                            link(tt(t.dir.SE[:, :, :], t.dir.S[:, :, :], t.f(3), ALU.mult))
                        for t in now:
                            dve.wait_ge(t.s["ks"], 1)
                            dve.wait_ge(t.s["vb"], 1)
                            link(tt(t.rhs[:, :, :], t.half(0, 0), t.f(1), ALU.mult))
                            tt(t.rhs[:, :, :], t.rhs[:, :, :], t.V[:, :, :], ALU.add).then_inc(t.s["rhs"], 1)
                        for t in now:
                            dve.wait_ge(t.s["vn"], 1)
                            tt(t.vd[:, :, :], t.half(1, 0), t.f(2), ALU.mult).then_inc(t.s["vd"], 1)
                        for t in now:
                            dve.wait_ge(t.s["up"], 1)
                            if k > 0:
                                dve.wait_ge(t.dir.bd, 2 * k)
                            link(tt(t.dir.S[:, :, :], t.dir.SE[:, :, :], t.half(0, 1), ALU.add), t.dir.new)

                @block.scalar
                def _(act):
                    def copy(out, src, sem):
                        act.activation(out, src, ACT.Copy).then_inc(sem, 1)

                    for t in units:
                        for r in HEAD:
                            copy(t.kbd[r, :, r], gd.k[r, :, ds(at(t), CH)], t.s["kbd"])
                    for t in units:
                        act.wait_ge(t.s["rows"], 1)
                        act.activation(t.eq[:, :, :], t.half(0, 0), ACT.Exp).then_inc(t.s["eq"], 1)
                    for t in units:
                        act.wait_ge(t.s["diff"], 1)
                        act.activation(t.E[:, :, :], t.E[:, :, :], ACT.Exp).then_inc(t.s["ramp"], 1)
                    for t in units:
                        copy(t.V[:, :, :], gd.v[:, :, ds(at(t), CH)], t.s["vs"])
                    for t in units:
                        act.wait_ge(t.s["turn"], 1)
                        copy(t.kT[:, :, :], t.wide(0), t.s["k_t"])
                        act.wait_ge(t.s["turn"], 2)
                        for r in HEAD:
                            copy(t.V[r, :, :], t.wide(1)[0:64, :, r], t.s["v_t"])
                    for t in units:
                        act.wait_ge(t.s["x0"], 1)
                        copy(t.X[:, :, :], t.wide(0), t.s["x_new"])
                    for lev in range(1, 6):
                        for t in units:
                            if lev < 5:
                                act.wait_ge(t.s["x_done"], lev)
                                copy(t.X[:, :, :], t.wide(1), t.s["x_new"])
                            act.wait_ge(t.s["xt_done"], lev)
                            copy(t.XT[:, :, :], t.wide(0), t.s["xt_new"])
                    for k in range(K2):
                        now = units[2 * k:2 * k + 2]
                        for t in now:
                            act.wait_ge(t.s["vd"], 1)
                            for r in HEAD:
                                copy(t.Vnd[r, :, r], t.half(1, 0)[r, :, :], t.s["vn_d"])
                        for t in now:
                            act.wait_ge(t.s["oo"], 1)
                            here = t.k * CH if t.d == 0 else (K2 - 1 - t.k) * CH
                            copy(t.dir.stg[:, :, here:here + CH], t.half(1, 1), t.s["o"])
                            act.wait_ge(t.dir.new, k + 1)
                            for r in HEAD:
                                copy(t.dir.Sd[r, :, r], t.dir.S[r, :, :], t.dir.bd)

                @block.sync
                def _(sp):
                    first = (i * (K2 * CH), i * (-K2 * CH) + (NCH - K2) * CH)
                    for d in range(2):
                        for t in units[d::2]:
                            sp.wait_ge(t.s["o"], 1)
                        sp.dma_start(out[d][:, ds(first[d], K2 * CH)].rearrange("(k p) t -> p k t", p=P),
                                     dirs[d].stg[:, :, :]).then_inc(s["stored"], 16)
                    sp.wait_ge(s["stored"], 32)
            clear(nc, s)


def spatial(nc, g, a, proj):
    with stage(nc, "sg", "loaded", "gelu", "own", "par", "squared", "summed", "shifted", "logged", "rooted", "normed",
               "turned", "tok", "mixed", "sq2", "y") as s:
        u, v, sq = s.sb("u", [P, SEQ]), s.sb("v", [P, SEQ]), s.sb("sq", [P, SEQ])
        wT, bias = s.sb("wT", [P, P]), s.sb("bias", [P, P])
        vt = s.sb("vt", [P, 8, P])
        par = s.sb("par", [P, 2])
        acc = s.ps("acc", [P, 2, 512])
        turned, mixed = s.ps("turned", [P, 8, P]), s.ps("mixed", [P, 8, P])
        with nc.Fori(0, 4) as i:
            with nc.Block() as block:
                @block.sync
                def _(sp):
                    sp.dma_start(u[:, :], proj[ds(i * P + G_SU * P, P), :]).then_inc(s["loaded"], 16)
                    sp.dma_start(v[:, :], proj[ds(i * P + G_SV * P, P), :]).then_inc(s["loaded"], 16)
                    sp.dma_start(wT[:, :], a["sgu_wt"][ds(i * P, P), :]).then_inc(s["loaded"], 16)
                    sp.dma_start(bias[:, :], a["sgu_b"][ds(i, 1), :].broadcast_to([P, P])).then_inc(s["loaded"], 16)

                @block.scalar
                def _(act):
                    act.wait_ge(s["loaded"], 64)
                    act.activation(v[:, :], v[:, :], ACT.Gelu).then_inc(s["gelu"], 1)
                    act.activation(u[:, :], u[:, :], ACT.Gelu).then_inc(s["gelu"], 1)
                    for n in range(2):
                        act.wait_ge(s["shifted"], n + 1)
                        rsqrt(act, s, sq[:, :], n + 1)

                @block.tensor
                def _(pe):
                    def total(sem):
                        pe.wait_ge(sem, 1)
                        for j in range(2):
                            mm = pe.matmul(acc[:, j, :], g.ones[:, :], sq[:, j * 512:j * 512 + 512],
                                           start=True, stop=True)
                        mm.then_inc(s["summed"], 1)

                    total(s["squared"])
                    pe.wait_ge(s["normed"], 1)
                    for c in range(8):
                        mm = pe.transpose(turned[:, c, :], v[:, c * P:(c + 1) * P], g.ident[:, :])
                    mm.then_inc(s["turned"], 1)
                    pe.wait_ge(s["tok"], 2)
                    for c in range(8):
                        mm = pe.matmul(mixed[:, c, :], vt[:, c, :], wT[:, :], start=True, stop=True)
                    mm.then_inc(s["mixed"], 1)
                    total(s["sq2"])

                @block.vector
                def _(dve):
                    link = chain(dve, s["own"])
                    link(dve.tensor_copy(par[:, 0:1], g.par[:, ds(i + g.col["sgv"], 1)]))
                    link(dve.tensor_copy(par[:, 1:2], g.par[:, ds(i + g.col["sgo"], 1)]))

                    def inverse(n):
                        dve.wait_ge(s["summed"], n)
                        link(dve.tensor_scalar(halves(sq[:, :]), acc[:, :, :], 1.0 / P, EPS, ALU.mult, ALU.add),
                             s["shifted"])
                        dve.wait_ge(s["rooted"], n)

                    dve.wait_ge(s["gelu"], 1)
                    link(dve.tensor_tensor(sq[:, :], v[:, :], v[:, :], ALU.mult), s["squared"])
                    inverse(1)
                    link(dve.scalar_tensor_tensor(v[:, :], v[:, :], par[:, 0:1], sq[:, :], ALU.mult, ALU.mult),
                         s["normed"])
                    dve.wait_ge(s["turned"], 1)
                    for n in range(2):
                        link(dve.tensor_copy(vt[:, 4 * n:4 * n + 4, :], turned[:, 4 * n:4 * n + 4, :]), s["tok"])
                    dve.wait_ge(s["mixed"], 1)
                    dve.wait_ge(s["loaded"], 64)
                    v8 = v[:, :].rearrange("p (c t) -> p c t", c=8)
                    for n in range(2):
                        link(dve.tensor_tensor(v8[:, 4 * n:4 * n + 4, :], mixed[:, 4 * n:4 * n + 4, :],
                                               bias[:, None, :].broadcast_to([P, 4, P]), ALU.add))
                    dve.wait_ge(s["gelu"], 2)
                    link(dve.tensor_tensor(v[:, :], v[:, :], u[:, :], ALU.mult))
                    link(dve.tensor_tensor(sq[:, :], v[:, :], v[:, :], ALU.mult), s["sq2"])
                    inverse(2)
                    link(dve.scalar_tensor_tensor(g.y[:, ds(i + 4, 1), :], v[:, None, :], par[:, 1:2],
                                                  sq[:, None, :], ALU.mult, ALU.mult))
            clear(nc, s)


def block3(nc, g, a, dram, out):
    proj = dram("proj3", (TILES_3 * P, SEQ))
    o_dram = [dram(f"o3_{d}", (4 * P, SEQ)) for d in range(2)]
    with g.parts("a3"):
        norm(nc, "n3", g, g.h, [(0, KD)], g.col["g3"], SEQ)
        dense(nc, "in3a", g, a["w_in_3"][:, 0:G_Z * P], G_Z, SEQ, proj[0:G_Z * P, :], conv=(5, 2, "gconv"))
        dense(nc, "in3", g, a["w_in_3"][:, G_Z * P:], TILES_3 - G_Z, SEQ, proj[G_Z * P:, :])
    with ExitStack() as ctx:
        sb = lambda n, shape: ctx.enter_context(nc.sbuf_tensor(n, shape, F32))
        gd = Shared()
        gd.a = a
        gd.all = sb("gd_all", [P, 3, 4, SEQ])
        gd.k, gd.q, gd.v = (gd.all[:, n, :, :] for n in range(3))
        gd.sc = sb("gd_sc", [P, 2, NCH, GK, 4])
        unit_heads(nc, "uq", g, proj, G_Q * P, gd.q, 0.125)
        unit_heads(nc, "uk", g, proj, G_K * P, gd.k, 1.0)
        gdn_gates(nc, g, proj, gd)
        with stage(nc, "gv", "loaded") as s:
            with nc.Block() as block:
                @block.sync
                def _(sp):
                    sp.dma_start(gd.v[:, :, :], proj[G_V * P:G_Z * P, :].rearrange("(k p) t -> p k t", p=P))\
                      .then_inc(s["loaded"], 16)
                    sp.wait_ge(s["loaded"], 16)
        gdn_chunks(nc, g, gd, o_dram)
    with nc.sbuf_tensor("y3", [P, KD, SEQ], F32) as y_sb:
        g.y = y_sb
        head_norm(nc, "hg", g, o_dram[0], 4, 0, EPS, (proj, G_Z), ACT.Silu, center=False, gain="gdng",
                  src2=o_dram[1])
        spatial(nc, g, a, proj)
        with g.parts("b3"):
            split_u(nc, "su3", g)
            dense(nc, "out3", g, a["w_out_3"], KD, SEQ)
    with g.parts("c3"):
        norm(nc, "nm3", g, g.h, [(0, KD)], g.col["gm3"], SEQ)
        ffn(nc, "ff3", g, a["w_ff1_3"], a["w_ff2_3"], [(4, KD)], SEQ, gated=False)
    norm(nc, "nf3", g, g.h, [(0, KD)], g.col["gf3"], SEQ, dest=out)


def cols(v):
    v = v.reshape(-1, v.shape[-1])
    K, C = v.shape
    return np.ascontiguousarray(v.reshape(K, C // P, P).transpose(2, 1, 0)).reshape(P, -1)


def block_diagonal(w):
    out = np.zeros((w.shape[0] // 2, P, P), w.dtype)
    out[:, 0:64, 0:64] = w[0::2]
    out[:, 64:, 64:] = w[1::2]
    return out.reshape(-1, P)


def layout(x):
    par, col = [], {}

    def put(name, block):
        col[name] = sum(b.shape[1] for b in par)
        par.append(block)

    z1 = lambda n: np.zeros((P, n), np.float32)
    put("g1", cols(x["norm_mix_g"][0]))
    put("lru", np.concatenate([np.concatenate(
        [cols(x["lru_conv_w"][0][:, t * P:(t + 1) * P])] +
        [cols(x[k][0][t * P:(t + 1) * P]) for k in ("lru_conv_b", "lru_gate_a_b", "lru_gate_x_b", "lru_a_param")] +
        [z1(LRU_PAR - 8)], 1) for t in range(4)], 1))
    put("cc", np.concatenate([np.concatenate(
        [cols(x["cc_conv_w"][0][:, t * P:(t + 1) * P]), cols(x["cc_conv_b"][0][t * P:(t + 1) * P])], 1)
        for t in range(4)], 1))
    put("ccg", cols(x["cc_ln_g"][0]))
    put("ccb", cols(x["cc_ln_b"][0]))
    put("go1", np.concatenate([cols(x["out_norm_lru_g"][0]), cols(x["out_norm_cc_g"][0])], 1))
    put("gm1", cols(x["norm_mlp_g"][0]))
    put("gf1", cols(x["norm_final_g"]))
    a = {
        "h0": np.ascontiguousarray(np.concatenate([x["meta_tokens"], x["x"][0]], 0).T),
        "w_in": x["w_in"][0], "w_out": x["w_out"][0], "w_mlp_up": x["w_mlp_up"][0], "w_mlp_down": x["w_mlp_down"][0],
        "lru_wa": block_diagonal(x["lru_gate_a_w"][0]), "lru_wx": block_diagonal(x["lru_gate_x_w"][0]),
    }
    layout2(x, a, put)
    layout3(x, a, put)
    a["par"] = np.ascontiguousarray(np.concatenate(par, 1))
    return a, col


def tiles_of(w, *spans):
    out = []
    for lo, hi in spans:
        out.append(w[:, lo:hi])
        if (hi - lo) % P:
            out.append(np.zeros((w.shape[0], -(hi - lo) % P), w.dtype))
    return np.concatenate(out, 1)


def level_masks():
    t, s_ = np.meshgrid(np.arange(P), np.arange(P), indexing="ij")
    same = t // CH == s_ // CH
    m = [same & (t >> (k + 1) == s_ >> (k + 1)) & ((t >> k) & 1 == 1) & ((s_ >> k) & 1 == 0) for k in range(6)]
    m += [same & (s_ < t), same & (s_ <= t)]
    low = np.stack(m, 1).astype(np.float32)
    return low.reshape(P, -1), np.ascontiguousarray(low.transpose(2, 1, 0)).reshape(P, -1)


def layout2(x, a, put):
    w = x["w_in_2"][0]
    m, r = 1032, 1032 + 1536
    a["w_in_2"] = tiles_of(w, (0, 1024), (m, m + 1536), (r, r + 1408), (1024, 1032))
    a["w_gu_2"] = np.stack([x["w_gate_2"][0].reshape(D, -1, P), x["w_up_2"][0].reshape(D, -1, P)], 2).reshape(D, -1)
    a["w_out_2"], a["w_down_2"] = x["w_out_2"][0], x["w_down_2"][0]
    put("g2", cols(x["ln1_g_2"][0]))
    put("gm2", cols(x["ln2_g_2"][0]))
    put("gf2", cols(x["lnf_g_2"]))
    put("mconv", cols(x["m_conv_2"][0]))
    mb = np.zeros((P, 2), np.float32)
    mb[0:4, 0], mb[0:4, 1] = x["m_b_i_2"][0], x["m_b_f_2"][0]
    put("mb", mb)
    put("mln", cols(x["m_ln_g_2"][0]))
    put("wlng", cols(x["rw_ln_g_2"][0]))
    put("wlnb", cols(x["rw_ln_b_2"][0]))
    mu = x["rw_mu_2"][0]
    put("wmu", cols(mu[1152:1408]))
    by_tile = [cols(v) for v in (mu[0:384], mu[384:768], mu[768:1152], x["rw_w0_2"][0], x["rw_a0_2"][0],
                                 x["rw_k_k_2"][0], x["rw_k_a_2"][0], x["rw_r_k_2"][0])]
    put("w", np.stack(by_tile, 2).reshape(P, -1))
    tile = lambda v: v.reshape(P, 3, P).transpose(1, 0, 2).reshape(3 * P, P)
    z = np.zeros((64, 384), np.float32)
    a["w_up"] = tile(np.concatenate([x["rw_w_up_2"][0], z]))
    a["a_up"] = tile(np.concatenate([z, x["rw_a_up_2"][0]]))
    a["g_up"] = tile(x["rw_g_up_2"][0])
    d = np.arange(P)
    theta = (1.0 / 10000.0 ** np.linspace(0.0, 1.0, 32, dtype=np.float32)).astype(np.float32)
    ang = np.arange(SEQ, dtype=np.float32)[None, :] * theta[d % 32][:, None]
    a["cos"] = np.cos(ang)
    a["sin"] = np.sin(ang) * np.where(d % 64 < 32, -1.0, 1.0).astype(np.float32)[:, None]
    a["swap"] = (d[:, None] == (d ^ 32)[None, :]).astype(np.float32)
    xx = np.arange(SEQ)[None, :] - d[:, None]
    log_g = np.log(1.0 - 2.0 ** (-5.0 - np.arange(6)))
    a["ramps"] = np.concatenate([np.where(xx >= 0, np.exp(np.maximum(xx, 0) * lg), 0.0) * 0.125
                                 for lg in log_g]).astype(np.float32)
    a["tri"] = np.where(xx[:, 0:512] >= 0, 0.0, -1e30).astype(np.float32)
    a["reset"] = np.broadcast_to((np.arange(SEQ) % CH != 0).astype(np.float32), (P, SEQ))
    a["low"], a["upp"] = level_masks()
    a["ident"] = np.eye(P, dtype=np.float32)
    a["mean64"] = np.kron(np.eye(2), np.full((64, 64), 1.0 / 64)).astype(np.float32)


def layout3(x, a, put):
    w = x["w_in_3"][0]
    gates = np.zeros((D, P), w.dtype)
    gates[:, 0:16], gates[:, 32:48] = w[:, 2064:2080], w[:, 2048:2064]
    a["w_in_3"] = np.concatenate([w[:, 0:2048], w[:, 2080:3104], gates, np.zeros((D, P), w.dtype)], 1)
    a["w_out_3"], a["w_ff1_3"], a["w_ff2_3"] = x["w_out_3"][0], x["w_ff1_3"][0], x["w_ff2_3"][0]
    put("g3", cols(x["norm_mix_3"][0]))
    put("gm3", cols(x["norm_ffn_3"][0]))
    put("gf3", cols(x["norm_final_3"]))
    put("gconv", cols(x["conv_w_3"][0]))
    gates3 = np.zeros((P, 2), np.float32)
    gates3[0:8, 0], gates3[8:16, 0] = x["dt_bias_fwd_3"][0], x["dt_bias_bwd_3"][0]
    gates3[0:8, 1], gates3[8:16, 1] = x["a_log_fwd_3"][0], x["a_log_bwd_3"][0]
    put("gates3", gates3)
    put("gdng", np.tile(x["gdn_norm_3"][0][:, None], (2, 4)))
    put("sgv", cols(x["sgu_v_norm_3"][0].reshape(-1)))
    put("sgo", cols(x["sgu_out_norm_3"][0].reshape(-1)))
    a["sgu_wt"] = x["sgu_w_3"][0].transpose(0, 2, 1).reshape(4 * P, P)
    a["sgu_b"] = x["sgu_b_3"][0]


def program(nc, a, out, col, blocks=(1, 2, 3)):
    g = Shared()
    g.col = col
    par_cols = a["par"].shape[1]
    dram = lambda n, shape: nc.dram_tensor(n, shape, F32, kind="Internal").ap()
    with ExitStack() as ctx:
        sb = lambda n, shape, dt=F32: ctx.enter_context(nc.sbuf_tensor(n, shape, dt))
        g.h = sb("h", [P, KD, T1])
        g.par = sb("par", [P, par_cols])
        g.ones, g.ident, g.mean64 = sb("ones", [P, P]), sb("ident", [P, P]), sb("mean64", [P, P])
        with stage(nc, "start", "loaded", "ones") as s:
            with nc.Block() as block:
                @block.sync
                def _(sp):
                    T = a["h0"].shape[1]
                    sp.dma_start(g.h[:, :, 0:T], a["h0"].rearrange("(k p) t -> p k t", p=P)).then_inc(s["loaded"], 16)
                    sp.dma_start(g.par[:, :], a["par"]).then_inc(s["loaded"], 16)
                    sp.dma_start(g.ident[:, :], a["ident"]).then_inc(s["loaded"], 16)
                    sp.dma_start(g.mean64[:, :], a["mean64"]).then_inc(s["loaded"], 16)
                    sp.wait_ge(s["loaded"], 64)

                @block.vector
                def _(dve):
                    dve.memset(g.ones[:, :], 1.0).then_inc(s["ones"], 1)

        @contextmanager
        def parts(name):
            with nc.sbuf_tensor(name + "_uhi", [P, KD, T1], F32R) as uhi, \
                 nc.sbuf_tensor(name + "_ulo", [P, KD, T1], F32R) as ulo:
                g.uhi, g.ulo = uhi, ulo
                yield

        g.parts = parts
        if 1 in blocks:
            block1(nc, g, a, dram("proj1", (TILES_1 * P, T1)))
        if 2 in blocks:
            block2(nc, g, a, dram)
        if 3 in blocks:
            block3(nc, g, a, dram, out)
        else:
            with stage(nc, "dump", "st") as s:
                with nc.Block() as block:
                    @block.sync
                    def _(sp):
                        sp.dma_start(out.rearrange("(k p) t -> p k t", p=P), g.h[:, :, 0:SEQ]).then_inc(s["st"], 16)
                        sp.wait_ge(s["st"], 16)


def kernel(**inputs):
    import concourse.bacc as bacc
    from concourse.bass_utils import run_bass_kernel_spmd

    arrays, col = layout({k: np.asarray(v) for k, v in inputs.items()})
    arrays = {k: np.ascontiguousarray(v) for k, v in arrays.items()}
    nc = bacc.Bacc("TRN2", target_bir_lowering=False, num_devices=1)
    a = {k: nc.dram_tensor(f"in_{k}", v.shape, F32, kind="ExternalInput").ap() for k, v in arrays.items()}
    out = nc.dram_tensor("out_t", (D, SEQ), F32, kind="ExternalOutput").ap()
    program(nc, a, out, col)
    r = run_bass_kernel_spmd(nc, [{f"in_{k}": v for k, v in arrays.items()}], core_ids=[0])
    return np.ascontiguousarray(r.results[0]["out_t"].T)[None]
```

```python
from contextlib import ExitStack, contextmanager

import numpy as np
import concourse.bass as bass
from concourse import mybir

F32 = mybir.dt.float32
F32R = mybir.dt.float32r
ACT = mybir.ActivationFunctionType
ALU = mybir.AluOpType
ds = bass.ds

P = 128
D = 1024
KD = D // P
SEQ = 1024
META = 16
EPS = 1e-6
CH = 64
NCH = SEQ // CH
M_Q, M_K, M_V, M_O, R_Q, R_K, R_V, R_G, W_R, W_K, W_V, W_WA, W_GL, M_GATE = (
    0, 2, 4, 6, 8, 11, 14, 17, 20, 23, 26, 29, 30, 31)
G_Q, G_K, G_V, G_Z, G_SU, G_SV, G_GATE = 0, 4, 8, 12, 16, 20, 24
TILES_1, TILES_2, TILES_3 = 16, 32, 26


class Stage(dict):
    pass


class Shared:
    pass


@contextmanager
def stage(nc, name, *names):
    with ExitStack() as ctx:
        s = Stage((n, ctx.enter_context(nc.semaphore(f"{name}_{n}"))) for n in names)
        s.sb = lambda n, shape, dt=F32: ctx.enter_context(nc.sbuf_tensor(f"{name}_{n}", shape, dt))
        s.ps = lambda n, shape, dt=F32: ctx.enter_context(nc.psum_tensor(f"{name}_{n}", shape, dt))
        yield s
        clear(nc, s)


def clear(nc, s, keep=None):
    sems = [sem for name, sem in s.items() if name != keep]
    with nc.Block() as block:
        @block.gpsimd
        def _(pool):
            for sem in sems[0::2]:
                pool.sem_clear(sem)

        @block.sync
        def _(sp):
            for sem in sems[1::2]:
                sp.sem_clear(sem)


def chain(eng, own):
    count = {}

    def link(ins, sem=None):
        sem = own if sem is None else sem
        count[id(sem)] = count.get(id(sem), 0) + 1
        ins.then_inc(sem, 1)
        eng.wait_ge(sem, count[id(sem)])

    return link


def own_chain(eng, s):
    eng.sem_clear(s["own"])
    return chain(eng, s["own"])


def rsqrt(act, s, x, n):
    act.activation(x, x, ACT.Ln).then_inc(s["logged"], 1)
    act.wait_ge(s["logged"], n)
    act.activation(x, x, ACT.Exp, scale=-0.5).then_inc(s["rooted"], 1)


def cuts(T):
    n = 4 if T == SEQ + META else 2
    return n, T // n


def flat(ps, T):
    n, w = cuts(T)
    return ps[:, 0:n, 0:w]


def sliced(ap, T):
    n, w = cuts(T)
    return ap.rearrange("p (n w) -> p n w", n=n)


DENSE = ("landed0", "landed1", "hi0", "hi1", "lo0", "lo1", "done0", "done1", "free0", "free1",
         "stored0", "stored1", "own", "act", "conv0", "conv1", "silu0", "silu1")


def weight_buffers(s):
    s.raw = [s.sb(f"raw{b}", [P, KD, P]) for b in range(2)]
    s.whi = [s.sb(f"whi{b}", [P, KD, P], F32R) for b in range(2)]
    s.wlo = [s.sb(f"wlo{b}", [P, KD, P], F32R) for b in range(2)]
    s.psum = s.ps("acc", [P, 8, 512])
    s.landed, s.hi, s.lo = [s["landed0"], s["landed1"]], [s["hi0"], s["hi1"]], [s["lo0"], s["lo1"]]
    s.done, s.free, s.stored = [s["done0"], s["done1"]], [s["free0"], s["free1"]], [s["stored0"], s["stored1"]]


def grant(nc, s):
    with nc.Block() as block:
        @block.gpsimd
        def _(pool):
            for sem in (*s.lo, *s.done, *s.free, s["act"]):
                pool.sem_inc(sem, 1)
            for sem in s.stored:
                pool.sem_inc(sem, 16)


def load_tile(sp, s, b, it, src, kt):
    sp.wait_ge(s.lo[b], it + 1)
    sp.dma_start(s.raw[b][:, 0:kt, :], src).then_inc(s.landed[b], 16)


def split_hi(act, s, b, it, kt):
    act.wait_ge(s.landed[b], (it + 1) * 16)
    act.wait_ge(s.done[b], it + 1)
    act.activation(s.whi[b][:, 0:kt, :], s.raw[b][:, 0:kt, :], ACT.Copy).then_inc(s.hi[b], 1)


def split_lo(pool, s, b, it, kt):
    pool.wait_ge(s.hi[b], it + 1)
    pool.tensor_tensor(s.wlo[b][:, 0:kt, :], s.raw[b][:, 0:kt, :], s.whi[b][:, 0:kt, :].bitcast(F32),
                       ALU.subtract).then_inc(s.lo[b], 1)


def product(pe, s, b, it, hi, lo, T, kt, late=None):
    n, w = cuts(T)
    pe.wait_ge(s.lo[b], it + 2)
    pe.wait_ge(s.free[b], it + 1)
    for k in range(kt):
        if late is not None and k >= kt - 2:
            pe.wait_ge(s["act"], late + k)
        for j in range(n):
            out = s.psum[:, 4 * b + j, 0:w]
            x_hi, x_lo = hi[:, k, j * w:j * w + w], lo[:, k, j * w:j * w + w]
            pe.matmul(out, s.whi[b][:, k, :], x_hi, start=(k == 0), stop=False)
            pe.matmul(out, s.whi[b][:, k, :], x_lo, start=False, stop=False)
            mm = pe.matmul(out, s.wlo[b][:, k, :], x_hi, start=False, stop=(k == kt - 1))
    mm.then_inc(s.done[b], 1)


def dense(nc, name, g, W, tiles, T, store=None, conv=None):
    Wt = W.rearrange("(k p) c -> p k c", p=P)
    pairs = tiles // 2
    with stage(nc, name, *DENSE) as s:
        weight_buffers(s)
        stg = [s.sb(f"stg{b}", [P, T]) for b in range(2)] if store is not None else None
        if conv:
            conv_tiles, taps, lead, col = conv
            first = conv_tiles // 2
            xs, par = s.sb("x", [P, taps - 1 + T]), s.sb("par", [P, taps])
            with nc.Block() as block:
                @block.vector
                def _(dve):
                    dve.memset(xs[:, :], 0.0).then_inc(s["own"], 1)
                    dve.wait_ge(s["own"], 1)
        grant(nc, s)
        with nc.Block() as block:
            @block.sync
            def _(sp):
                with sp.Fori(0, pairs) as i:
                    for b in range(2):
                        load_tile(sp, s, b, i, Wt[:, :, ds(i * (2 * P) + b * P, P)], KD)

            @block.scalar
            def _(act):
                def put(b, i, convolved=False):
                    if convolved:
                        act.wait_ge(s[f"conv{b}"], i + 1)
                        act.activation(stg[b][:, :], stg[b][:, :], ACT.Silu).then_inc(s[f"silu{b}"], 1)
                        act.wait_ge(s[f"silu{b}"], i + 1)
                    else:
                        act.wait_ge(s.free[b], i + 2)
                    act.dma_start(store[ds(i * (2 * P) + b * P, P), :], stg[b][:, :]).then_inc(s.stored[b], 16)

                if store is None:
                    with act.Fori(0, pairs) as i:
                        for b in range(2):
                            split_hi(act, s, b, i, KD)
                else:
                    for b in range(2):
                        split_hi(act, s, b, 0, KD)
                    if conv:
                        with act.Fori(0, first) as i:
                            for b in range(2):
                                put(b, i, convolved=True)
                                split_hi(act, s, b, i + 1, KD)
                    rest = first if conv else 0
                    with act.Fori(0, pairs - 1 - rest) as i:
                        for b in range(2):
                            put(b, i + rest)
                            split_hi(act, s, b, i + (rest + 1), KD)
                    for b in range(2):
                        put(b, pairs - 1)
                    for b in range(2):
                        act.wait_ge(s.stored[b], 16 * pairs + 16)

            @block.gpsimd
            def _(pool):
                with pool.Fori(0, pairs) as i:
                    for b in range(2):
                        split_lo(pool, s, b, i, KD)

            @block.tensor
            def _(pe):
                with pe.Fori(0, pairs) as i:
                    for b in range(2):
                        product(pe, s, b, i, g.uhi, g.ulo, T, KD)

            @block.vector
            def _(dve):
                def convolved(b, i):
                    dve.wait_ge(s.done[b], i + 2)
                    dve.tensor_tensor(sliced(xs[:, lead:lead + T], T), acc(b), sliced(g.inv[:, 0:T], T),
                                      ALU.mult).then_inc(s.free[b], 1)
                    link = own_chain(dve, s)
                    link(dve.tensor_copy(par[:, :], g.par[:, ds(i * (2 * taps) + (b * taps + g.col[col]), taps)]))
                    dve.wait_ge(s.free[b], i + 2)
                    dve.wait_ge(s.stored[b], i * 16 + 16)
                    y = stg[b][:, :]
                    link(dve.tensor_scalar(y, xs[:, 0:T], par[:, 0:1], None, ALU.mult))
                    for k in range(1, taps - 1):
                        link(dve.scalar_tensor_tensor(y, xs[:, k:k + T], par[:, k:k + 1], y, ALU.mult, ALU.add))
                    dve.scalar_tensor_tensor(y, xs[:, taps - 1:taps - 1 + T], par[:, taps - 1:taps], y,
                                             ALU.mult, ALU.add).then_inc(s[f"conv{b}"], 1)
                    dve.wait_ge(s[f"conv{b}"], i + 1)

                def plain(b, i):
                    dve.wait_ge(s.done[b], i + 2)
                    if store is not None:
                        dve.wait_ge(s.stored[b], i * 16 + 16)
                        dve.tensor_tensor(sliced(stg[b][:, :], T), acc(b), sliced(g.inv[:, 0:T], T), ALU.mult)\
                           .then_inc(s.free[b], 1)
                    else:
                        n, w = cuts(T)
                        h = g.h[:, ds(i * 2 + b, 1), 0:T].rearrange("p a (n w) -> p (a n) w", n=n)
                        dve.tensor_tensor(h, h, acc(b), ALU.add).then_inc(s.free[b], 1)

                acc = lambda b: flat(s.psum[:, 4 * b:4 * b + 4, :], T)
                rest = first if conv else 0
                if conv:
                    with dve.Fori(0, first) as i:
                        for b in range(2):
                            convolved(b, i)
                with dve.Fori(0, pairs - rest) as i:
                    for b in range(2):
                        plain(b, i + rest)


def ffn(nc, name, g, Wup, Wdown, groups, T, gated):
    up, down = (W.rearrange("(k p) c -> p k c", p=P) for W in (Wup, Wdown))
    n, w = cuts(T)
    with stage(nc, name, *DENSE) as s:
        weight_buffers(s)
        xhi = s.sb("xhi", [P, 8, T], F32R)
        xlo = s.sb("xlo", [P, 8, T], F32R)
        sq = s.sb("sq", [P, T])
        silu = s.sb("silu", [P, T]) if gated else None
        inv = sliced(g.inv[:, 0:T], T)
        grant(nc, s)

        def walk(eng, do_up, do_down):
            before, tile = 0, 0
            for many, kt in groups:
                ups = kt if gated else kt // 2
                per = ups + KD // 2

                def one(o):
                    with eng.Fori(0, ups) as j:
                        do_up(j, o * per + before + j, o * kt + tile, kt, o)
                    with eng.Fori(0, KD // 2) as j:
                        do_down(j, o * per + before + ups + j, o * kt + tile, kt, o)

                if many > 1:
                    with eng.Fori(0, many) as o:
                        one(o)
                else:
                    one(0)
                before += many * per
                tile += many * kt

        with nc.Block() as block:
            @block.sync
            def _(sp):
                def do_up(j, it, tile, kt, o):
                    for b in range(2):
                        at = tile * (2 * P if gated else P) + j * (2 * P) + b * P
                        load_tile(sp, s, b, it, up[:, :, ds(at, P)], KD)

                def do_down(j, it, tile, kt, o):
                    for b in range(2):
                        load_tile(sp, s, b, it, down[:, ds(tile, kt), ds(j * (2 * P) + b * P, P)], kt)

                walk(sp, do_up, do_down)

            @block.scalar
            def _(act):
                def do_up(j, it, tile, kt, o):
                    for b in range(2):
                        split_hi(act, s, b, it, KD)
                    if gated:
                        act.wait_ge(s["free0"], it + 2)
                        act.activation(silu[:, :], silu[:, :], ACT.Silu).then_inc(s["silu0"], 1)

                def do_down(j, it, tile, kt, o):
                    for b in range(2):
                        split_hi(act, s, b, it, kt)

                walk(act, do_up, do_down)

            @block.gpsimd
            def _(pool):
                def do_up(j, it, tile, kt, o):
                    for b in range(2):
                        split_lo(pool, s, b, it, KD)

                def do_down(j, it, tile, kt, o):
                    for b in range(2):
                        split_lo(pool, s, b, it, kt)

                walk(pool, do_up, do_down)

            @block.tensor
            def _(pe):
                def do_up(j, it, tile, kt, o):
                    for b in range(2):
                        product(pe, s, b, it, g.uhi, g.ulo, T, KD)

                def do_down(j, it, tile, kt, o):
                    pe.wait_ge(s["act"], tile + (kt - 1))
                    product(pe, s, 0, it, xhi, xlo, T, kt, late=tile + 2)
                    product(pe, s, 1, it, xhi, xlo, T, kt)

                walk(pe, do_up, do_down)

            @block.vector
            def _(dve):
                def split(link, m):
                    link(dve.tensor_copy(xhi[:, ds(m, 1), :], sq[:, None, :]))
                    dve.tensor_tensor(xlo[:, ds(m, 1), :], sq[:, None, :],
                                      xhi[:, ds(m, 1), :].bitcast(F32), ALU.subtract).then_inc(s["act"], 1)

                def do_up(j, it, tile, kt, o):
                    if gated:
                        dve.wait_ge(s["done0"], it + 2)
                        dve.wait_ge(s["act"], tile + j + 1)
                        dve.tensor_tensor(sliced(silu[:, :], T), flat(s.psum[:, 0:4, :], T), inv, ALU.mult)\
                           .then_inc(s["free0"], 1)
                        link = own_chain(dve, s)
                        dve.wait_ge(s["done1"], it + 2)
                        dve.tensor_tensor(sliced(sq[:, :], T), flat(s.psum[:, 4:8, :], T), inv, ALU.mult)\
                           .then_inc(s["free1"], 1)
                        dve.wait_ge(s["free1"], it + 2)
                        dve.wait_ge(s["silu0"], tile + j + 1)
                        link(dve.tensor_tensor(sq[:, :], sq[:, :], silu[:, :], ALU.mult))
                        split(link, j)
                        return
                    for b in range(2):
                        link = own_chain(dve, s)
                        dve.wait_ge(s.done[b], it + 2)
                        dve.wait_ge(s["act"], tile + j * 2 + (b + 1))
                        dve.tensor_scalar(sliced(sq[:, :], T), flat(s.psum[:, 4 * b:4 * b + 4, :], T),
                                          0.0, None, ALU.max).then_inc(s.free[b], 1)
                        dve.wait_ge(s.free[b], it + 2)
                        link(dve.tensor_tensor(sq[:, :], sq[:, :], g.inv[:, 0:T], ALU.mult))
                        link(dve.tensor_tensor(sq[:, :], sq[:, :], sq[:, :], ALU.mult))
                        split(link, j * 2 + b)

                def do_down(j, it, tile, kt, o):
                    for b in range(2):
                        dve.wait_ge(s.done[b], it + 2)
                        h = g.h[:, ds(j * 2 + b, 1), 0:T].rearrange("p a (n w) -> p (a n) w", n=n)
                        dve.tensor_tensor(h, h, flat(s.psum[:, 4 * b:4 * b + 4, :], T), ALU.add)\
                           .then_inc(s.free[b], 1)

                walk(dve, do_up, do_down)


def norm_h(nc, name, g, gain, T, first=0, dest="u"):
    split = isinstance(dest, str) and dest == "u"
    with stage(nc, name, "eps", "sq_a", "sq_d", "sq_p", "added", "summed", "logged", "rooted", "upper", "lower",
               "whole_d", "whole_p", "stored") as s:
        buf = [s.sb(f"buf{k}", [P, T]) for k in range(KD)]
        tot, low = s.sb("tot", [P, T]), s.sb("eps", [P, 1])
        acc = s.ps("acc", [P, 4, 512])
        inv = g.inv[:, 0:T] if split else s.sb("inv", [P, T])[:, :]
        gained = g.uhi if split else s.sb("gained", [P, KD, T])
        n, w = cuts(T)
        x = lambda k: g.h[:, k, first:first + T]
        with nc.Block() as block:
            @block.scalar
            def _(act):
                def upper(k):
                    act.activation(gained[:, k, 0:T], x(k), ACT.Copy, scale=g.par[:, gain + k:gain + k + 1])\
                       .then_inc(s["upper"], 1)

                for k in range(3, KD):
                    act.activation(buf[k][:, :], x(k), ACT.Square).then_inc(s["sq_a"], 1)
                for k in range(5):
                    upper(k)
                act.wait_ge(s["summed"], 1)
                act.wait_ge(s["eps"], 1)
                act.activation(sliced(inv, T), flat(acc, T), ACT.Ln, scale=1.0 / D, bias=low[:, 0:1])\
                   .then_inc(s["logged"], 1)
                act.wait_ge(s["logged"], 1)
                act.activation(inv, inv, ACT.Exp, scale=-0.5).then_inc(s["rooted"], 1)
                for k in range(5, KD):
                    upper(k)

            @block.gpsimd
            def _(pool):
                for k in (1, 2):
                    pool.tensor_tensor(buf[k][:, :], x(k), x(k), ALU.mult).then_inc(s["sq_p"], 1)
                if not split:
                    pool.wait_ge(s["rooted"], 1)
                    for k in (2, 5):
                        pool.wait_ge(s["upper"], k + 1)
                        pool.tensor_tensor(g.h[:, k, 0:T], gained[:, k, :], inv, ALU.mult).then_inc(s["whole_p"], 1)

            @block.vector
            def _(dve):
                dve.memset(low[:, :], EPS).then_inc(s["eps"], 1)
                dve.tensor_tensor(buf[0][:, :], x(0), x(0), ALU.mult).then_inc(s["sq_d"], 1)
                dve.wait_ge(s["sq_a"], 2)
                dve.tensor_tensor(tot[:, :], buf[3][:, :], buf[4][:, :], ALU.add).then_inc(s["added"], 1)
                for k in range(5, KD):
                    dve.wait_ge(s["sq_a"], k - 2)
                    dve.wait_ge(s["added"], k - 4)
                    dve.tensor_tensor(tot[:, :], tot[:, :], buf[k][:, :], ALU.add).then_inc(s["added"], 1)
                if split:
                    for k in range(KD):
                        dve.wait_ge(s["upper"], k + 1)
                        dve.scalar_tensor_tensor(g.ulo[:, k, 0:T], x(k), g.par[:, gain + k:gain + k + 1],
                                                 g.uhi[:, k, 0:T].bitcast(F32), ALU.mult, ALU.subtract)\
                           .then_inc(s["lower"], 1)
                else:
                    dve.wait_ge(s["rooted"], 1)
                    for k in (0, 1, 3, 4, 6, 7):
                        dve.wait_ge(s["upper"], k + 1)
                        dve.tensor_tensor(g.h[:, k, 0:T], gained[:, k, :], inv, ALU.mult).then_inc(s["whole_d"], 1)

            @block.tensor
            def _(pe):
                parts = [(buf[0], "sq_d", 1), (buf[1], "sq_p", 1), (buf[2], "sq_p", 2), (tot, "added", KD - 4)]
                for m, (t, sem, count) in enumerate(parts):
                    pe.wait_ge(s[sem], count)
                    for j in range(n):
                        mm = pe.matmul(acc[:, j, 0:w], g.ones[:, :], t[:, j * w:j * w + w], start=(m == 0),
                                       stop=(m == len(parts) - 1))
                mm.then_inc(s["summed"], 1)

            @block.sync
            def _(sp):
                if not isinstance(dest, str):
                    for k, sem, count in ((0, "whole_d", 1), (1, "whole_d", 2), (2, "whole_p", 1), (3, "whole_d", 3),
                                          (4, "whole_d", 4), (6, "whole_d", 5), (5, "whole_p", 2), (7, "whole_d", 6)):
                        sp.wait_ge(s[sem], count)
                        sp.dma_start(dest[k * P:(k + 1) * P, :], g.h[:, k, 0:T]).then_inc(s["stored"], 16)
                    sp.wait_ge(s["stored"], 16 * KD)


def norm(nc, name, g, src, groups, gain, T):
    NB = 4
    with stage(nc, name, "eps", "squared", "added", "summed", "logged", "rooted", "scaled", "upper", "low_p",
               "low_d") as s:
        buf = [s.sb(f"buf{b}", [P, T]) for b in range(NB)]
        tot, inv = ([s.sb(f"{n}{b}", [P, T]) for b in range(len(groups))] for n in ("tot", "inv"))
        low = s.sb("eps", [P, 1])
        acc = s.ps("acc", [P, 8, 512])
        n, w = cuts(T)
        tiles = [(gi, k) for gi, (a, b) in enumerate(groups) for k in range(a, b)]
        x = lambda k: src[:, k, 0:T]
        bank = lambda gi: flat(acc[:, 4 * gi:4 * gi + 4, :], T)

        def free(eng, k):
            eng.wait_ge(s["upper"], k + 1)
            eng.wait_ge(s["low_d"] if k % 2 else s["low_p"], k // 2 + 1)

        with nc.Block() as block:
            @block.scalar
            def _(act):
                for gi, k in tiles:
                    if k >= NB:
                        act.wait_ge(s["added"], k - NB + 1)
                    act.activation(buf[k % NB][:, :], x(k), ACT.Square).then_inc(s["squared"], 1)
                act.wait_ge(s["eps"], 1)
                for gi, (a, b) in enumerate(groups):
                    act.wait_ge(s["summed"], gi + 1)
                    act.activation(sliced(inv[gi][:, :], T), bank(gi), ACT.Ln, scale=1.0 / ((b - a) * P),
                                   bias=low[:, 0:1]).then_inc(s["logged"], 1)
                    act.wait_ge(s["logged"], gi + 1)
                    act.activation(inv[gi][:, :], inv[gi][:, :], ACT.Exp, scale=-0.5).then_inc(s["rooted"], 1)
                for gi, k in tiles:
                    act.wait_ge(s["scaled"], k + 1)
                    act.activation(g.uhi[:, k, 0:T], buf[k % NB][:, :], ACT.Copy).then_inc(s["upper"], 1)

            @block.tensor
            def _(pe):
                for gi, (a, b) in enumerate(groups):
                    pe.wait_ge(s["added"], b)
                    for j in range(n):
                        mm = pe.matmul(acc[:, 4 * gi + j, 0:w], g.ones[:, :], tot[gi][:, j * w:j * w + w],
                                       start=True, stop=True)
                    mm.then_inc(s["summed"], 1)

            @block.vector
            def _(dve):
                def lower(k):
                    dve.wait_ge(s["upper"], k + 1)
                    dve.tensor_tensor(g.ulo[:, k, 0:T], buf[k % NB][:, :], g.uhi[:, k, 0:T].bitcast(F32),
                                      ALU.subtract).then_inc(s["low_d"], 1)

                dve.memset(low[:, :], EPS).then_inc(s["eps"], 1)
                for gi, k in tiles:
                    dve.wait_ge(s["squared"], k + 1)
                    if k == groups[gi][0]:
                        ins = dve.tensor_copy(tot[gi][:, :], buf[k % NB][:, :])
                    else:
                        dve.wait_ge(s["added"], k)
                        ins = dve.tensor_tensor(tot[gi][:, :], tot[gi][:, :], buf[k % NB][:, :], ALU.add)
                    ins.then_inc(s["added"], 1)
                for gi, k in tiles:
                    dve.wait_ge(s["rooted"], gi + 1)
                    if k >= NB:
                        free(dve, k - NB)
                    dve.scalar_tensor_tensor(buf[k % NB][:, :], x(k), g.par[:, gain + k:gain + k + 1],
                                             inv[gi][:, :], ALU.mult, ALU.mult).then_inc(s["scaled"], 1)
                    if k % 2 == 0 and k > 0:
                        lower(k - 1)
                lower(tiles[-1][1])

            @block.gpsimd
            def _(pool):
                for gi, k in tiles[0::2]:
                    pool.wait_ge(s["upper"], k + 1)
                    pool.tensor_tensor(g.ulo[:, k, 0:T], buf[k % NB][:, :], g.uhi[:, k, 0:T].bitcast(F32),
                                       ALU.subtract).then_inc(s["low_p"], 1)


T1 = SEQ + META
LRU_HALO, CC_HALO = 3, 30
LRU_PAR = 10


def lru(nc, g, proj, wa, wx):
    two = range(2)
    with stage(nc, "lru", "zero", *[f"{n}{j}" for j in two for n in ("x_in", "g_in", "wa_in", "wx_in")], "par", "abs",
               "power", "conv", "gated", "sig_a", "sig_x", "loga", "decay", "tanh", "gates", "gelu", "root",
               "own", "y") as s:
        xl, xc, gate, r, ig, a, th = ([s.sb(f"{n}{j}", [P, w]) for j in two] for n, w in
                                      (("xl", LRU_HALO + T1), ("xc", T1), ("gate", T1), ("r", T1), ("ig", T1),
                                       ("a", T1), ("th", T1)))
        w_a, w_x = ([s.sb(f"{n}{j}", [P, P]) for j in two] for n in ("wa", "wx"))
        par, tiny = s.sb("par", [P, 2, LRU_PAR]), s.sb("tiny", [P, 4, 2])
        acc = s.ps("acc", [P, 8, 512])
        n, w = cuts(T1)
        with nc.Block() as block:
            @block.vector
            def _(dve):
                for t in xl:
                    dve.memset(t[:, 0:LRU_HALO], 0.0).then_inc(s["zero"], 1)
        clear(nc, s)
        with nc.Fori(0, 2) as i:
            with nc.Block() as block:
                @block.sync
                def _(sp):
                    for j in two:
                        at = lambda tile: ds(i * (2 * P) + (tile + j) * P, P)
                        sp.dma_start(xl[j][:, LRU_HALO:], proj[at(0), :]).then_inc(s[f"x_in{j}"], 16)
                        sp.dma_start(w_a[j][:, :], wa[at(0), :]).then_inc(s[f"wa_in{j}"], 16)
                        sp.dma_start(w_x[j][:, :], wx[at(0), :]).then_inc(s[f"wx_in{j}"], 16)
                        sp.dma_start(gate[j][:, :], proj[at(4), :]).then_inc(s[f"g_in{j}"], 16)

                @block.vector
                def _(dve):
                    link = chain(dve, s["own"])
                    dve.tensor_copy(par[:, :, :].rearrange("p a b -> p (a b)"),
                                    g.par[:, ds(i * (2 * LRU_PAR) + g.col["lru"], 2 * LRU_PAR)])\
                       .then_inc(s["par"], 1)
                    dve.wait_ge(s["par"], 1)
                    for j in two:
                        p_ = lambda k: par[:, j, k:k + 1]
                        dve.wait_ge(s[f"x_in{j}"], 16)
                        link(dve.tensor_scalar(xc[j][:, :], xl[j][:, 0:T1], p_(0), p_(4), ALU.mult, ALU.add))
                        for k in range(1, 4):
                            link(dve.scalar_tensor_tensor(xc[j][:, :], xl[j][:, k:k + T1], p_(k), xc[j][:, :],
                                                          ALU.mult, ALU.add), s["conv"] if k == 3 else None)
                    dve.wait_ge(s["power"], 1)
                    e, z, z2, q = (tiny[:, k, :] for k in range(4))
                    link(dve.tensor_scalar(z, e, 2.0, None, ALU.add))
                    link(dve.reciprocal(z, z))
                    link(dve.tensor_tensor(z, z, e, ALU.mult))
                    link(dve.tensor_tensor(z2, z, z, ALU.mult))
                    link(dve.tensor_scalar(q, z2, 1.0 / 15, 1.0 / 13, ALU.mult, ALU.add))
                    for m in (11, 9, 7, 5, 3, 1):
                        link(dve.tensor_tensor(q, q, z2, ALU.mult))
                        link(dve.tensor_scalar(q, q, 1.0 / m, None, ALU.add))
                    link(dve.tensor_tensor(q, q, z, ALU.mult))
                    link(dve.tensor_scalar(z, par[:, :, 7], -1.0, 0.0, ALU.mult, ALU.max))
                    link(dve.scalar_tensor_tensor(q, q, 2.0, z, ALU.mult, ALU.add))
                    link(dve.tensor_scalar(q, q, -8.0, None, ALU.mult))
                    for j in two:
                        dve.wait_ge(s["sig_a"], j + 1)
                        dve.tensor_scalar(r[j][:, :], r[j][:, :], q[:, j:j + 1], None, ALU.mult)\
                           .then_inc(s["loga"], 1)
                        dve.wait_ge(s["sig_x"], j + 1)
                        link(dve.tensor_tensor(ig[j][:, :], ig[j][:, :], xc[j][:, :], ALU.mult))
                    for j in two:
                        dve.wait_ge(s["decay"], j + 1)
                        link(dve.tensor_tensor(xc[j][:, :], a[j][:, :], a[j][:, :], ALU.mult))
                        dve.wait_ge(s["tanh"], j + 1)
                        dve.scalar_tensor_tensor(th[j][:, :], xc[j][:, :], 1.0, th[j][:, :], ALU.add, ALU.mult)\
                           .then_inc(s["gates"], 1)
                    for j in two:
                        dve.wait_ge(s["root"], j + 1)
                        link(dve.tensor_tensor(ig[j][:, :], ig[j][:, :], th[j][:, :], ALU.mult))
                        link(dve.tensor_tensor_scan(xc[j][:, :], a[j][:, :], ig[j][:, :], 0.0, ALU.mult, ALU.add))
                        dve.wait_ge(s["gelu"], j + 1)
                        dve.tensor_tensor(g.y[:, ds(i * 2 + j, 1), :], xc[j][:, None, :], gate[j][:, None, :],
                                          ALU.mult).then_inc(s["y"], 1)

                @block.tensor
                def _(pe):
                    for j in two:
                        pe.wait_ge(s["conv"], j + 1)
                        for b, (wt, name, read) in enumerate(((w_a, "wa_in", "sig_a"), (w_x, "wx_in", "sig_x"))):
                            pe.wait_ge(s[f"{name}{j}"], 16)
                            if j:
                                pe.wait_ge(s[read], 1)
                            for m in range(n):
                                mm = pe.matmul(acc[:, 4 * b + m, 0:w], wt[j][:, :], xc[j][:, m * w:m * w + w],
                                               start=True, stop=True)
                            mm.then_inc(s["gated"], 1)

                @block.scalar
                def _(act):
                    act.wait_ge(s["par"], 1)
                    act.activation(tiny[:, 0, :], par[:, :, 7], ACT.Abs).then_inc(s["abs"], 1)
                    act.wait_ge(s["abs"], 1)
                    act.activation(tiny[:, 0, :], tiny[:, 0, :], ACT.Exp, scale=-1.0).then_inc(s["power"], 1)
                    for j in two:
                        for b, (x, sem) in enumerate(((r, "sig_a"), (ig, "sig_x"))):
                            act.wait_ge(s["gated"], 2 * j + b + 1)
                            act.activation(sliced(x[j][:, :], T1), flat(acc[:, 4 * b:4 * b + 4, :], T1), ACT.Sigmoid,
                                           bias=par[:, j, 5 + b:6 + b]).then_inc(s[sem], 1)
                    for j in two:
                        act.wait_ge(s["loga"], j + 1)
                        act.activation(a[j][:, :], r[j][:, :], ACT.Exp).then_inc(s["decay"], 1)
                        act.activation(th[j][:, :], r[j][:, :], ACT.Tanh, scale=-1.0).then_inc(s["tanh"], 1)
                    for j in two:
                        act.wait_ge(s["gates"], j + 1)
                        act.activation(th[j][:, :], th[j][:, :], ACT.Sqrt).then_inc(s["root"], 1)
                    for j in two:
                        act.wait_ge(s[f"g_in{j}"], 16)
                        act.activation(gate[j][:, :], gate[j][:, :], ACT.Gelu_apprx_tanh).then_inc(s["gelu"], 1)
            clear(nc, s)


CC_TAPS = 31
CC_PAR = CC_TAPS + 1


def conv_mixer(nc, g, proj):
    on_pe = 12
    with stage(nc, "cc", "zero", "par", *[f"{n}{j}" for j in range(2) for n in ("v_in", "g_in")], "sig", "glu",
               "diag", "taps", "own", "y") as s:
        v, gate, acc, diag = ([s.sb(f"{n}{j}", shape) for j in range(2)] for n, shape in
                              (("v", [P, CC_HALO + T1]), ("gate", [P, T1]), ("acc", [P, T1]), ("diag", [P, on_pe, P])))
        par = s.sb("par", [P, 2, CC_PAR])
        ps = s.ps("acc", [P, 8, 512])
        n, w = cuts(T1)
        with nc.Block() as block:
            @block.vector
            def _(dve):
                for t in v:
                    dve.memset(t[:, 0:CC_HALO], 0.0).then_inc(s["zero"], 1)
        clear(nc, s)
        with nc.Fori(0, 2) as i:
            with nc.Block() as block:
                @block.sync
                def _(sp):
                    for j in range(2):
                        sp.dma_start(v[j][:, CC_HALO:], proj[ds(i * (2 * P) + (8 + j) * P, P), :])\
                          .then_inc(s[f"v_in{j}"], 16)
                        sp.dma_start(gate[j][:, :], proj[ds(i * (2 * P) + (12 + j) * P, P), :])\
                          .then_inc(s[f"g_in{j}"], 16)

                @block.scalar
                def _(act):
                    for j in range(2):
                        act.wait_ge(s[f"g_in{j}"], 16)
                        act.activation(gate[j][:, :], gate[j][:, :], ACT.Sigmoid).then_inc(s["sig"], 1)

                @block.gpsimd
                def _(pool):
                    pool.wait_ge(s["par"], 1)
                    for j in range(2):
                        pool.tensor_tensor(diag[j][:, :, :], g.ident[:, None, :].broadcast_to([P, on_pe, P]),
                                           par[:, j, 0:on_pe].unsqueeze(2).broadcast_to([P, on_pe, P]), ALU.mult)\
                            .then_inc(s["diag"], 1)
                        if j:
                            pool.wait_ge(s["sig"], 2)
                            pool.wait_ge(s["v_in1"], 16)
                            pool.tensor_tensor(v[1][:, CC_HALO:], v[1][:, CC_HALO:], gate[1][:, :], ALU.mult)\
                                .then_inc(s["glu"], 1)

                @block.tensor
                def _(pe):
                    for j in range(2):
                        if j:
                            pe.wait_ge(s["glu"], 1)
                        else:
                            pe.wait_ge(s["y"], 1)
                        pe.wait_ge(s["diag"], j + 1)
                        for b in range(n):
                            for k in range(on_pe):
                                mm = pe.matmul(ps[:, 4 * j + b, 0:w], diag[j][:, k, :],
                                               v[j][:, k + b * w:k + b * w + w],
                                               start=(k == 0), stop=(k == on_pe - 1))
                        mm.then_inc(s["taps"], 1)

                @block.vector
                def _(dve):
                    link = chain(dve, s["own"])
                    dve.tensor_copy(par[:, :, :].rearrange("p a b -> p (a b)"),
                                    g.par[:, ds(i * (2 * CC_PAR) + g.col["cc"], 2 * CC_PAR)]).then_inc(s["par"], 1)
                    dve.wait_ge(s["par"], 1)
                    dve.wait_ge(s["sig"], 1)
                    dve.wait_ge(s["v_in0"], 16)
                    link(dve.tensor_tensor(v[0][:, CC_HALO:], v[0][:, CC_HALO:], gate[0][:, :], ALU.mult), s["y"])
                    for j in range(2):
                        if j:
                            dve.wait_ge(s["glu"], 1)
                        link(dve.tensor_scalar(acc[j][:, :], v[j][:, on_pe:on_pe + T1], par[:, j, on_pe:on_pe + 1],
                                               par[:, j, CC_TAPS:CC_TAPS + 1], ALU.mult, ALU.add))
                        for k in range(on_pe + 1, CC_TAPS):
                            link(dve.scalar_tensor_tensor(acc[j][:, :], v[j][:, k:k + T1], par[:, j, k:k + 1],
                                                          acc[j][:, :], ALU.mult, ALU.add))
                        dve.wait_ge(s["taps"], j + 1)
                        y = g.y[:, ds(i * 2 + (4 + j), 1), :].rearrange("p a (n w) -> p (a n) w", n=n)
                        link(dve.tensor_tensor(y,
                                               flat(ps[:, 4 * j:4 * j + 4, :], T1), sliced(acc[j][:, :], T1),
                                               ALU.add))
            clear(nc, s)
    with stage(nc, "ccln", "summed", "centred", "squared", "shifted", "logged", "rooted", "scaled", "own", "silu") as s:
        acc = s.ps("acc", [P, 8, 512])
        mean, inv = s.sb("mean", [P, T1]), s.sb("inv", [P, T1])
        sq = [s.sb(f"sq{b}", [P, T1]) for b in range(2)]
        n, w = cuts(T1)
        with nc.Block() as block:
            @block.tensor
            def _(pe):
                for k in range(4):
                    for j in range(n):
                        mm = pe.matmul(acc[:, j, 0:w], g.ones[:, :], g.y[:, 4 + k, j * w:j * w + w],
                                       start=(k == 0), stop=(k == 3))
                mm.then_inc(s["summed"], 1)
                for k in range(4):
                    pe.wait_ge(s["squared"], k + 1)
                    for j in range(n):
                        mm = pe.matmul(acc[:, 4 + j, 0:w], g.ones[:, :], sq[k % 2][:, j * w:j * w + w],
                                       start=(k == 0), stop=(k == 3))
                    mm.then_inc(s["summed"], 1)

            @block.vector
            def _(dve):
                link = chain(dve, s["own"])
                dve.wait_ge(s["summed"], 1)
                link(dve.tensor_scalar(sliced(mean[:, :], T1), flat(acc[:, 0:4, :], T1), 1.0 / (4 * P), None,
                                       ALU.mult))
                for k in range(4):
                    dve.tensor_tensor(g.y[:, 4 + k, :], g.y[:, 4 + k, :], mean[:, :], ALU.subtract)\
                       .then_inc(s["centred"], 1)
                dve.wait_ge(s["centred"], 4)
                dve.wait_ge(s["summed"], 5)
                dve.tensor_scalar(sliced(inv[:, :], T1), flat(acc[:, 4:8, :], T1), 1.0 / (4 * P), EPS,
                                  ALU.mult, ALU.add).then_inc(s["shifted"], 1)
                dve.wait_ge(s["rooted"], 1)
                for k in range(4):
                    link(dve.scalar_tensor_tensor(g.y[:, 4 + k, :], g.y[:, 4 + k, :],
                                                  g.par[:, g.col["ccg"] + k:g.col["ccg"] + k + 1], inv[:, :],
                                                  ALU.mult, ALU.mult), s["scaled"])

            @block.scalar
            def _(act):
                for k in range(4):
                    act.wait_ge(s["centred"], k + 1)
                    if k >= 2:
                        act.wait_ge(s["summed"], k)
                    act.activation(sq[k % 2][:, :], g.y[:, 4 + k, :], ACT.Square).then_inc(s["squared"], 1)
                act.wait_ge(s["shifted"], 1)
                rsqrt(act, s, inv[:, :], 1)
                for k in range(4):
                    act.wait_ge(s["scaled"], k + 1)
                    act.activation(g.y[:, 4 + k, :], g.y[:, 4 + k, :], ACT.Silu,
                                   bias=g.par[:, g.col["ccb"] + k:g.col["ccb"] + k + 1]).then_inc(s["silu"], 1)


def block1(nc, g, a, proj):
    with g.parts("a1"):
        norm_h(nc, "n1", g, g.col["g1"], T1)
        dense(nc, "in1", g, a["w_in"], TILES_1, T1, proj)
    with nc.sbuf_tensor("y1", [P, KD, T1], F32) as y:
        g.y = y
        lru(nc, g, proj, a["lru_wa"], a["lru_wx"])
        conv_mixer(nc, g, proj)
        with g.parts("b1"):
            norm(nc, "no1", g, g.y, [(0, 4), (4, KD)], g.col["go1"], T1)
            dense(nc, "out1", g, a["w_out"], KD, T1)
    with g.parts("c1"):
        norm_h(nc, "nm1", g, g.col["gm1"], T1)
        ffn(nc, "ff1", g, a["w_mlp_up"], a["w_mlp_down"], [(4, KD)], T1, gated=False)
    norm_h(nc, "nf1", g, g.col["gf1"], SEQ, first=META, dest="h")


def halves(ap):
    return ap.rearrange("p (n w) -> p n w", n=2)


def mlstm_gates(nc, g, proj, rows):
    with stage(nc, "mg", "loaded", "own", "abs", "power", "log", "sum", "em", "stored") as s:
        names = ("gi", "gf", "l", "m", "b", "c", "top", "one")
        gi, gf, l, m, b, c, top, one = (s.sb(n, [4, SEQ]) for n in names)
        with nc.Block() as block:
            @block.sync
            def _(sp):
                at = M_GATE * P
                sp.dma_start(gi[:, :], proj[at:at + 4, :]).then_inc(s["loaded"], 16)
                sp.dma_start(gf[:, :], proj[at + 4:at + 8, :]).then_inc(s["loaded"], 16)
                sp.wait_ge(s["sum"], 1)
                sp.dma_start(rows[0:4, :], top[:, :]).then_inc(s["stored"], 16)
                sp.dma_start(rows[8:12, :], c[:, :]).then_inc(s["stored"], 16)
                sp.wait_ge(s["em"], 1)
                sp.dma_start(rows[4:8, :], b[:, :]).then_inc(s["stored"], 16)
                sp.wait_ge(s["stored"], 48)

            @block.scalar
            def _(act):
                bf = g.par[0:4, g.col["mb"] + 1:g.col["mb"] + 2]
                act.wait_ge(s["loaded"], 32)
                act.activation(l[:, :], gf[:, :], ACT.Abs, bias=bf).then_inc(s["abs"], 1)
                act.wait_ge(s["abs"], 1)
                act.activation(l[:, :], l[:, :], ACT.Exp, scale=-1.0).then_inc(s["power"], 1)
                act.wait_ge(s["power"], 1)
                act.activation(l[:, :], l[:, :], ACT.Ln, bias=1.0).then_inc(s["log"], 1)
                act.wait_ge(s["sum"], 1)
                act.activation(b[:, :], m[:, :], ACT.Exp).then_inc(s["em"], 1)

            @block.vector
            def _(dve):
                link = chain(dve, s["own"])
                bi, bf = (g.par[0:4, g.col["mb"] + k:g.col["mb"] + k + 1] for k in range(2))
                link(dve.memset(one[:, :], 1.0))
                dve.wait_ge(s["loaded"], 32)
                link(dve.tensor_scalar(m[:, :], gf[:, :], bf, 0.0, ALU.add, ALU.min))
                dve.wait_ge(s["log"], 1)
                link(dve.tensor_tensor(m[:, :], m[:, :], l[:, :], ALU.subtract))
                link(dve.tensor_tensor_scan(b[:, :], one[:, :], m[:, :], 0.0, ALU.mult, ALU.add))
                link(dve.scalar_tensor_tensor(c[:, :], gi[:, :], bi, b[:, :], ALU.add, ALU.subtract))
                link(dve.tensor_tensor_scan(top[:, :], c[:, :], c[:, :], -3e38, ALU.max, ALU.max))
                link(dve.scalar_tensor_tensor(m[:, :], b[:, :], -1.0, top[:, :], ALU.mult, ALU.subtract))
                link(dve.tensor_scalar(top[:, :], top[:, :], -1.0, None, ALU.mult), s["sum"])


def attention(nc, name, g, proj, y, pairs, q0, k0, v0, y0, rows=None, tri=None, ramps=None, rotary=None):
    lstm = rows is not None
    blocks = []
    for n in range(2):
        for sb in range(4 * n + 4):
            j0 = max(sb * P, 512 * n)
            blocks.append((n, sb, j0, 512 * (n + 1) - j0))
    steps = [(hh, *blk) for blk in blocks for hh in range(2)]
    last = {(hh, n): max(m for m, st in enumerate(steps) if st[:2] == (hh, n)) for hh in range(2) for n in range(2)}
    cv = 128 if lstm else 64
    with stage(nc, name, "const", "v_in", "k_in", "q_in", "mb_in", "em_in", "ck_in", "turned", "values", "arg",
               "weight", "score", "prob", "out", "own", "result", "stored", "one", "swapped", "times_cos",
               "rotated", "spread") as s:
        q, v = s.sb("q", [P, SEQ]), s.sb("v", [P, SEQ])
        k = None if lstm else s.sb("k", [P, SEQ])
        kz = [s.sb(f"k{hh}", [P, SEQ]) for hh in range(2)]
        vt = [s.sb(f"vt{hh}", [P, 8, cv]) for hh in range(2)]
        pr = [s.sb(f"p{b}", [P, 512]) for b in range(4)]
        res = [s.sb(f"res{hh}", [64, SEQ]) for hh in range(2)]
        sc = s.ps("score", [P, 4, 512])
        turned = sc[:, 0:2, :].rearrange("p n (b c) -> p (n b) c", c=P)
        o = s.ps("o", [P, 2, 2, 512])
        head = lambda t, hh: t[64 * hh:64 * hh + 64]
        if lstm:
            e = [s.sb(f"e{b}", [P, 512]) for b in range(4)]
            mb, em, ck = ([s.sb(f"{n}{hh}", [P, w]) for hh in range(2)]
                          for n, w in (("mb", SEQ), ("em", SEQ), ("ck", 8)))
            tr, den, rec = s.sb("tri", [P, 512]), s.sb("den", [P, 512]), s.sb("rec", [64, 512])
            consts = [(tr, tri)]
        else:
            mb = [s.sb(f"ramp{hh}", [P, SEQ]) for hh in range(2)]
            cos, sin, swap, part = s.sb("c", [P, SEQ]), s.sb("s", [P, SEQ]), s.sb("sw", [P, P]), s.sb("part", [P, SEQ])
            consts = list(zip((cos, sin, swap), rotary))
        with nc.Block() as block:
            @block.sync
            def _(sp):
                for t, src in consts:
                    sp.dma_start(t[:, :], src).then_inc(s["const"], 16)
                sp.wait_ge(s["const"], 16 * len(consts))

            @block.vector
            def _(dve):
                for hh in range(2):
                    dve.memset(head(kz[hh], 1 - hh), 0.0).then_inc(s["one"], 1)
                    if lstm:
                        dve.memset(vt[hh][:, :, 64:128], 1.0).then_inc(s["one"], 1)
        clear(nc, s)
        with nc.Fori(0, pairs) as i:
            with nc.Block() as block:
                @block.sync
                def _(sp):
                    loads = [(q, q0, P, "q_in"), (v, v0, P, "v_in")]
                    loads[1:1] = ([(head(kz[hh], hh), k0 + 64 * hh, 64, "k_in") for hh in range(2)] if lstm
                                  else [(k, k0, P, "k_in")])
                    for t, at, size, n in loads:
                        sp.dma_start(t[:, :], proj[ds(i * P + at, size), :]).then_inc(s[n], 16)
                    for hh in range(2):
                        if lstm:
                            row = lambda n: rows[ds(i * 2 + (n * 4 + hh), 1), :]
                            sp.dma_start(mb[hh][:, :], row(0).broadcast_to([P, SEQ])).then_inc(s["mb_in"], 16)
                            sp.dma_start(em[hh][64:128, :], row(1).broadcast_to([64, SEQ])).then_inc(s["em_in"], 16)
                            sp.dma_start(ck[hh][:, :], row(2).rearrange("a (s p) -> p (a s)", p=P),
                                         allow_slow_non_contiguous=True).then_inc(s["ck_in"], 16)
                        else:
                            sp.dma_start(mb[hh][:, :], ramps[ds(i * (2 * P) + hh * P, P), :]).then_inc(s["mb_in"], 16)
                    sp.wait_ge(s["result"], 4)
                    for hh in range(2):
                        sp.dma_start(y[ds(i * P + (y0 + 64 * hh), 64), :], res[hh][:, :]).then_inc(s["stored"], 16)
                    sp.wait_ge(s["stored"], 32)

                @block.tensor
                def _(pe):
                    if not lstm:
                        for n, (x, name_) in enumerate(((q, "q_in"), (k, "k_in"))):
                            pe.wait_ge(s[name_], 16)
                            for b in range(2):
                                mm = pe.matmul(o[:, n, b, :], swap[:, :], x[:, b * 512:b * 512 + 512],
                                               start=True, stop=True)
                            mm.then_inc(s["swapped"], 1)
                    pe.wait_ge(s["v_in"], 16)
                    for b in range(8):
                        mm = pe.transpose(turned[:, b, :], v[:, b * P:(b + 1) * P], g.ident[:, :])
                    mm.then_inc(s["turned"], 1)
                    if lstm:
                        pe.wait_ge(s["q_in"], 16)
                        pe.wait_ge(s["k_in"], 32)
                    else:
                        pe.wait_ge(s["rotated"], 2)
                        pe.wait_ge(s["spread"], 2)
                    pe.wait_ge(s["values"], 2)

                    def values(m):
                        hh, n, sb, j0, w = steps[m]
                        pe.wait_ge(s["prob"], m + 1)
                        pe.matmul(o[0:cv, hh, n, j0 - 512 * n:512], vt[hh][:, sb, :], pr[m % 4][:, 0:w],
                                  start=(sb == 0), stop=(m == last[hh, n])).then_inc(s["out"], 1)

                    for m, (hh, n, sb, j0, w) in enumerate(steps):
                        if m >= 4:
                            pe.wait_ge(s["prob"], m - 3)
                        pe.matmul(sc[:, m % 4, 0:w], kz[hh][:, sb * P:(sb + 1) * P], q[:, j0:j0 + w],
                                  start=True, stop=True).then_inc(s["score"], 1)
                        if m >= 2:
                            values(m - 2)
                    for m in (len(steps) - 2, len(steps) - 1):
                        values(m)

                if lstm:
                    @block.scalar
                    def _(act):
                        for m, (hh, n, sb, j0, w) in enumerate(steps):
                            act.wait_ge(s["arg"], m + 1)
                            act.activation(e[m % 4][:, 0:w], e[m % 4][:, 0:w], ACT.Exp).then_inc(s["weight"], 1)
                else:
                    @block.scalar
                    def _(act):
                        act.wait_ge(s["rotated"], 2)
                        for hh in range(2):
                            act.activation(head(kz[hh], hh), head(k, hh), ACT.Copy).then_inc(s["spread"], 1)

                    @block.gpsimd
                    def _(pool):
                        for n, x in enumerate((q, k)):
                            pool.wait_ge(s["swapped"], n + 1)
                            pool.tensor_tensor(x[:, :], x[:, :], cos[:, :], ALU.mult).then_inc(s["times_cos"], 1)

                @block.vector
                def _(dve):
                    link = chain(dve, s["own"])
                    if not lstm:
                        for n, x in enumerate((q, k)):
                            dve.wait_ge(s["swapped"], n + 1)
                            link(dve.tensor_tensor(halves(part[:, :]), o[:, n, :, :], halves(sin[:, :]), ALU.mult))
                            dve.wait_ge(s["times_cos"], n + 1)
                            link(dve.tensor_tensor(x[:, :], x[:, :], part[:, :], ALU.add), s["rotated"])
                    dve.wait_ge(s["turned"], 1)
                    for hh in range(2):
                        dve.tensor_copy(vt[hh][:, :, 0:64], turned[:, :, 64 * hh:64 * hh + 64])\
                           .then_inc(s["values"], 1)
                    dve.wait_ge(s["mb_in"], 32)
                    if lstm:
                        dve.wait_ge(s["ck_in"], 32)
                        dve.wait_ge(s["em_in"], 32)

                    def arg(m):
                        hh, n, sb, j0, w = steps[m]
                        if m >= 4:
                            dve.wait_ge(s["prob"], m - 3)
                        if j0 == sb * P:
                            ins = dve.scalar_tensor_tensor(e[m % 4][:, 0:w], mb[hh][:, j0:j0 + w],
                                                           ck[hh][:, sb:sb + 1], tr[:, 0:w], ALU.add, ALU.min)
                        else:
                            ins = dve.tensor_scalar(e[m % 4][:, 0:w], mb[hh][:, j0:j0 + w], ck[hh][:, sb:sb + 1], 0.0,
                                                    ALU.add, ALU.min)
                        ins.then_inc(s["arg"], 1)

                    def result(hh, n):
                        dve.wait_ge(s["out"], last[hh, n] + 1)
                        r = res[hh][:, 512 * n:512 * n + 512]
                        if lstm:
                            dn = den[64:128, :]
                            link(dve.scalar_tensor_tensor(dn, o[64:128, hh, n, :], -1.0,
                                                          em[hh][64:128, 512 * n:512 * n + 512], ALU.mult, ALU.max))
                            link(dve.tensor_tensor(dn, o[64:128, hh, n, :], dn, ALU.max))
                            link(dve.reciprocal(rec[:, :], den[64:128, :]))
                            dve.tensor_tensor(r, o[0:64, hh, n, :], rec[:, :], ALU.mult).then_inc(s["result"], 1)
                            dve.wait_ge(s["result"], 2 * n + hh + 1)
                        else:
                            dve.tensor_copy(r, o[0:64, hh, n, :]).then_inc(s["result"], 1)

                    if lstm:
                        arg(0)
                        arg(1)
                    due = {last[hh, n] + 3: (hh, n) for hh in range(2) for n in range(2)}
                    for m, (hh, n, sb, j0, w) in enumerate(steps):
                        if lstm and m + 2 < len(steps):
                            arg(m + 2)
                        dve.wait_ge(s["score"], m + 1)
                        if m >= 4:
                            dve.wait_ge(s["out"], m - 3)
                        if lstm:
                            dve.wait_ge(s["weight"], m + 1)
                            dve.scalar_tensor_tensor(pr[m % 4][:, 0:w], sc[:, m % 4, 0:w], 0.125,
                                                     e[m % 4][:, 0:w], ALU.mult, ALU.mult).then_inc(s["prob"], 1)
                        else:
                            at = j0 - sb * P
                            dve.tensor_tensor(pr[m % 4][:, 0:w], sc[:, m % 4, 0:w], mb[hh][:, at:at + w],
                                              ALU.mult).then_inc(s["prob"], 1)
                        if m in due:
                            result(*due[m])
                    for hh in range(2):
                        result(hh, 1)
            clear(nc, s)


def head_norm(nc, name, g, src, tiles, y0, eps, gate_rows, act_gate, center=True, gain=None, bias=None,
              extra=None, src2=None, per=3):
    names = ("x_in", "g_in", "e_in")
    with stage(nc, name, *[f"{n}{j}" for n in names for j in range(per)], "ready", "summed", "centred", "squared",
               "var", "logged", "rooted", "gate", "own", "par", "scaled", "eps", "out") as s:
        x, gt, sq = ([s.sb(f"{n}{j}", [P, SEQ]) for j in range(per)] for n in ("x", "gate", "sq"))
        ex = [s.sb(f"ex{j}", [P, SEQ]) for j in range(per)] if extra is not None or src2 is not None else None
        par, low = s.sb("par", [P, 2, per]), s.sb("eps", [P, 1])
        acc = s.ps("acc", [P, 2 * per, 512])
        bank = lambda j: acc[:, 2 * j:2 * j + 2, :]
        other = extra if extra is not None else src2
        with nc.Block() as block:
            @block.vector
            def _(dve):
                dve.memset(low[:, :], eps).then_inc(s["eps"], 1)
                dve.wait_ge(s["eps"], 1)
        clear(nc, s)
        with nc.Fori(0, tiles // per) as i:
            at = lambda j: i * (per * P) + j * P
            with nc.Block() as block:
                @block.sync
                def _(sp):
                    for j in range(per):
                        sp.dma_start(x[j][:, :], src[ds(at(j) + (y0 * P if src2 is None else 0), P), :])\
                          .then_inc(s[f"x_in{j}"], 16)
                        if other is not None:
                            sp.dma_start(ex[j][:, :], other[ds(at(j), P), :]).then_inc(s[f"e_in{j}"], 16)
                        sp.dma_start(gt[j][:, :], gate_rows[0][ds(at(j) + gate_rows[1] * P, P), :])\
                          .then_inc(s[f"g_in{j}"], 16)

                @block.tensor
                def _(pe):
                    def mean(j, of):
                        for b in range(2):
                            mm = pe.matmul(bank(j)[:, b, :], g.mean64[:, :], of[:, b * 512:b * 512 + 512],
                                           start=True, stop=True)
                        return mm

                    if center:
                        for j in range(per):
                            pe.wait_ge(s[f"x_in{j}"], 16)
                            mean(j, x[j]).then_inc(s["summed"], 1)
                    for j in range(per):
                        pe.wait_ge(s["squared"], j + 1)
                        mean(j, sq[j]).then_inc(s["var"], 1)

                @block.vector
                def _(dve):
                    if gain is not None:
                        dve.tensor_copy(par[:, 0, :], g.par[:, ds(i * per + g.col[gain], per)]).then_inc(s["par"], 1)
                    if bias is not None:
                        dve.tensor_copy(par[:, 1, :], g.par[:, ds(i * per + g.col[bias], per)]).then_inc(s["par"], 1)
                    for j in range(per):
                        if src2 is not None:
                            dve.wait_ge(s[f"x_in{j}"], 16)
                            dve.wait_ge(s[f"e_in{j}"], 16)
                            dve.tensor_tensor(x[j][:, :], x[j][:, :], ex[j][:, :], ALU.add).then_inc(s["centred"], 1)
                        else:
                            dve.wait_ge(s["summed"], j + 1)
                            dve.tensor_tensor(halves(x[j][:, :]), halves(x[j][:, :]), bank(j), ALU.subtract)\
                               .then_inc(s["centred"], 1)
                    if gain is not None:
                        dve.wait_ge(s["par"], 1 if bias is None else 2)
                    for j in range(per):
                        dve.wait_ge(s["rooted"], j + 1)
                        if gain is not None:
                            ins = dve.scalar_tensor_tensor(x[j][:, :], x[j][:, :], par[:, 0, j:j + 1], sq[j][:, :],
                                                           ALU.mult, ALU.mult)
                        else:
                            ins = dve.tensor_tensor(x[j][:, :], x[j][:, :], sq[j][:, :], ALU.mult)
                        if extra is not None:
                            ins.then_inc(s["own"], 1)
                            dve.wait_ge(s["own"], j + 1)
                            dve.wait_ge(s[f"e_in{j}"], 16)
                            ins = dve.scalar_tensor_tensor(x[j][:, :], x[j][:, :], par[:, 1, j:j + 1], ex[j][:, :],
                                                           ALU.add, ALU.add)
                        ins.then_inc(s["scaled"], 1)

                @block.gpsimd
                def _(pool):
                    for j in range(per):
                        pool.wait_ge(s["scaled"], j + 1)
                        pool.wait_ge(s["gate"], j + 1)
                        pool.tensor_tensor(g.y[:, ds(i * per + (y0 + j), 1), 0:SEQ], x[j][:, None, :],
                                           gt[j][:, None, :], ALU.mult).then_inc(s["out"], 1)

                @block.scalar
                def _(act):
                    for j in range(per):
                        act.wait_ge(s["centred"], j + 1)
                        act.activation(sq[j][:, :], x[j][:, :], ACT.Square).then_inc(s["squared"], 1)
                    for j in range(per):
                        act.wait_ge(s["var"], j + 1)
                        act.activation(halves(sq[j][:, :]), bank(j), ACT.Ln, bias=low[:, 0:1])\
                           .then_inc(s["logged"], 1)
                    for j in range(per):
                        act.wait_ge(s["logged"], j + 1)
                        act.activation(sq[j][:, :], sq[j][:, :], ACT.Exp, scale=-0.5).then_inc(s["rooted"], 1)
                    for j in range(per):
                        act.wait_ge(s[f"g_in{j}"], 16)
                        act.activation(gt[j][:, :], gt[j][:, :], act_gate).then_inc(s["gate"], 1)
            clear(nc, s)


W_PAR = 8


def shifted(link, dve, x, d, mu, out, sem=None):
    link(dve.tensor_tensor(d, x[:, 0:SEQ], x[:, 1:SEQ + 1], ALU.subtract))
    link(dve.scalar_tensor_tensor(out, d, mu, x[:, 1:SEQ + 1], ALU.mult, ALU.add), sem)


def rwkv_inputs(nc, g, a, proj, rw, gate, extra):
    with stage(nc, "wp", "const", "zero", "loaded", "shift", "own", "tanh", "sig", "proj", "sw", "sa", "g_out",
               "cum", "ep", "en", "diff", "el", "sqkk", "normed", "length", "logged", "rooted", "prod", "extra",
               "stored", "r_done", "k_done", "v_done", "p_out", "pown") as s:
        x = [s.sb(f"x{n}", [P, 1 + SEQ]) for n in range(3)]
        d, dv, wa, gl = (s.sb(n, [P, SEQ]) for n in ("d", "dv", "wal", "gll"))
        lora = [s.sb(f"lora{n}", [P, P]) for n in range(3)]
        par, reset = s.sb("par", [P, W_PAR]), s.sb("reset", [P, SEQ])
        r, k, av, lw, cum, eP, eN = (s.sb(n, [P, SEQ]) for n in ("r", "k", "a", "lw", "cum", "eP", "eN"))
        acc = s.ps("acc", [P, 8, 512])
        with nc.Block() as block:
            @block.sync
            def _(sp):
                sp.dma_start(reset[:, :], a["reset"]).then_inc(s["const"], 16)
                sp.wait_ge(s["zero"], 3)
                sp.dma_start(x[0][:, 1:], proj[W_WA * P:W_WA * P + P, :]).then_inc(s["loaded"], 16)
                sp.dma_start(x[1][:, 1:], proj[W_GL * P:W_GL * P + P, :]).then_inc(s["loaded"], 16)
                sp.wait_ge(s["const"], 16)

            @block.vector
            def _(dve):
                link = chain(dve, s["own"])
                for n in range(3):
                    link(dve.memset(x[n][:, 0:1], 0.0), s["zero"])
                dve.wait_ge(s["loaded"], 32)
                c = g.col["wmu"]
                shifted(link, dve, x[0], d[:, :], g.par[:, c:c + 1], wa[:, :], s["shift"])
                shifted(link, dve, x[1], d[:, :], g.par[:, c + 1:c + 2], gl[:, :], s["shift"])

            @block.scalar
            def _(act):
                act.wait_ge(s["shift"], 1)
                act.activation(wa[0:64, :], wa[0:64, :], ACT.Tanh).then_inc(s["tanh"], 1)
                act.wait_ge(s["shift"], 2)
                act.activation(gl[:, :], gl[:, :], ACT.Sigmoid).then_inc(s["sig"], 1)
        clear(nc, s)
        with nc.Fori(0, 3) as i:
            with nc.Block() as block:
                @block.sync
                def _(sp):
                    for n, name in enumerate(("w_up", "a_up", "g_up")):
                        sp.dma_start(lora[n][:, :], a[name][ds(i * P, P), :]).then_inc(s["const"], 16)
                    for n, t in enumerate((W_R, W_K, W_V)):
                        sp.dma_start(x[n][:, 1:], proj[ds(i * P + t * P, P), :]).then_inc(s["loaded"], 16)
                    sp.wait_ge(s["g_out"], 1)
                    sp.dma_start(gate[ds(i * P, P), :], cum[:, :]).then_inc(s["stored"], 16)
                    sp.wait_ge(s["extra"], 1)
                    sp.dma_start(extra[ds(i * P, P), :], lw[:, :]).then_inc(s["stored"], 16)
                    sp.wait_ge(s["stored"], 32)

                @block.tensor
                def _(pe):
                    pe.wait_ge(s["const"], 48)
                    for n, src in enumerate((wa, wa, gl)):
                        for j in range(2):
                            mm = pe.matmul(acc[:, 2 * n + j, :], lora[n][:, :], src[:, j * 512:j * 512 + 512],
                                           start=True, stop=True)
                        mm.then_inc(s["proj"], 1)
                    for sem in (s["sqkk"], s["prod"]):
                        pe.wait_ge(sem, 1)
                        for j in range(2):
                            mm = pe.matmul(acc[:, 6 + j, :], g.mean64[:, :], d[:, j * 512:j * 512 + 512],
                                           start=True, stop=True)
                        mm.then_inc(s["normed"], 1)

                @block.scalar
                def _(act):
                    act.wait_ge(s["loaded"], 48)
                    act.wait_ge(s["shift"], 1)
                    act.wait_ge(s["proj"], 1)
                    act.activation(halves(lw[:, :]), acc[:, 0:2, :], ACT.Sigmoid, bias=par[:, 3:4]).then_inc(s["sw"], 1)
                    act.wait_ge(s["proj"], 2)
                    act.activation(halves(av[:, :]), acc[:, 2:4, :], ACT.Sigmoid, bias=par[:, 4:5]).then_inc(s["sa"], 1)
                    act.wait_ge(s["cum"], 1)
                    act.activation(eP[:, :], cum[:, :], ACT.Exp).then_inc(s["ep"], 1)
                    act.activation(eN[:, :], cum[:, :], ACT.Exp, scale=-1.0).then_inc(s["en"], 1)
                    act.wait_ge(s["diff"], 1)
                    act.activation(lw[:, :], lw[:, :], ACT.Exp).then_inc(s["el"], 1)
                    act.wait_ge(s["proj"], 3)
                    act.wait_ge(s["en"], 1)
                    act.activation(halves(cum[:, :]), acc[:, 4:6, :], ACT.Copy).then_inc(s["g_out"], 1)
                    act.wait_ge(s["length"], 1)
                    rsqrt(act, s, d[:, :], 1)

                @block.gpsimd
                def _(pool):
                    link = chain(pool, s["pown"])
                    tt = pool.tensor_tensor
                    at = lambda t: t[:, ds(i, 1), :]
                    one = lambda t: t[:, None, :]
                    pool.wait_ge(s["loaded"], 48)
                    pool.wait_ge(s["shift"], 1)
                    link(tt(dv[:, :], x[2][:, 0:SEQ], x[2][:, 1:], ALU.subtract))
                    link(tt(dv[:, :], dv[:, :], par[:, 2:3].broadcast_to([P, SEQ]), ALU.mult))
                    link(tt(at(rw.arrays["v"]), one(dv), x[2][:, None, 1:], ALU.add), s["v_done"])
                    pool.wait_ge(s["k_done"], 1)
                    pool.wait_ge(s["en"], 1)
                    tt(at(rw.arrays["kappa"]), x[1][:, None, 1:], one(eN), ALU.mult).then_inc(s["p_out"], 1)
                    pool.wait_ge(s["ep"], 1)
                    pool.wait_ge(s["r_done"], 1)
                    tt(at(rw.arrays["rho"]), one(r), one(eP), ALU.mult).then_inc(s["p_out"], 1)

                @block.vector
                def _(dve):
                    link = chain(dve, s["own"])
                    at = lambda t: t[:, ds(i, 1), :]
                    one = lambda t: t[:, None, :]
                    link(dve.tensor_copy(par[:, :], g.par[:, ds(i * W_PAR + g.col["w"], W_PAR)]), s["shift"])
                    dve.wait_ge(s["loaded"], 48)
                    shifted(link, dve, x[0], d[:, :], par[:, 0:1], r[:, :], s["r_done"])
                    shifted(link, dve, x[1], d[:, :], par[:, 1:2], k[:, :])
                    dve.wait_ge(s["sw"], 1)
                    link(dve.tensor_scalar(lw[:, :], lw[:, :], -float(np.exp(-0.5)), None, ALU.mult))
                    link(dve.tensor_tensor_scan(cum[:, :], reset[:, :], lw[:, :], 0.0, ALU.mult, ALU.add), s["cum"])
                    link(dve.tensor_tensor(lw[:, :], cum[:, :], lw[:, :], ALU.subtract), s["diff"])
                    kk, k2 = x[0][:, 1:], x[1][:, 1:]
                    link(dve.tensor_scalar(kk, k[:, :], par[:, 5:6], None, ALU.mult))
                    link(dve.tensor_tensor(d[:, :], kk, kk, ALU.mult), s["sqkk"])
                    dve.wait_ge(s["sa"], 1)
                    link(dve.tensor_scalar(k2, av[:, :], -1.0, par[:, 6:7], ALU.add, ALU.mult))
                    link(dve.scalar_tensor_tensor(k2, k2, 1.0, k[:, :], ALU.add, ALU.mult), s["k_done"])
                    dve.wait_ge(s["normed"], 1)
                    dve.tensor_scalar(halves(d[:, :]), acc[:, 6:8, :], 64.0 * 2.0 ** 20, 1e-24 * 2.0 ** 20,
                                      ALU.mult, ALU.max).then_inc(s["length"], 1)
                    dve.wait_ge(s["rooted"], 1)
                    link(dve.scalar_tensor_tensor(kk, kk, 2.0 ** 10, d[:, :], ALU.mult, ALU.mult))
                    dve.wait_ge(s["el"], 1)
                    link(dve.tensor_tensor(at(rw.arrays["alpha"]), x[0][:, None, 1:], one(lw), ALU.mult))
                    link(dve.tensor_tensor(kk, kk, av[:, :], ALU.mult))
                    dve.wait_ge(s["ep"], 1)
                    dve.wait_ge(s["en"], 1)
                    link(dve.scalar_tensor_tensor(at(rw.arrays["beta"]), x[0][:, None, 1:], -1.0, one(eN),
                                                  ALU.mult, ALU.mult))
                    link(dve.tensor_copy(rw.last[:, ds(i, 1), :], eP[:, None, CH - 1::CH]))
                    link(dve.scalar_tensor_tensor(d[:, :], r[:, :], par[:, 7:8], k2, ALU.mult, ALU.mult), s["prod"])
                    dve.wait_ge(s["normed"], 2)
                    link(dve.tensor_scalar(halves(lw[:, :]), acc[:, 6:8, :], 64.0, None, ALU.mult))
                    dve.wait_ge(s["v_done"], 1)
                    link(dve.tensor_tensor(one(lw), one(lw), at(rw.arrays["v"]), ALU.mult), s["extra"])
            clear(nc, s)


def spread(link, eng, out, src, at, sem):
    link(eng.tensor_copy(out[0:64, :, 0:64], src[0:64, :, ds(at, CH)]), sem)
    link(eng.tensor_copy(out[64:P, :, 64:P], src[64:P, :, ds(at, CH)]), sem)


HEAD = (slice(0, 64), slice(64, P))


def rwkv_chunks(nc, g, a, rw, out):
    N, U = 3, 4
    names = ("al", "be", "ka", "v", "gram", "x_low", "x1", "xt1", "at", "d_t", "b_bd", "c_t", "k_t", "b_t", "v_d",
             "v_t", "bv", "kv", "mk", "y_done", "yp", "x_done", "x_new", "xt_done", "xt_new")
    with stage(nc, "wc", *[f"{n}{u}" for u in range(U) for n in names], "const", "zero", "zero_p", "own", "pown",
               "plc", "rhs", "rhs_s", "z", "z_s", "z_bd", "s_mm", "s_new", "s_bd", "yo", "tok", "stored") as s:
        low, upp = s.sb("low", [P, P]), s.sb("upp", [P, 8, CH])
        units = []
        for u in range(U):
            t = Shared()
            t.s = {n: s[f"{n}{u}"] for n in names}
            t.al, t.be, t.ka, t.v, t.B, t.kT, t.bT, t.Vd, t.X, t.XT, t.yp, t.mk = (
                s.sb(n + str(u), [P, N, P]) for n in ("al", "be", "ka", "v", "B", "kT", "bT", "Vd", "X", "XT",
                                                      "yp", "mk"))
            t.ATc, t.CT, t.DT, t.V, t.BV, t.kV = (
                s.sb(n + str(u), [P, N, CH]) for n in ("ATc", "CT", "DT", "V", "BV", "kV"))
            t.b = [s.ps(f"b{n}_{u}", [P, 512]) for n in range(2)]
            t.wide = lambda n, t=t: t.b[n][:, 0:N * P].rearrange("p (n c) -> p n c", n=N)
            t.half = lambda n, h, t=t: t.b[n][:, h * N * CH:(h + 1) * N * CH].rearrange("p (n c) -> p n c", n=N)
            t.two = lambda n, t=t: t.b[n][:, 0:N * P].rearrange("p (n b c) -> p n b c", n=N, b=2)
            units.append(t)
        rhs, Z, S, SkV = (s.sb(n, [P, N, CH]) for n in ("rhs", "Z", "S", "SkV"))
        Zd, Sd = ([s.sb(n + str(b), [P, N, P]) for b in range(2)] for n in ("Zd", "Sd"))
        plc = s.sb("plc", [P, N, U])
        yT = s.sb("yT", [P, N, U * CH])
        m_ = lambda k: upp[:, k:k + 1, :].broadcast_to([P, N, CH])
        mh = lambda k, r: upp[r, k:k + 1, :].broadcast_to([64, N, CH])
        idb = g.ident[:, None, :].broadcast_to([P, N, P])
        arr = rw.arrays
        every = lambda: enumerate(units)
        with nc.Block() as block:
            @block.sync
            def _(sp):
                for r in HEAD:
                    sp.dma_start(upp[r, :, :], a["upp"].rearrange("p (k c) -> p k c", k=8)[r, :, r])\
                      .then_inc(s["const"], 16)
                sp.dma_start(low[:, :], a["low"][:, 0:P]).then_inc(s["const"], 16)
                sp.wait_ge(s["const"], 48)

            @block.vector
            def _(dve):
                for t in units:
                    for x in (t.al, t.be, t.ka, t.v):
                        dve.memset(x[:, :, :], 0.0).then_inc(s["zero"], 1)
                for x in (S, *Zd):
                    dve.memset(x[:, :, :], 0.0).then_inc(s["zero"], 1)

            @block.gpsimd
            def _(pool):
                for t in units:
                    for x in (t.B, t.XT, t.mk):
                        pool.memset(x[:, :, :], 0.0).then_inc(s["zero_p"], 1)
                for x in Sd:
                    pool.memset(x[:, :, :], 0.0).then_inc(s["zero_p"], 1)
        clear(nc, s)
        with nc.Block() as block:
            @block.sync
            def _(sp):
                sp.sem_inc(s["stored"], 16)
        with nc.Fori(0, NCH // U) as i:
            at = lambda u: i * (U * CH) + u * CH
            with nc.Block() as block:
                @block.gpsimd
                def _(pool):
                    link = chain(pool, s["pown"])
                    for u, t in every():
                        spread(link, pool, t.ka, arr["kappa"], at(u), t.s["ka"])
                    for u, t in every():
                        spread(link, pool, t.v, arr["v"], at(u), t.s["v"])
                    link(pool.tensor_copy(plc[:, :, :], rw.last[:, :, ds(i * U, U)]), s["plc"])
                    for lev in range(1, 6):
                        for u, t in every():
                            if lev == 1:
                                pool.wait_ge(t.s["at"], 1)
                            else:
                                pool.wait_ge(t.s["y_done"], lev - 1)
                            for r in HEAD:
                                link(pool.tensor_tensor(t.mk[r, :, r], t.ATc[r, :, :], mh(lev, r), ALU.mult),
                                     t.s["mk"])

                @block.tensor
                def _(pe):
                    def each(out, lhsT, rhs_, sem):
                        for p in range(N):
                            mm = pe.matmul(out[:, p], lhsT[:, p, :], rhs_(p), start=True, stop=True)
                        mm.then_inc(sem, 1)

                    def turn(out, x, sem):
                        for p in range(N):
                            mm = pe.transpose(out[:, p, :], x[:, p, :], g.ident[:, :])
                        mm.then_inc(sem, 1)

                    of = lambda x: (lambda p: x[:, p, :])
                    both = lambda u: (lambda p: rw.all[:, 0:2, p, ds(at(u), CH)])
                    for u, t in every():
                        pe.wait_ge(t.s["al"], 2)
                        pe.wait_ge(t.s["be"], 2)
                        each(t.wide(0), t.al, of(t.be), t.s["gram"])
                        each(t.two(1), t.be, both(u), t.s["gram"])
                    for u, t in every():
                        pe.wait_ge(t.s["x_low"], 1)
                        pe.wait_ge(t.s["ka"], 2)
                        each(t.two(0), t.ka, both(u), t.s["gram"])
                        pe.wait_ge(t.s["at"], 1)
                        pe.wait_ge(t.s["d_t"], 1)
                        turn(t.wide(1), t.ka, t.s["gram"])
                    for u, t in every():
                        pe.wait_ge(t.s["b_bd"], 2)
                        pe.wait_ge(t.s["c_t"], 1)
                        turn(t.wide(0), t.be, t.s["gram"])
                        pe.wait_ge(t.s["v"], 2)
                        pe.wait_ge(t.s["k_t"], 1)
                        turn(t.wide(1), t.v, t.s["gram"])
                    for u, t in every():
                        pe.wait_ge(t.s["b_t"], 1)
                        pe.wait_ge(t.s["v_t"], 2)
                        each(t.half(0, 0), t.B, of(t.V), t.s["gram"])
                        each(t.half(1, 0), t.kT, of(t.V), t.s["gram"])
                    for lev in range(1, 6):
                        for u, t in every():
                            pe.wait_ge(t.s["mk"], 2 * lev)
                            if lev == 1:
                                pe.wait_ge(t.s["bv"], 1)
                                pe.wait_ge(t.s["x1"], 1)
                            else:
                                pe.wait_ge(t.s["x_new"], lev - 1)
                                pe.wait_ge(t.s["xt_new"], lev - 1)
                            each(t.wide(0), t.mk, of(t.X), t.s["y_done"])
                        for u, t in every():
                            pe.wait_ge(t.s["yp"], lev)
                            if lev == 1:
                                pe.wait_ge(t.s["kv"], 1)
                                pe.wait_ge(t.s["xt1"], 1)
                            if lev < 5:
                                each(t.wide(1), t.XT, of(t.yp), t.s["x_done"])
                            each(t.wide(0), t.yp, of(t.XT), t.s["xt_done"])

                    def outputs(c):
                        t = units[c]
                        pe.wait_ge(s["z_bd"], 2 * c + 2)
                        if c > 0:
                            pe.wait_ge(s["s_bd"], 2 * c)
                        for p in range(N):
                            o = t.half(1, 1)[:, p, :]
                            pe.matmul(o, t.Vd[:, p, :], t.CT[:, p, :], start=True, stop=False)
                            pe.matmul(o, Sd[c % 2][:, p, :], arr["rho"][:, p, ds(at(c), CH)], start=False, stop=False)
                            mm = pe.matmul(o, Zd[c % 2][:, p, :], t.DT[:, p, :], start=False, stop=True)
                        mm.then_inc(s["yo"], 1)

                    for c, t in every():
                        pe.wait_ge(t.s["xt_new"], 5)
                        if c > 0:
                            pe.wait_ge(s["s_new"], c)
                        each(t.half(0, 0), t.al, of(S), s["rhs"])
                        if c > 0:
                            outputs(c - 1)
                        pe.wait_ge(s["rhs_s"], c + 1)
                        each(t.half(1, 0), t.XT, of(rhs), s["z"])
                        pe.wait_ge(s["z_s"], c + 1)
                        each(t.half(0, 1), t.bT, of(Z), s["s_mm"])
                    outputs(U - 1)

                @block.vector
                def _(dve):
                    link = chain(dve, s["own"])
                    tt = dve.tensor_tensor
                    for u, t in every():
                        for r in HEAD:
                            dve.tensor_copy(t.al[r, :, r], arr["alpha"][r, :, ds(at(u), CH)]).then_inc(t.s["al"], 1)
                    for u, t in every():
                        dve.wait_ge(t.s["gram"], 1)
                        tt(t.X[:, :, :], t.wide(0), low[:, None, :].broadcast_to([P, N, P]), ALU.mult)\
                          .then_inc(t.s["x_low"], 1)
                        dve.wait_ge(t.s["at"], 1)
                        tt(t.DT[:, :, :], t.two(1)[:, :, 1, :], m_(7), ALU.mult).then_inc(t.s["d_t"], 1)
                    for u, t in every():
                        dve.wait_ge(t.s["gram"], 3)
                        for r in HEAD:
                            tt(t.B[r, :, r], t.two(0)[r, :, 0, :], mh(6, r), ALU.mult).then_inc(t.s["b_bd"], 1)
                        tt(t.CT[:, :, :], t.two(0)[:, :, 1, :], m_(7), ALU.mult).then_inc(t.s["c_t"], 1)
                        dve.wait_ge(t.s["x_low"], 1)
                        tt(t.X[:, :, :], t.X[:, :, :], idb, ALU.add).then_inc(t.s["x1"], 1)
                        for r in HEAD:
                            ins = tt(t.XT[r, :, r], t.ATc[r, :, :], mh(0, r), ALU.mult)
                            link(ins)
                        tt(t.XT[:, :, :], t.XT[:, :, :], idb, ALU.add).then_inc(t.s["xt1"], 1)
                    for u, t in every():
                        dve.wait_ge(t.s["gram"], 7)
                        dve.tensor_copy(t.BV[:, :, :], t.half(0, 0)).then_inc(t.s["bv"], 1)
                    for lev in range(1, 6):
                        for u, t in every():
                            dve.wait_ge(t.s["y_done"], lev)
                            if lev > 1:
                                dve.wait_ge(t.s["xt_done"], lev - 1)
                            tt(t.yp[:, :, :], t.wide(0), idb, ALU.add).then_inc(t.s["yp"], 1)
                    dve.wait_ge(s["plc"], 1)
                    for c, t in every():
                        dve.wait_ge(t.s["kv"], 1)
                        dve.wait_ge(t.s["bv"], 1)
                        link(tt(SkV[:, :, :], S[:, :, :], t.kV[:, :, :], ALU.add))
                        dve.wait_ge(s["rhs"], c + 1)
                        tt(rhs[:, :, :], t.half(0, 0), t.BV[:, :, :], ALU.add).then_inc(s["rhs_s"], 1)
                        dve.wait_ge(s["z"], c + 1)
                        if c > 0:
                            dve.wait_ge(s["z_bd"], 2 * c)
                            dve.wait_ge(s["s_bd"], 2 * c)
                        dve.tensor_copy(Z[:, :, :], t.half(1, 0)).then_inc(s["z_s"], 1)
                        dve.wait_ge(s["s_mm"], c + 1)
                        link(tt(S[:, :, :], SkV[:, :, :], t.half(0, 1), ALU.add))
                        link(tt(S[:, :, :], S[:, :, :], plc[:, :, c:c + 1].broadcast_to([P, N, CH]), ALU.mult),
                             s["s_new"])

                @block.scalar
                def _(act):
                    def copy(out, src, sem):
                        act.activation(out, src, ACT.Copy).then_inc(sem, 1)

                    for u, t in every():
                        for r in HEAD:
                            copy(t.be[r, :, r], arr["beta"][r, :, ds(at(u), CH)], t.s["be"])
                    for u, t in every():
                        act.wait_ge(t.s["gram"], 2)
                        copy(t.ATc[:, :, :], t.two(1)[:, :, 0, :], t.s["at"])
                    for u, t in every():
                        act.wait_ge(t.s["gram"], 4)
                        copy(t.kT[:, :, :], t.wide(1), t.s["k_t"])
                    for u, t in every():
                        act.wait_ge(t.s["gram"], 5)
                        copy(t.bT[:, :, :], t.wide(0), t.s["b_t"])
                        act.wait_ge(t.s["gram"], 6)
                        copy(t.Vd[:, :, :], t.wide(1), t.s["v_d"])
                        for r in HEAD:
                            copy(t.V[r, :, :], t.wide(1)[r, :, r], t.s["v_t"])
                    for u, t in every():
                        act.wait_ge(t.s["gram"], 8)
                        copy(t.kV[:, :, :], t.half(1, 0), t.s["kv"])
                    for lev in range(1, 6):
                        for u, t in every():
                            if lev < 5:
                                act.wait_ge(t.s["x_done"], lev)
                                copy(t.X[:, :, :], t.wide(1), t.s["x_new"])
                            act.wait_ge(t.s["xt_done"], lev)
                            copy(t.XT[:, :, :], t.wide(0), t.s["xt_new"])

                    def collect(c):
                        if c == 0:
                            act.wait_ge(s["stored"], i * 16 + 16)
                        act.wait_ge(s["yo"], c + 1)
                        act.activation(yT[:, :, c * CH:c * CH + CH], units[c].half(1, 1), ACT.Copy)\
                           .then_inc(s["tok"], 1)

                    for c in range(U):
                        act.wait_ge(s["z_s"], c + 1)
                        for r in HEAD:
                            copy(Zd[c % 2][r, :, r], Z[r, :, :], s["z_bd"])
                        if c > 0:
                            collect(c - 1)
                        act.wait_ge(s["s_new"], c + 1)
                        for r in HEAD:
                            copy(Sd[(c + 1) % 2][r, :, r], S[r, :, :], s["s_bd"])
                    collect(U - 1)

                @block.sync
                def _(sp):
                    sp.wait_ge(s["tok"], U)
                    sp.dma_start(out[:, ds(i * (U * CH), U * CH)].rearrange("(k p) t -> p k t", p=P),
                                 yT[:, :, :]).then_inc(s["stored"], 16)
            clear(nc, s, keep="stored")
        with nc.Block() as block:
            @block.sync
            def _(sp):
                sp.wait_ge(s["stored"], 16 * (NCH // U + 1))


def block2(nc, g, a, dram):
    proj, y = dram("proj2", (TILES_2 * P, SEQ)), dram("mixed2", (D, SEQ))
    rows, gate, extra = dram("rows2", (12, SEQ)), dram("gate2", (3 * P, SEQ)), dram("extra2", (3 * P, SEQ))
    with g.parts("a2"):
        norm_h(nc, "n2", g, g.col["g2"], SEQ)
        dense(nc, "in2", g, a["w_in_2"], TILES_2, SEQ, proj, conv=(M_V, 4, 3, "mconv"))
    mlstm_gates(nc, g, proj, rows)
    attention(nc, "ml", g, proj, y, 2, M_Q * P, M_K * P, M_V * P, 0, rows=rows, tri=a["tri"])
    attention(nc, "rt", g, proj, y, 3, R_Q * P, R_K * P, R_V * P, 2 * P, ramps=a["ramps"],
              rotary=(a["cos"], a["sin"], a["swap"]))
    with ExitStack() as ctx:
        rw = Shared()
        rw.all = ctx.enter_context(nc.sbuf_tensor("rw_all", [P, 5, 3, SEQ], F32))
        rw.arrays = {n: rw.all[:, k, :, :] for k, n in enumerate(("alpha", "rho", "beta", "kappa", "v"))}
        rw.last = ctx.enter_context(nc.sbuf_tensor("rw_last", [P, 3, NCH], F32))
        rwkv_inputs(nc, g, a, proj, rw, gate, extra)
        rwkv_chunks(nc, g, a, rw, y[5 * P:8 * P, :])
    with nc.sbuf_tensor("y2", [P, KD, SEQ], F32) as y_sb:
        g.y = y_sb
        head_norm(nc, "hm", g, y, 2, 0, 1e-5, (proj, M_O), ACT.Sigmoid, gain="mln", per=2)
        head_norm(nc, "hr", g, y, 3, 2, 1e-5, (proj, R_G), ACT.Silu)
        head_norm(nc, "hw", g, y, 3, 5, 64e-5, (gate, 0), ACT.Copy, gain="wlng", bias="wlnb", extra=extra)
        with g.parts("b2"):
            split_u(nc, "su2", g)
            dense(nc, "out2", g, a["w_out_2"], KD, SEQ)
    with g.parts("c2"):
        norm_h(nc, "nm2", g, g.col["gm2"], SEQ)
        ffn(nc, "ff2", g, a["w_gu_2"], a["w_down_2"], [(2, 8), (1, 6)], SEQ, gated=True)
    norm_h(nc, "nf2", g, g.col["gf2"], SEQ, dest="h")


def split_u(nc, name, g):
    with stage(nc, name, "upper", "lower") as s:
        with nc.Block() as block:
            @block.scalar
            def _(act):
                for k in range(KD):
                    act.activation(g.uhi[:, k, 0:SEQ], g.y[:, k, 0:SEQ], ACT.Copy).then_inc(s["upper"], 1)

            @block.vector
            def _(dve):
                for k in range(KD):
                    dve.wait_ge(s["upper"], k + 1)
                    dve.tensor_tensor(g.ulo[:, k, 0:SEQ], g.y[:, k, 0:SEQ], g.uhi[:, k, 0:SEQ].bitcast(F32),
                                      ALU.subtract).then_inc(s["lower"], 1)


def unit_heads(nc, g, proj, gd):
    tiles = [(gd.k, G_K, j, 1.0) for j in range(4)] + [(gd.q, G_Q, j, 0.125) for j in range(4)]
    with stage(nc, "uh", *[f"in{n}" for n in range(8)], "v_in", "eps", "squared", "summed", "logged", "rooted",
               "out") as s:
        sq = [s.sb(f"sq{j}", [P, SEQ]) for j in range(4)]
        low = s.sb("eps", [P, 1])
        acc = s.ps("acc", [P, 8, 512])
        bank = lambda n: acc[:, 2 * (n % 4):2 * (n % 4) + 2, :]
        rows = lambda at: proj[at * P:(at + 1) * P, :]
        with nc.Block() as block:
            @block.sync
            def _(sp):
                for n, (out, row, j, _) in enumerate(tiles):
                    sp.dma_start(out[:, j, :], rows(row + j)).then_inc(s[f"in{n}"], 16)
                sp.dma_start(gd.v, proj[G_V * P:G_Z * P, :].rearrange("(k p) t -> p k t", p=P))\
                  .then_inc(s["v_in"], 16)
                sp.wait_ge(s["v_in"], 16)

            @block.scalar
            def _(act):
                act.wait_ge(s["eps"], 1)
                for half in range(2):
                    now = list(enumerate(tiles))[4 * half:4 * half + 4]
                    for n, (out, _, j, _) in now:
                        act.wait_ge(s[f"in{n}"], 16)
                        if half:
                            act.wait_ge(s["out"], n - 3)
                        act.activation(sq[n % 4][:, :], out[:, j, :], ACT.Square).then_inc(s["squared"], 1)
                    for n, _ in now:
                        act.wait_ge(s["summed"], n + 1)
                        act.activation(halves(sq[n % 4][:, :]), bank(n), ACT.Ln, scale=64.0, bias=low[:, 0:1])\
                           .then_inc(s["logged"], 1)
                    for n, _ in now:
                        act.wait_ge(s["logged"], n + 1)
                        act.activation(sq[n % 4][:, :], sq[n % 4][:, :], ACT.Exp, scale=-0.5)\
                           .then_inc(s["rooted"], 1)

            @block.tensor
            def _(pe):
                for n in range(8):
                    pe.wait_ge(s["squared"], n + 1)
                    for b in range(2):
                        mm = pe.matmul(bank(n)[:, b, :], g.mean64[:, :], sq[n % 4][:, b * 512:b * 512 + 512],
                                       start=True, stop=True)
                    mm.then_inc(s["summed"], 1)

            @block.vector
            def _(dve):
                dve.memset(low[:, :], EPS).then_inc(s["eps"], 1)
                for n, (out, _, j, scale) in enumerate(tiles):
                    dve.wait_ge(s["rooted"], n + 1)
                    dve.scalar_tensor_tensor(out[:, j, :], out[:, j, :], scale, sq[n % 4][:, :],
                                             ALU.mult, ALU.mult).then_inc(s["out"], 1)


GK = 6


def gdn_gates(nc, g, proj, gd):
    with stage(nc, "gg", "loaded", "own", "abs", "power", "log", "alog", "sig", "decay", "turned", "tok", "sum",
               "exps", "arg") as s:
        x, l = s.sb("x", [48, SEQ]), s.sb("l", [16, SEQ])
        ea = s.sb("ea", [16, 1])
        low, upp = s.sb("low", [P, P]), s.sb("upp", [P, P])
        tok = s.sb("tok", [P, NCH, 24])
        turned = s.ps("turned", [P, 2, 8, 64])
        acc = s.ps("acc", [P, 2, 512])
        c = g.col["gates3"]
        sums = lambda d: acc[:, d, 0:NCH * 4].rearrange("p (c h) -> p c h", h=4)
        ends = lambda d: acc[:, d, 64:64 + NCH * 4].rearrange("p (c h) -> p c h", h=4)
        with nc.Block() as block:
            @block.sync
            def _(sp):
                sp.dma_start(x[:, :], proj[G_GATE * P:G_GATE * P + 48, :]).then_inc(s["loaded"], 16)
                sp.dma_start(low[:, :], gd.a["low"][:, 7 * P:8 * P]).then_inc(s["loaded"], 16)
                sp.dma_start(upp[:, :], gd.a["upp"][:, 7 * P:8 * P]).then_inc(s["loaded"], 16)

            @block.scalar
            def _(act):
                act.wait_ge(s["loaded"], 48)
                dt = g.par[0:16, c:c + 1]
                act.activation(l[:, :], x[0:16, :], ACT.Abs, bias=dt).then_inc(s["abs"], 1)
                act.activation(ea[:, :], g.par[0:16, c + 1:c + 2], ACT.Exp).then_inc(s["alog"], 1)
                act.wait_ge(s["abs"], 1)
                act.activation(l[:, :], l[:, :], ACT.Exp, scale=-1.0).then_inc(s["power"], 1)
                act.wait_ge(s["power"], 1)
                act.activation(l[:, :], l[:, :], ACT.Ln, bias=1.0).then_inc(s["log"], 1)
                act.activation(x[32:48, :], x[32:48, :], ACT.Sigmoid).then_inc(s["sig"], 1)
                for d in range(2):
                    act.wait_ge(s["arg"], d + 1)
                    for n in (1, 2, 3):
                        act.activation(gd.sc[:, d, :, n, :], gd.sc[:, d, :, n, :], ACT.Exp).then_inc(s["exps"], 1)

            @block.vector
            def _(dve):
                link = chain(dve, s["own"])
                dve.wait_ge(s["loaded"], 48)
                dve.wait_ge(s["abs"], 1)
                link(dve.tensor_scalar(x[0:16, :], x[0:16, :], g.par[0:16, c:c + 1], 0.0, ALU.add, ALU.max))
                dve.wait_ge(s["log"], 1)
                link(dve.tensor_tensor(x[0:16, :], x[0:16, :], l[:, :], ALU.add))
                dve.wait_ge(s["alog"], 1)
                link(dve.tensor_scalar(x[0:16, :], x[0:16, :], ea[:, 0:1], -1.0, ALU.mult, ALU.mult), s["decay"])
                dve.wait_ge(s["turned"], 1)
                for hh in range(2):
                    for b in range(2):
                        link(dve.tensor_copy(tok[64 * hh:64 * hh + 64, 8 * b:8 * b + 8, :],
                                             turned[0:64, b, :, hh:48:2]), s["tok"])
                dve.wait_ge(s["sum"], 1)
                for d in range(2):
                    sc = gd.sc[:, d, :, :, :]
                    link(dve.tensor_copy(sc[:, :, 0, :], sums(d)))
                    link(dve.tensor_copy(sc[:, :, 1, :], sums(d)))
                    link(dve.scalar_tensor_tensor(sc[:, :, 2, :], ends(d), 64.0, sc[:, :, 0, :],
                                                  ALU.mult, ALU.subtract))
                    link(dve.tensor_scalar(sc[:, :, 3, :], ends(d), 64.0, None, ALU.mult), s["arg"])
                    beta = tok[:, :, 16 + 4 * d:20 + 4 * d]
                    link(dve.tensor_scalar(sc[:, :, 4, :], beta, -1.0, None, ALU.mult))
                    link(dve.tensor_copy(sc[:, :, 5, :], beta))
                for d in range(2):
                    sc = gd.sc[:, d, :, :, :]
                    dve.wait_ge(s["exps"], 3 * d + 3)
                    link(dve.tensor_tensor(sc[:, :, 1, :], sc[:, :, 1, :], sc[:, :, 4, :], ALU.mult))

            @block.tensor
            def _(pe):
                pe.wait_ge(s["decay"], 1)
                pe.wait_ge(s["sig"], 1)
                for n in range(NCH):
                    mm = pe.transpose(turned[0:64, n // 8, n % 8, 0:48], x[:, n * CH:n * CH + CH],
                                      g.ident[0:48, 0:48])
                mm.then_inc(s["turned"], 1)
                pe.wait_ge(s["tok"], 4)
                for d, mask in enumerate((upp, low)):
                    r = tok[:, :, 4 * d:4 * d + 4]
                    pe.matmul(sums(d), mask[:, :], r, start=True, stop=True)
                    mm = pe.matmul(ends(d), g.mean64[:, :], r, start=True, stop=True)
                mm.then_inc(s["sum"], 1)


def gdn_chunks(nc, g, gd, out):
    N, K2 = 4, 2
    names = ("sc", "kbd", "vs", "dg", "db", "rows", "dots", "turn", "x0", "eq", "diff", "ramp", "at", "em", "c_t",
             "xt1", "k_t", "v_t", "vb", "q_g", "mk", "y_done", "yp", "x_done", "x_new", "xt_done", "xt_new", "ks",
             "rhs", "vn", "vd", "vn_d", "up", "oo", "o")
    with stage(nc, "gc", *[f"{n}{u}" for u in range(2 * K2) for n in names], "const", "zero", "zero_p", "own",
               "pown", "s_new0", "s_new1", "s_bd0", "s_bd1", "stored") as s:
        low, upp = s.sb("low", [P, 7, CH]), s.sb("upp", [P, 7, CH])
        idc, ones64 = s.sb("idc", [P, CH]), s.sb("ones64", [P, P])
        dirs, units = [], []
        for d in range(2):
            t = Shared()
            t.S, t.SE, t.Sd = s.sb(f"S{d}", [P, N, CH]), s.sb(f"SE{d}", [P, N, CH]), s.sb(f"Sd{d}", [P, N, P])
            t.stg = s.sb(f"stg{d}", [P, N, K2 * CH])
            t.new, t.bd = s[f"s_new{d}"], s[f"s_bd{d}"]
            t.mT = (upp, low)[d]
            dirs.append(t)
        for u in range(2 * K2):
            t = Shared()
            t.k, t.d = u // 2, u % 2
            t.dir = dirs[t.d]
            t.s = {n: s[f"{n}{u}"] for n in names}
            t.kbd, t.kT, t.X, t.XT, t.yp, t.mk = (
                s.sb(n + str(u), [P, N, P]) for n in ("kbd", "kT", "X", "XT", "yp", "mk"))
            t.dg, t.db, t.E, t.ATc, t.CT, t.eq, t.V = (
                s.sb(n + str(u), [P, N, CH]) for n in ("dg", "db", "E", "ATc", "CT", "eq", "V"))
            t.rhs, t.vd, t.Vnd = t.dg, t.db, t.yp
            t.sc = s.sb(f"sc{u}", [P, GK, N])
            t.b = [s.ps(f"b{n}_{u}", [P, 512]) for n in range(2)]
            t.wide = lambda n, t=t: t.b[n][:, :].rearrange("p (n c) -> p n c", n=N)
            t.half = lambda n, h, t=t: t.b[n][:, 256 * h:256 * h + 256].rearrange("p (n c) -> p n c", n=N)
            t.two = lambda n, t=t: t.b[n][:, :].rearrange("p (n b c) -> p n b c", n=N, b=2)
            t.m = lambda k, t=t: t.dir.mT[:, k:k + 1, :].broadcast_to([P, N, CH])
            t.mh = lambda k, r, t=t: t.dir.mT[r, k:k + 1, :].broadcast_to([64, N, CH])
            t.f = lambda n, t=t: t.sc[:, n, :].unsqueeze(2).broadcast_to([P, N, CH])
            units.append(t)
        idn = idc[:, None, :].broadcast_to([P, N, CH])
        idb = g.ident[:, None, :].broadcast_to([P, N, P])
        with nc.Block() as block:
            @block.sync
            def _(sp):
                for r in HEAD:
                    for t, n in ((low, "low"), (upp, "upp")):
                        src = gd.a[n].rearrange("p (k c) -> p k c", k=8)
                        sp.dma_start(t[r, 0:6, :], src[r, 0:6, r]).then_inc(s["const"], 16)
                        sp.dma_start(t[r, 6:7, :], src[r, 7:8, r]).then_inc(s["const"], 16)
                    sp.dma_start(idc[r, :], gd.a["ident"][r, r]).then_inc(s["const"], 16)
                sp.wait_ge(s["const"], 160)

            @block.vector
            def _(dve):
                dve.tensor_scalar(ones64[:, :], g.mean64[:, :], 64.0, None, ALU.mult).then_inc(s["zero"], 1)
                for t in units:
                    dve.memset(t.kbd[:, :, :], 0.0).then_inc(s["zero"], 1)
                for t in dirs:
                    dve.memset(t.S[:, :, :], 0.0).then_inc(s["zero"], 1)

            @block.gpsimd
            def _(pool):
                for t in units:
                    for x in (t.XT, t.mk):
                        pool.memset(x[:, :, :], 0.0).then_inc(s["zero_p"], 1)
                for t in dirs:
                    pool.memset(t.Sd[:, :, :], 0.0).then_inc(s["zero_p"], 1)
        clear(nc, s)
        with nc.Block() as block:
            @block.sync
            def _(sp):
                sp.sem_inc(s["stored"], 32)
        with nc.Fori(0, NCH // K2) as i:
            chunk = lambda t: i * K2 + t.k if t.d == 0 else i * (-K2) + (NCH - 1 - t.k)
            at = lambda t: i * (K2 * CH) + t.k * CH if t.d == 0 else i * (-K2 * CH) + (NCH - 1 - t.k) * CH
            with nc.Block() as block:
                @block.gpsimd
                def _(pool):
                    link = chain(pool, s["pown"])
                    tt = pool.tensor_tensor
                    for t in units:
                        link(pool.tensor_copy(t.sc[:, :, :], gd.sc[:, t.d, ds(chunk(t), 1), :, :]
                                              .rearrange("p a k n -> p (a k) n")), t.s["sc"])
                    for t in units:
                        link(tt(t.dg[:, :, :], idn, t.f(0), ALU.mult), t.s["dg"])
                    for t in units:
                        pool.wait_ge(t.s["ramp"], 1)
                        link(tt(t.CT[:, :, :], t.E[:, :, :], t.m(6), ALU.mult), t.s["em"])
                    for lev in range(1, 6):
                        for t in units:
                            if lev == 1:
                                pool.wait_ge(t.s["at"], 1)
                            else:
                                pool.wait_ge(t.s["y_done"], lev - 1)
                            for r in HEAD:
                                link(tt(t.mk[r, :, r], t.ATc[r, :, :], t.mh(lev, r), ALU.mult), t.s["mk"])
                        if lev == 1:
                            for t in units:
                                pool.wait_ge(t.s["eq"], 1)
                                link(tt(t.eq[:, :, :], t.eq[:, :, :], gd.q[:, :, ds(at(t), CH)], ALU.mult),
                                     t.s["q_g"])
                                pool.wait_ge(t.s["v_t"], 2)
                                link(tt(t.V[:, :, :], t.V[:, :, :], t.f(5), ALU.mult), t.s["vb"])

                @block.tensor
                def _(pe):
                    def each(out, lhsT, rhs_, sem):
                        for p in range(N):
                            mm = pe.matmul(out[:, p], lhsT[:, p, :], rhs_(p), start=True, stop=True)
                        mm.then_inc(sem, 1)

                    def turn(out, x, sem):
                        for p in range(N):
                            mm = pe.transpose(out[:, p, :], x[:, p, :], g.ident[:, :])
                        mm.then_inc(sem, 1)

                    of = lambda x: (lambda p: x[:, p, :])
                    for t in units:
                        pe.wait_ge(t.s["kbd"], 2)
                        each(t.two(1), t.kbd, lambda p: gd.all[:, 0:2, p, ds(at(t), CH)], t.s["dots"])
                        pe.wait_ge(t.s["dg"], 1)
                        pe.wait_ge(t.s["db"], 1)
                        pe.matmul(t.half(0, 0), ones64[:, :], t.dg[:, :, :], start=True, stop=True)
                        pe.matmul(t.half(0, 1), ones64[:, :], t.db[:, :, :], start=True, stop=True)\
                          .then_inc(t.s["rows"], 1)
                    for t in units:
                        pe.wait_ge(t.s["eq"], 1)
                        pe.wait_ge(t.s["at"], 1)
                        turn(t.wide(0), t.kbd, t.s["turn"])
                        pe.wait_ge(t.s["c_t"], 1)
                        pe.wait_ge(t.s["vs"], 1)
                        turn(t.wide(1)[0:64], t.V, t.s["turn"])
                    for t in units:
                        pe.wait_ge(t.s["k_t"], 1)
                        pe.wait_ge(t.s["xt1"], 1)
                        turn(t.wide(0), t.XT, t.s["x0"])
                    for lev in range(1, 6):
                        for t in units:
                            pe.wait_ge(t.s["mk"], 2 * lev)
                            pe.wait_ge(t.s["x_new"], lev)
                            if lev > 1:
                                pe.wait_ge(t.s["xt_new"], lev - 1)
                            each(t.wide(0), t.mk, of(t.X), t.s["y_done"])
                        for t in units:
                            pe.wait_ge(t.s["yp"], lev)
                            if lev == 1:
                                pe.wait_ge(t.s["v_t"], 2)
                            if lev < 5:
                                each(t.wide(1), t.XT, of(t.yp), t.s["x_done"])
                            each(t.wide(0), t.yp, of(t.XT), t.s["xt_done"])
                    for k in range(K2):
                        now = units[2 * k:2 * k + 2]
                        for t in now:
                            pe.wait_ge(t.s["xt_new"], 5)
                            if k > 0:
                                pe.wait_ge(t.dir.new, k)
                            each(t.half(0, 0), t.kbd, of(t.dir.S), t.s["ks"])
                        for t in now:
                            pe.wait_ge(t.s["rhs"], 1)
                            each(t.half(1, 0), t.XT, of(t.rhs), t.s["vn"])
                        for t in now:
                            pe.wait_ge(t.s["vd"], 1)
                            each(t.half(0, 1), t.kT, of(t.vd), t.s["up"])
                        for t in now:
                            pe.wait_ge(t.s["vn_d"], 2)
                            pe.wait_ge(t.s["q_g"], 1)
                            if k > 0:
                                pe.wait_ge(t.dir.bd, 2 * k)
                            for p in range(N):
                                o = t.half(1, 1)[:, p, :]
                                pe.matmul(o, t.dir.Sd[:, p, :], t.eq[:, p, :], start=True, stop=False)
                                mm = pe.matmul(o, t.Vnd[:, p, :], t.CT[:, p, :], start=False, stop=True)
                            mm.then_inc(t.s["oo"], 1)

                @block.vector
                def _(dve):
                    link = chain(dve, s["own"])
                    tt = dve.tensor_tensor
                    for t in units:
                        dve.wait_ge(t.s["sc"], 1)
                        tt(t.db[:, :, :], idn, t.f(4), ALU.mult).then_inc(t.s["db"], 1)
                    for t in units:
                        dve.wait_ge(t.s["eq"], 1)
                        link(tt(t.E[:, :, :], t.half(0, 0), t.f(0), ALU.subtract))
                        dve.tensor_scalar(t.E[:, :, :], t.E[:, :, :], 0.0, None, ALU.min).then_inc(t.s["diff"], 1)
                    for t in units:
                        dve.wait_ge(t.s["dots"], 1)
                        dve.wait_ge(t.s["ramp"], 1)
                        link(tt(t.ATc[:, :, :], t.two(1)[:, :, 0, :], t.E[:, :, :], ALU.mult))
                        link(tt(t.ATc[:, :, :], t.half(0, 1), t.ATc[:, :, :], ALU.mult), t.s["at"])
                        dve.wait_ge(t.s["em"], 1)
                        tt(t.CT[:, :, :], t.two(1)[:, :, 1, :], t.CT[:, :, :], ALU.mult).then_inc(t.s["c_t"], 1)
                    for t in units:
                        for r in HEAD:
                            link(tt(t.XT[r, :, r], t.ATc[r, :, :], t.mh(0, r), ALU.mult))
                        tt(t.XT[:, :, :], t.XT[:, :, :], idb, ALU.add).then_inc(t.s["xt1"], 1)
                    for lev in range(1, 6):
                        for t in units:
                            dve.wait_ge(t.s["y_done"], lev)
                            if lev > 1:
                                dve.wait_ge(t.s["xt_done"], lev - 1)
                            tt(t.yp[:, :, :], t.wide(0), idb, ALU.add).then_inc(t.s["yp"], 1)
                    for k in range(K2):
                        now = units[2 * k:2 * k + 2]
                        for t in now:
                            link(tt(t.dir.SE[:, :, :], t.dir.S[:, :, :], t.f(3), ALU.mult))
                        for t in now:
                            dve.wait_ge(t.s["ks"], 1)
                            dve.wait_ge(t.s["vb"], 1)
                            link(tt(t.rhs[:, :, :], t.half(0, 0), t.f(1), ALU.mult))
                            tt(t.rhs[:, :, :], t.rhs[:, :, :], t.V[:, :, :], ALU.add).then_inc(t.s["rhs"], 1)
                        for t in now:
                            dve.wait_ge(t.s["vn"], 1)
                            tt(t.vd[:, :, :], t.half(1, 0), t.f(2), ALU.mult).then_inc(t.s["vd"], 1)
                        for t in now:
                            dve.wait_ge(t.s["up"], 1)
                            if k > 0:
                                dve.wait_ge(t.dir.bd, 2 * k)
                            link(tt(t.dir.S[:, :, :], t.dir.SE[:, :, :], t.half(0, 1), ALU.add), t.dir.new)

                @block.scalar
                def _(act):
                    def copy(out, src, sem):
                        act.activation(out, src, ACT.Copy).then_inc(sem, 1)

                    for t in units:
                        for r in HEAD:
                            copy(t.kbd[r, :, r], gd.k[r, :, ds(at(t), CH)], t.s["kbd"])
                    for t in units:
                        act.wait_ge(t.s["rows"], 1)
                        act.activation(t.eq[:, :, :], t.half(0, 0), ACT.Exp).then_inc(t.s["eq"], 1)
                    for t in units:
                        act.wait_ge(t.s["diff"], 1)
                        act.activation(t.E[:, :, :], t.E[:, :, :], ACT.Exp).then_inc(t.s["ramp"], 1)
                    for t in units:
                        copy(t.V[:, :, :], gd.v[:, :, ds(at(t), CH)], t.s["vs"])
                    for t in units:
                        act.wait_ge(t.s["turn"], 1)
                        copy(t.kT[:, :, :], t.wide(0), t.s["k_t"])
                        act.wait_ge(t.s["turn"], 2)
                        for r in HEAD:
                            copy(t.V[r, :, :], t.wide(1)[0:64, :, r], t.s["v_t"])
                    for t in units:
                        act.wait_ge(t.s["x0"], 1)
                        copy(t.X[:, :, :], t.wide(0), t.s["x_new"])
                    for lev in range(1, 6):
                        for t in units:
                            if lev < 5:
                                act.wait_ge(t.s["x_done"], lev)
                                copy(t.X[:, :, :], t.wide(1), t.s["x_new"])
                            act.wait_ge(t.s["xt_done"], lev)
                            copy(t.XT[:, :, :], t.wide(0), t.s["xt_new"])
                    for k in range(K2):
                        now = units[2 * k:2 * k + 2]
                        for t in now:
                            act.wait_ge(t.s["vd"], 1)
                            for r in HEAD:
                                copy(t.Vnd[r, :, r], t.half(1, 0)[r, :, :], t.s["vn_d"])
                        if k == 0:
                            act.wait_ge(s["stored"], i * 32 + 32)
                        for t in now:
                            act.wait_ge(t.s["oo"], 1)
                            here = t.k * CH if t.d == 0 else (K2 - 1 - t.k) * CH
                            copy(t.dir.stg[:, :, here:here + CH], t.half(1, 1), t.s["o"])
                            act.wait_ge(t.dir.new, k + 1)
                            for r in HEAD:
                                copy(t.dir.Sd[r, :, r], t.dir.S[r, :, :], t.dir.bd)

                @block.sync
                def _(sp):
                    first = (i * (K2 * CH), i * (-K2 * CH) + (NCH - K2) * CH)
                    for d in range(2):
                        for t in units[d::2]:
                            sp.wait_ge(t.s["o"], 1)
                        sp.dma_start(out[d][:, ds(first[d], K2 * CH)].rearrange("(k p) t -> p k t", p=P),
                                     dirs[d].stg[:, :, :]).then_inc(s["stored"], 16)
            clear(nc, s, keep="stored")
        with nc.Block() as block:
            @block.sync
            def _(sp):
                sp.wait_ge(s["stored"], 32 * (NCH // K2 + 1))


def spatial(nc, g, a, proj):
    two = range(2)
    with stage(nc, "sg", *[f"{n}{j}" for j in two for n in ("u_in", "v_in", "w_in", "b_in")], "gelu", "par", "eps",
               "squared", "summed", "logged", "rooted", "normed", "turned", "tok", "mixed", "biased", "gated", "own",
               "y") as s:
        u, v, sq = ([s.sb(f"{n}{j}", [P, SEQ]) for j in two] for n in ("u", "v", "sq"))
        wT, bias = ([s.sb(f"{n}{j}", [P, P]) for j in two] for n in ("wT", "bias"))
        vt = [s.sb(f"vt{j}", [P, 8, P]) for j in two]
        par, low = s.sb("par", [P, 2, 2]), s.sb("eps", [P, 1])
        acc = [s.ps(f"acc{j}", [P, 2, 512]) for j in two]
        wide = [s.ps(f"wide{j}", [P, 8, P]) for j in two]
        half = lambda t, n: t[:, 4 * n:4 * n + 4, :]
        with nc.Block() as block:
            @block.vector
            def _(dve):
                dve.memset(low[:, :], EPS).then_inc(s["eps"], 1)
        clear(nc, s)
        with nc.Fori(0, 2) as i:
            with nc.Block() as block:
                @block.sync
                def _(sp):
                    for j in two:
                        at = lambda tile: ds(i * (2 * P) + (tile + j) * P, P)
                        sp.dma_start(v[j][:, :], proj[at(G_SV), :]).then_inc(s[f"v_in{j}"], 16)
                        sp.dma_start(u[j][:, :], proj[at(G_SU), :]).then_inc(s[f"u_in{j}"], 16)
                        sp.dma_start(wT[j][:, :], a["sgu_wt"][at(0), :]).then_inc(s[f"w_in{j}"], 16)
                        sp.dma_start(bias[j][:, :], a["sgu_b"][ds(i * 2 + j, 1), :].broadcast_to([P, P]))\
                          .then_inc(s[f"b_in{j}"], 16)

                @block.scalar
                def _(act):
                    for j in two:
                        act.wait_ge(s[f"v_in{j}"], 16)
                        act.activation(v[j][:, :], v[j][:, :], ACT.Gelu).then_inc(s["gelu"], 1)
                    for j in two:
                        act.wait_ge(s[f"u_in{j}"], 16)
                        act.activation(u[j][:, :], u[j][:, :], ACT.Gelu).then_inc(s["gelu"], 1)
                    for n in two:
                        for j in two:
                            act.wait_ge(s["summed"], 2 * n + j + 1)
                            act.activation(halves(sq[j][:, :]), acc[j][:, :, :], ACT.Ln, scale=1.0 / P,
                                           bias=low[:, 0:1]).then_inc(s["logged"], 1)
                            act.wait_ge(s["logged"], 2 * n + j + 1)
                            act.activation(sq[j][:, :], sq[j][:, :], ACT.Exp, scale=-0.5).then_inc(s["rooted"], 1)

                @block.tensor
                def _(pe):
                    def total(m):
                        pe.wait_ge(s["squared"], m + 1)
                        for b in two:
                            mm = pe.matmul(acc[m % 2][:, b, :], g.ones[:, :], sq[m % 2][:, b * 512:b * 512 + 512],
                                           start=True, stop=True)
                        mm.then_inc(s["summed"], 1)

                    for j in two:
                        total(j)
                    for j in two:
                        pe.wait_ge(s["normed"], j + 1)
                        for c in range(8):
                            mm = pe.transpose(wide[j][:, c, :], v[j][:, c * P:(c + 1) * P], g.ident[:, :])
                        mm.then_inc(s["turned"], 1)
                    for j in two:
                        pe.wait_ge(s["tok"], 2 * j + 2)
                        pe.wait_ge(s[f"w_in{j}"], 16)
                        for c in range(8):
                            mm = pe.matmul(wide[j][:, c, :], vt[j][:, c, :], wT[j][:, :], start=True, stop=True)
                        mm.then_inc(s["mixed"], 1)
                    for j in two:
                        total(2 + j)

                @block.vector
                def _(dve):
                    link = chain(dve, s["own"])
                    for n, name in enumerate(("sgv", "sgo")):
                        dve.tensor_copy(par[:, n, :], g.par[:, ds(i * 2 + g.col[name], 2)]).then_inc(s["par"], 1)
                    dve.wait_ge(s["par"], 2)
                    for j in two:
                        dve.wait_ge(s["gelu"], j + 1)
                        dve.tensor_tensor(sq[j][:, :], v[j][:, :], v[j][:, :], ALU.mult).then_inc(s["squared"], 1)
                    for j in two:
                        dve.wait_ge(s["rooted"], j + 1)
                        dve.scalar_tensor_tensor(v[j][:, :], v[j][:, :], par[:, 0, j:j + 1], sq[j][:, :],
                                                 ALU.mult, ALU.mult).then_inc(s["normed"], 1)
                    for j in two:
                        dve.wait_ge(s["turned"], j + 1)
                        for n in two:
                            dve.tensor_copy(half(vt[j], n), half(wide[j], n)).then_inc(s["tok"], 1)
                    for j in two:
                        dve.wait_ge(s["mixed"], j + 1)
                        dve.wait_ge(s[f"b_in{j}"], 16)
                        v8 = v[j][:, :].rearrange("p (c t) -> p c t", c=8)
                        for n in two:
                            dve.tensor_tensor(half(v8, n), half(wide[j], n),
                                              bias[j][:, None, :].broadcast_to([P, 4, P]), ALU.add)\
                               .then_inc(s["biased"], 1)
                        dve.wait_ge(s["biased"], 2 * j + 2)
                        dve.wait_ge(s["gelu"], 4)
                        link(dve.tensor_tensor(v[j][:, :], v[j][:, :], u[j][:, :], ALU.mult), s["gated"])
                        dve.tensor_tensor(sq[j][:, :], v[j][:, :], v[j][:, :], ALU.mult).then_inc(s["squared"], 1)
                    for j in two:
                        dve.wait_ge(s["rooted"], 2 + j + 1)
                        dve.scalar_tensor_tensor(g.y[:, ds(i * 2 + (4 + j), 1), :], v[j][:, None, :],
                                                 par[:, 1, j:j + 1], sq[j][:, None, :], ALU.mult, ALU.mult)\
                           .then_inc(s["y"], 1)
            clear(nc, s)


def block3(nc, g, a, dram, out):
    proj = dram("proj3", (TILES_3 * P, SEQ))
    o_dram = [dram(f"o3_{d}", (4 * P, SEQ)) for d in range(2)]
    with g.parts("a3"):
        norm_h(nc, "n3", g, g.col["g3"], SEQ)
        dense(nc, "in3", g, a["w_in_3"], TILES_3, SEQ, proj, conv=(G_Z, 5, 2, "gconv"))
    with ExitStack() as ctx:
        sb = lambda n, shape: ctx.enter_context(nc.sbuf_tensor(n, shape, F32))
        gd = Shared()
        gd.a = a
        gd.all = sb("gd_all", [P, 3, 4, SEQ])
        gd.k, gd.q, gd.v = (gd.all[:, n, :, :] for n in range(3))
        gd.sc = sb("gd_sc", [P, 2, NCH, GK, 4])
        unit_heads(nc, g, proj, gd)
        gdn_gates(nc, g, proj, gd)
        gdn_chunks(nc, g, gd, o_dram)
    with nc.sbuf_tensor("y3", [P, KD, SEQ], F32) as y_sb:
        g.y = y_sb
        head_norm(nc, "hg", g, o_dram[0], 4, 0, EPS, (proj, G_Z), ACT.Silu, center=False, gain="gdng",
                  src2=o_dram[1], per=2)
        spatial(nc, g, a, proj)
        with g.parts("b3"):
            split_u(nc, "su3", g)
            dense(nc, "out3", g, a["w_out_3"], KD, SEQ)
    with g.parts("c3"):
        norm_h(nc, "nm3", g, g.col["gm3"], SEQ)
        ffn(nc, "ff3", g, a["w_ff1_3"], a["w_ff2_3"], [(4, KD)], SEQ, gated=False)
    norm_h(nc, "nf3", g, g.col["gf3"], SEQ, dest=out)


def cols(v):
    v = v.reshape(-1, v.shape[-1])
    K, C = v.shape
    return np.ascontiguousarray(v.reshape(K, C // P, P).transpose(2, 1, 0)).reshape(P, -1)


def block_diagonal(w):
    out = np.zeros((w.shape[0] // 2, P, P), w.dtype)
    out[:, 0:64, 0:64] = w[0::2]
    out[:, 64:, 64:] = w[1::2]
    return out.reshape(-1, P)


def layout(x):
    par, col = [], {}

    def put(name, block):
        col[name] = sum(b.shape[1] for b in par)
        par.append(block)

    z1 = lambda n: np.zeros((P, n), np.float32)
    put("g1", cols(x["norm_mix_g"][0]))
    put("lru", np.concatenate([np.concatenate(
        [cols(x["lru_conv_w"][0][:, t * P:(t + 1) * P])] +
        [cols(x[k][0][t * P:(t + 1) * P]) for k in ("lru_conv_b", "lru_gate_a_b", "lru_gate_x_b", "lru_a_param")] +
        [z1(LRU_PAR - 8)], 1) for t in range(4)], 1))
    put("cc", np.concatenate([np.concatenate(
        [cols(x["cc_conv_w"][0][:, t * P:(t + 1) * P]), cols(x["cc_conv_b"][0][t * P:(t + 1) * P])], 1)
        for t in range(4)], 1))
    put("ccg", cols(x["cc_ln_g"][0]))
    put("ccb", cols(x["cc_ln_b"][0]))
    put("go1", np.concatenate([cols(x["out_norm_lru_g"][0]), cols(x["out_norm_cc_g"][0])], 1))
    put("gm1", cols(x["norm_mlp_g"][0]))
    put("gf1", cols(x["norm_final_g"]))
    a = {
        "h0": np.ascontiguousarray(np.concatenate([x["meta_tokens"], x["x"][0]], 0).T),
        "w_in": x["w_in"][0], "w_out": x["w_out"][0], "w_mlp_up": x["w_mlp_up"][0], "w_mlp_down": x["w_mlp_down"][0],
        "lru_wa": block_diagonal(x["lru_gate_a_w"][0]), "lru_wx": block_diagonal(x["lru_gate_x_w"][0]),
    }
    layout2(x, a, put)
    layout3(x, a, put)
    a["par"] = np.ascontiguousarray(np.concatenate(par, 1))
    return a, col


def tiles_of(w, *spans):
    out = []
    for lo, hi in spans:
        out.append(w[:, lo:hi])
        if (hi - lo) % P:
            out.append(np.zeros((w.shape[0], -(hi - lo) % P), w.dtype))
    return np.concatenate(out, 1)


def level_masks():
    t, s_ = np.meshgrid(np.arange(P), np.arange(P), indexing="ij")
    same = t // CH == s_ // CH
    m = [same & (t >> (k + 1) == s_ >> (k + 1)) & ((t >> k) & 1 == 1) & ((s_ >> k) & 1 == 0) for k in range(6)]
    m += [same & (s_ < t), same & (s_ <= t)]
    low = np.stack(m, 1).astype(np.float32)
    return low.reshape(P, -1), np.ascontiguousarray(low.transpose(2, 1, 0)).reshape(P, -1)


def layout2(x, a, put):
    w = x["w_in_2"][0]
    m, r = 1032, 1032 + 1536
    a["w_in_2"] = tiles_of(w, (0, 1024), (m, m + 1536), (r, r + 1408), (1024, 1032))
    a["w_gu_2"] = np.stack([x["w_gate_2"][0].reshape(D, -1, P), x["w_up_2"][0].reshape(D, -1, P)], 2).reshape(D, -1)
    a["w_out_2"], a["w_down_2"] = x["w_out_2"][0], x["w_down_2"][0]
    put("g2", cols(x["ln1_g_2"][0]))
    put("gm2", cols(x["ln2_g_2"][0]))
    put("gf2", cols(x["lnf_g_2"]))
    put("mconv", cols(x["m_conv_2"][0]))
    mb = np.zeros((P, 2), np.float32)
    mb[0:4, 0], mb[0:4, 1] = x["m_b_i_2"][0], x["m_b_f_2"][0]
    put("mb", mb)
    put("mln", cols(x["m_ln_g_2"][0]))
    put("wlng", cols(x["rw_ln_g_2"][0]))
    put("wlnb", cols(x["rw_ln_b_2"][0]))
    mu = x["rw_mu_2"][0]
    put("wmu", cols(mu[1152:1408]))
    by_tile = [cols(v) for v in (mu[0:384], mu[384:768], mu[768:1152], x["rw_w0_2"][0], x["rw_a0_2"][0],
                                 x["rw_k_k_2"][0], x["rw_k_a_2"][0], x["rw_r_k_2"][0])]
    put("w", np.stack(by_tile, 2).reshape(P, -1))
    tile = lambda v: v.reshape(P, 3, P).transpose(1, 0, 2).reshape(3 * P, P)
    z = np.zeros((64, 384), np.float32)
    a["w_up"] = tile(np.concatenate([x["rw_w_up_2"][0], z]))
    a["a_up"] = tile(np.concatenate([z, x["rw_a_up_2"][0]]))
    a["g_up"] = tile(x["rw_g_up_2"][0])
    d = np.arange(P)
    theta = (1.0 / 10000.0 ** np.linspace(0.0, 1.0, 32, dtype=np.float32)).astype(np.float32)
    ang = np.arange(SEQ, dtype=np.float32)[None, :] * theta[d % 32][:, None]
    a["cos"] = np.cos(ang)
    a["sin"] = np.sin(ang) * np.where(d % 64 < 32, -1.0, 1.0).astype(np.float32)[:, None]
    a["swap"] = (d[:, None] == (d ^ 32)[None, :]).astype(np.float32)
    xx = np.arange(SEQ)[None, :] - d[:, None]
    log_g = np.log(1.0 - 2.0 ** (-5.0 - np.arange(6)))
    a["ramps"] = np.concatenate([np.where(xx >= 0, np.exp(np.maximum(xx, 0) * lg), 0.0) * 0.125
                                 for lg in log_g]).astype(np.float32)
    a["tri"] = np.where(xx[:, 0:512] >= 0, 0.0, -1e30).astype(np.float32)
    a["reset"] = np.broadcast_to((np.arange(SEQ) % CH != 0).astype(np.float32), (P, SEQ))
    a["low"], a["upp"] = level_masks()
    a["ident"] = np.eye(P, dtype=np.float32)
    a["mean64"] = np.kron(np.eye(2), np.full((64, 64), 1.0 / 64)).astype(np.float32)


def layout3(x, a, put):
    w = x["w_in_3"][0]
    gates = np.zeros((D, P), w.dtype)
    gates[:, 0:16], gates[:, 32:48] = w[:, 2064:2080], w[:, 2048:2064]
    a["w_in_3"] = np.concatenate([w[:, 0:2048], w[:, 2080:3104], gates, np.zeros((D, P), w.dtype)], 1)
    a["w_out_3"], a["w_ff1_3"], a["w_ff2_3"] = x["w_out_3"][0], x["w_ff1_3"][0], x["w_ff2_3"][0]
    put("g3", cols(x["norm_mix_3"][0]))
    put("gm3", cols(x["norm_ffn_3"][0]))
    put("gf3", cols(x["norm_final_3"]))
    put("gconv", cols(x["conv_w_3"][0]))
    gates3 = np.zeros((P, 2), np.float32)
    gates3[0:8, 0], gates3[8:16, 0] = x["dt_bias_fwd_3"][0], x["dt_bias_bwd_3"][0]
    gates3[0:8, 1], gates3[8:16, 1] = x["a_log_fwd_3"][0], x["a_log_bwd_3"][0]
    put("gates3", gates3)
    put("gdng", np.tile(x["gdn_norm_3"][0][:, None], (2, 4)))
    put("sgv", cols(x["sgu_v_norm_3"][0].reshape(-1)))
    put("sgo", cols(x["sgu_out_norm_3"][0].reshape(-1)))
    a["sgu_wt"] = x["sgu_w_3"][0].transpose(0, 2, 1).reshape(4 * P, P)
    a["sgu_b"] = x["sgu_b_3"][0]


def program(nc, a, out, col, blocks=(1, 2, 3)):
    g = Shared()
    g.col = col
    par_cols = a["par"].shape[1]
    dram = lambda n, shape: nc.dram_tensor(n, shape, F32, kind="Internal").ap()
    with ExitStack() as ctx:
        sb = lambda n, shape, dt=F32: ctx.enter_context(nc.sbuf_tensor(n, shape, dt))
        g.h = sb("h", [P, KD, T1])
        g.par = sb("par", [P, par_cols])
        g.ones, g.ident, g.mean64 = sb("ones", [P, P]), sb("ident", [P, P]), sb("mean64", [P, P])
        with stage(nc, "start", "loaded", "ones") as s:
            with nc.Block() as block:
                @block.sync
                def _(sp):
                    T = a["h0"].shape[1]
                    sp.dma_start(g.h[:, :, 0:T], a["h0"].rearrange("(k p) t -> p k t", p=P)).then_inc(s["loaded"], 16)
                    sp.dma_start(g.par[:, :], a["par"]).then_inc(s["loaded"], 16)
                    sp.dma_start(g.ident[:, :], a["ident"]).then_inc(s["loaded"], 16)
                    sp.dma_start(g.mean64[:, :], a["mean64"]).then_inc(s["loaded"], 16)
                    sp.wait_ge(s["loaded"], 64)

                @block.vector
                def _(dve):
                    dve.memset(g.ones[:, :], 1.0).then_inc(s["ones"], 1)

        @contextmanager
        def parts(name):
            with nc.sbuf_tensor(name + "_uhi", [P, KD, T1], F32R) as uhi, \
                 nc.sbuf_tensor(name + "_ulo", [P, KD, T1], F32R) as ulo, \
                 nc.sbuf_tensor(name + "_inv", [P, T1], F32) as inv:
                g.uhi, g.ulo, g.inv = uhi, ulo, inv
                yield

        g.parts = parts
        if 1 in blocks:
            block1(nc, g, a, dram("proj1", (TILES_1 * P, T1)))
        if 2 in blocks:
            block2(nc, g, a, dram)
        if 3 in blocks:
            block3(nc, g, a, dram, out)
        else:
            with stage(nc, "dump", "st") as s:
                with nc.Block() as block:
                    @block.sync
                    def _(sp):
                        sp.dma_start(out.rearrange("(k p) t -> p k t", p=P), g.h[:, :, 0:SEQ]).then_inc(s["st"], 16)
                        sp.wait_ge(s["st"], 16)


def kernel(**inputs):
    import concourse.bacc as bacc
    from concourse.bass_utils import run_bass_kernel_spmd

    arrays, col = layout({k: np.asarray(v) for k, v in inputs.items()})
    arrays = {k: np.ascontiguousarray(v) for k, v in arrays.items()}
    nc = bacc.Bacc("TRN2", target_bir_lowering=False, num_devices=1)
    a = {k: nc.dram_tensor(f"in_{k}", v.shape, F32, kind="ExternalInput").ap() for k, v in arrays.items()}
    out = nc.dram_tensor("out_t", (D, SEQ), F32, kind="ExternalOutput").ap()
    program(nc, a, out, col)
    r = run_bass_kernel_spmd(nc, [{f"in_{k}": v for k, v in arrays.items()}], core_ids=[0])
    return np.ascontiguousarray(r.results[0]["out_t"].T)[None]
```
